# Optimizing a Trainium2 kernel written in Bass

```python
import math
import jax, jax.numpy as jnp
from jax import lax
import numpy as np

D_MODEL = 1024
BATCH = 1
SEQ = 1024
DEPTH = 1
DEC_BATCH = 8
DEC_SEQ = 4
PAST_LEN = 1024
PAGE_SIZE = 128

HEAD_DIM = 64
ATTN_GROUPS = ((128, 1), (512, 4), (2048, 16))
HEADS_PER_GROUP = 4
N_ATTN_HEADS = HEADS_PER_GROUP * len(ATTN_GROUPS)
ATTN_WIDTH = N_ATTN_HEADS * HEAD_DIM
SSM_WIDTH = D_MODEL - ATTN_WIDTH
SSM_GROUP = 16
SSM_GROUPS = SSM_WIDTH // SSM_GROUP
SSM_STATE = 64
IN_WIDTH = 3 * ATTN_WIDTH + SSM_WIDTH
ROT_DIM = HEAD_DIM // 4
ROPE_THETA = 500000.0
N_MEM = 256
X_HEADS = 4
X_HEAD_DIM = D_MODEL // X_HEADS
D_FF = 2816
CONV_W = 3
EPS = 1e-6

kernel_name = "hymba_s5_longnet_convffn_step"

def rmsnorm(x, g):
    xf = x.astype(jnp.float32)
    y = xf * lax.rsqrt(jnp.mean(xf * xf, axis=-1, keepdims=True) + EPS)
    return (y * g.astype(jnp.float32)).astype(x.dtype)

def rope_partial(x, pos):
    half = ROT_DIM // 2
    inv = jnp.power(jnp.float32(ROPE_THETA), -jnp.arange(half, dtype=jnp.float32) * 2.0 / ROT_DIM)
    ang = pos.astype(jnp.float32)[:, None] * inv[None, :]
    cos = jnp.cos(ang)[None, :, None, :]
    sin = jnp.sin(ang)[None, :, None, :]
    xr = x[..., :ROT_DIM].astype(jnp.float32)
    x1, x2 = xr[..., :half], xr[..., half:]
    rot = jnp.concatenate([x1 * cos - x2 * sin, x2 * cos + x1 * sin], axis=-1)
    return jnp.concatenate([rot.astype(x.dtype), x[..., ROT_DIM:]], axis=-1)

def dilated_attn_prompt(q, k, v, window, dil):
    B, L, H, E = q.shape
    S = L // dil
    blk = window // dil
    nb = -(-S // blk)
    Sp = nb * blk

    def to_blocks(t):
        t = t.reshape(B, S, dil, H, E)
        t = jnp.pad(t, ((0, 0), (0, Sp - S), (0, 0), (0, 0), (0, 0)))
        return t.reshape(B, nb, blk, dil, H, E)

    def band(t):
        tp = jnp.pad(t, ((0, 0), (1, 0), (0, 0), (0, 0), (0, 0), (0, 0)))
        return jnp.concatenate([tp[:, :-1], tp[:, 1:]], axis=2)

    qb = to_blocks(q)
    kb = band(to_blocks(k))
    vb = band(to_blocks(v))
    s = jnp.einsum('bnqrhe,bnkrhe->bnrhqk', qb, kb, preferred_element_type=jnp.float32)
    qi = jnp.arange(nb)[:, None, None] * blk + jnp.arange(blk)[None, :, None]
    ki = (jnp.arange(nb)[:, None, None] - 1) * blk + jnp.arange(2 * blk)[None, None, :]
    delta = qi - ki
    mask = (delta >= 0) & (delta <= blk) & (ki >= 0)
    s = jnp.where(mask[None, :, None, None], s, -jnp.inf)
    lse = jax.nn.logsumexp(s, axis=-1)
    p = jnp.exp(s - lse[..., None])
    o = jnp.einsum('bnrhqk,bnkrhe->bnqrhe', p.astype(v.dtype), vb)
    o = o.reshape(B, Sp, dil, H, E)[:, :S].reshape(B, L, H, E)
    lse = jnp.transpose(lse, (0, 1, 4, 2, 3)).reshape(B, Sp, dil, H)[:, :S].reshape(B, L, H)
    return o, lse

def dilated_attn_sample(q, k_all, v_all, window, dil, n_buf):
    T = q.shape[1]
    n_keys = window // dil + 1
    idx = n_buf + jnp.arange(T)[:, None] - dil * jnp.arange(n_keys)[None, :]
    valid = idx >= 0
    idx = jnp.maximum(idx, 0)
    kg = k_all[:, idx]
    vg = v_all[:, idx]
    s = jnp.einsum('bthe,btjhe->bthj', q, kg, preferred_element_type=jnp.float32)
    s = jnp.where(valid[None, :, None, :], s, -jnp.inf)
    lse = jax.nn.logsumexp(s, axis=-1)
    p = jnp.exp(s - lse[..., None])
    o = jnp.einsum('bthj,btjhe->bthe', p.astype(vg.dtype), vg)
    return o, lse

def s5_scan(u, s0_re, s0_im, p):
    uf = u.astype(jnp.float32)
    lam_re = p['ssm_lam_re'].astype(jnp.float32)
    lam_im = p['ssm_lam_im'].astype(jnp.float32)
    dt = jnp.exp(p['ssm_log_dt'].astype(jnp.float32))[:, None]
    mag = jnp.exp(lam_re * dt)
    a_re = mag * jnp.cos(lam_im * dt)
    a_im = mag * jnp.sin(lam_im * dt)
    den = lam_re * lam_re + lam_im * lam_im
    nr, ni = a_re - 1.0, a_im
    c_re = (nr * lam_re + ni * lam_im) / den
    c_im = (ni * lam_re - nr * lam_im) / den
    bu_re = jnp.einsum('blgh,gph->blgp', uf, p['ssm_b_re'].astype(jnp.float32))
    bu_im = jnp.einsum('blgh,gph->blgp', uf, p['ssm_b_im'].astype(jnp.float32))
    b_re = c_re * bu_re - c_im * bu_im
    b_im = c_re * bu_im + c_im * bu_re
    s0r = s0_re.astype(jnp.float32)
    s0i = s0_im.astype(jnp.float32)
    b_re = b_re.at[:, 0].add(a_re * s0r - a_im * s0i)
    b_im = b_im.at[:, 0].add(a_re * s0i + a_im * s0r)
    ar = jnp.broadcast_to(a_re, b_re.shape)
    ai = jnp.broadcast_to(a_im, b_im.shape)

    def combine(e1, e2):
        a1r, a1i, b1r, b1i = e1
        a2r, a2i, b2r, b2i = e2
        return (a2r * a1r - a2i * a1i, a2r * a1i + a2i * a1r,
                a2r * b1r - a2i * b1i + b2r, a2r * b1i + a2i * b1r + b2i)

    _, _, h_re, h_im = lax.associative_scan(combine, (ar, ai, b_re, b_im), axis=1)
    y = (jnp.einsum('blgp,ghp->blgh', h_re, p['ssm_c_re'].astype(jnp.float32))
         - jnp.einsum('blgp,ghp->blgh', h_im, p['ssm_c_im'].astype(jnp.float32))
         + p['ssm_d'].astype(jnp.float32) * uf)
    return y.astype(u.dtype), h_re[:, -1], h_im[:, -1]

def parallel_mixer(xn, pos, past_kv, s0_re, s0_im, p):
    B, L, _ = xn.shape
    z = xn @ p['w_in']
    q = z[..., :ATTN_WIDTH].reshape(B, L, N_ATTN_HEADS, HEAD_DIM)
    k = z[..., ATTN_WIDTH:2 * ATTN_WIDTH].reshape(B, L, N_ATTN_HEADS, HEAD_DIM)
    v = z[..., 2 * ATTN_WIDTH:3 * ATTN_WIDTH].reshape(B, L, N_ATTN_HEADS, HEAD_DIM)
    u = z[..., 3 * ATTN_WIDTH:].reshape(B, L, SSM_GROUPS, SSM_GROUP)
    q = rope_partial(rmsnorm(q, p['q_norm']), pos) * (HEAD_DIM ** -0.5)
    k = rope_partial(rmsnorm(k, p['k_norm']), pos)
    outs, lses, new_kv = [], [], []
    for g, (win, dil) in enumerate(ATTN_GROUPS):
        hs = slice(g * HEADS_PER_GROUP, (g + 1) * HEADS_PER_GROUP)
        qg, kg, vg = q[:, :, hs], k[:, :, hs], v[:, :, hs]
        if past_kv is None:
            o, lse = dilated_attn_prompt(qg, kg, vg, win, dil)
            keep = min(win, L)
            new_kv.append(jnp.stack([kg[:, L - keep:], vg[:, L - keep:]], axis=2))
        else:
            buf = past_kv[g]
            k_all = jnp.concatenate([buf[:, :, 0], kg], axis=1)
            v_all = jnp.concatenate([buf[:, :, 1], vg], axis=1)
            o, lse = dilated_attn_sample(qg, k_all, v_all, win, dil, buf.shape[1])
            new_kv.append(jnp.stack([kg, vg], axis=2))
        outs.append(o)
        lses.append(lse)
    alpha = jax.nn.softmax(jnp.stack(lses, axis=2), axis=2)
    attn = (jnp.stack(outs, axis=2) * alpha[..., None].astype(xn.dtype)).reshape(B, L, ATTN_WIDTH)
    y, h_re, h_im = s5_scan(u, s0_re, s0_im, p)
    zs = jax.nn.gelu(y.reshape(B, L, SSM_WIDTH))
    ssm_out = zs * jax.nn.sigmoid(zs @ p['w_glu'] + p['b_glu'])
    mixed = jnp.concatenate([rmsnorm(attn, p['attn_out_norm']), rmsnorm(ssm_out, p['ssm_out_norm'])], axis=-1)
    return mixed @ p['w_out'], new_kv, h_re, h_im

def memory_kv(mem, p):
    B = mem.shape[0]
    kv = (rmsnorm(mem, p['norm_mem']) @ p['w_xkv']).reshape(B, N_MEM, 2, X_HEADS, X_HEAD_DIM)
    return jnp.stack([rmsnorm(kv[:, :, 0], p['xk_norm']), kv[:, :, 1]], axis=2)

def cross_attention(hn, mkv, p):
    B, L, _ = hn.shape
    q = rmsnorm((hn @ p['w_xq']).reshape(B, L, X_HEADS, X_HEAD_DIM), p['xq_norm']) * (X_HEAD_DIM ** -0.5)
    s = jnp.einsum('blhe,bmhe->bhlm', q, mkv[:, :, 0], preferred_element_type=jnp.float32)
    pr = jax.nn.softmax(s, axis=-1)
    o = jnp.einsum('bhlm,bmhe->blhe', pr.astype(hn.dtype), mkv[:, :, 1]).reshape(B, L, D_MODEL)
    return o @ p['w_xo']

def conv_ffn(hn, conv_buf, p):
    up = hn @ p['w_up']
    L = up.shape[1]
    padded = jnp.concatenate([conv_buf.astype(up.dtype), up], axis=1)
    cw = p['conv_w']
    c = p['conv_b'] + sum(cw[i] * padded[:, i:i + L] for i in range(CONV_W))
    gate, val = jnp.split(c, 2, axis=-1)
    return (jax.nn.silu(gate) * val) @ p['w_down'], padded[:, -(CONV_W - 1):]

def decoder_layer(x, pos, past_kv, s0_re, s0_im, conv_buf, mkv, p):
    mix, new_kv, h_re, h_im = parallel_mixer(rmsnorm(x, p['norm_mix']), pos, past_kv, s0_re, s0_im, p)
    h = x + mix
    h = h + cross_attention(rmsnorm(h, p['norm_x']), mkv, p)
    f, new_conv = conv_ffn(rmsnorm(h, p['norm_ffn']), conv_buf, p)
    return h + f, new_kv, h_re, h_im, new_conv

def setup_inputs(seed: int = 0) -> dict:
    key = jax.random.key(seed)
    ks = iter(jax.random.split(key, 64))
    f32 = jnp.float32

    def nrm(shape, scale):
        return scale * jax.random.normal(next(ks), shape, f32)

    def gain(shape):
        return 1.0 + 0.02 * jax.random.normal(next(ks), shape, f32)

    bufs = [min(w, PAST_LEN) for w, _ in ATTN_GROUPS]
    G, P, H = SSM_GROUPS, SSM_STATE, SSM_GROUP
    lam_im = jnp.pi * jnp.broadcast_to(jnp.arange(P, dtype=f32), (DEPTH, G, P))
    return {
        'x_prompt': nrm((BATCH, SEQ, D_MODEL), 1.0),
        'x_sample': nrm((DEC_BATCH, DEC_SEQ, D_MODEL), 1.0),
        'mem_prompt': nrm((BATCH, N_MEM, D_MODEL), 1.0),
        'cache_kv_dil1': nrm((DEPTH, DEC_BATCH, bufs[0], 2, HEADS_PER_GROUP, HEAD_DIM), 1.0),
        'cache_kv_dil4': nrm((DEPTH, DEC_BATCH, bufs[1], 2, HEADS_PER_GROUP, HEAD_DIM), 1.0),
        'cache_kv_dil16': nrm((DEPTH, DEC_BATCH, bufs[2], 2, HEADS_PER_GROUP, HEAD_DIM), 1.0),
        'state_ssm_re': nrm((DEPTH, DEC_BATCH, G, P), 0.5),
        'state_ssm_im': nrm((DEPTH, DEC_BATCH, G, P), 0.5),
        'state_ffn_conv': nrm((DEPTH, DEC_BATCH, CONV_W - 1, 2 * D_FF), 1.0),
        'cache_mem_kv': nrm((DEPTH, DEC_BATCH, N_MEM, 2, X_HEADS, X_HEAD_DIM), 1.0),
        'norm_mix': gain((DEPTH, D_MODEL)),
        'w_in': nrm((DEPTH, D_MODEL, IN_WIDTH), D_MODEL ** -0.5),
        'q_norm': gain((DEPTH, HEAD_DIM)),
        'k_norm': gain((DEPTH, HEAD_DIM)),
        'ssm_lam_re': -0.5 + nrm((DEPTH, G, P), 0.01),
        'ssm_lam_im': lam_im + nrm((DEPTH, G, P), 0.01),
        'ssm_log_dt': jax.random.uniform(next(ks), (DEPTH, G), f32, math.log(1e-3), math.log(1e-1)),
        'ssm_b_re': nrm((DEPTH, G, P, H), (2 * H) ** -0.5),
        'ssm_b_im': nrm((DEPTH, G, P, H), (2 * H) ** -0.5),
        'ssm_c_re': nrm((DEPTH, G, H, P), P ** -0.5),
        'ssm_c_im': nrm((DEPTH, G, H, P), P ** -0.5),
        'ssm_d': nrm((DEPTH, G, H), 1.0),
        'w_glu': nrm((DEPTH, SSM_WIDTH, SSM_WIDTH), SSM_WIDTH ** -0.5),
        'b_glu': nrm((DEPTH, SSM_WIDTH), 0.01),
        'attn_out_norm': gain((DEPTH, ATTN_WIDTH)),
        'ssm_out_norm': gain((DEPTH, SSM_WIDTH)),
        'w_out': nrm((DEPTH, D_MODEL, D_MODEL), D_MODEL ** -0.5),
        'norm_x': gain((DEPTH, D_MODEL)),
        'norm_mem': gain((DEPTH, D_MODEL)),
        'w_xq': nrm((DEPTH, D_MODEL, D_MODEL), D_MODEL ** -0.5),
        'w_xkv': nrm((DEPTH, D_MODEL, 2 * D_MODEL), D_MODEL ** -0.5),
        'xq_norm': gain((DEPTH, X_HEAD_DIM)),
        'xk_norm': gain((DEPTH, X_HEAD_DIM)),
        'w_xo': nrm((DEPTH, D_MODEL, D_MODEL), D_MODEL ** -0.5),
        'norm_ffn': gain((DEPTH, D_MODEL)),
        'w_up': nrm((DEPTH, D_MODEL, 2 * D_FF), D_MODEL ** -0.5),
        'conv_w': nrm((DEPTH, CONV_W, 2 * D_FF), CONV_W ** -0.5),
        'conv_b': nrm((DEPTH, 2 * D_FF), 0.01),
        'w_down': nrm((DEPTH, D_FF, D_MODEL), D_FF ** -0.5),
    }

def reference(x_prompt, x_sample, mem_prompt, cache_kv_dil1, cache_kv_dil4, cache_kv_dil16,
              state_ssm_re, state_ssm_im, state_ffn_conv, cache_mem_kv,
              norm_mix, w_in, q_norm, k_norm, ssm_lam_re, ssm_lam_im, ssm_log_dt,
              ssm_b_re, ssm_b_im, ssm_c_re, ssm_c_im, ssm_d, w_glu, b_glu,
              attn_out_norm, ssm_out_norm, w_out, norm_x, norm_mem, w_xq, w_xkv,
              xq_norm, xk_norm, w_xo, norm_ffn, w_up, conv_w, conv_b, w_down):
    Bp, Lp = x_prompt.shape[0], x_prompt.shape[1]
    pos_p = jnp.arange(Lp)
    pos_s = PAST_LEN + jnp.arange(x_sample.shape[1])
    yp, ys = x_prompt, x_sample
    n_g = len(ATTN_GROUPS)
    kv_p = [[] for _ in range(n_g)]
    kv_s = [[] for _ in range(n_g)]
    re_p, im_p, conv_p, mem_p = [], [], [], []
    re_s, im_s, conv_s = [], [], []
    for l in range(DEPTH):
        p = dict(norm_mix=norm_mix[l], w_in=w_in[l], q_norm=q_norm[l], k_norm=k_norm[l],
                 ssm_lam_re=ssm_lam_re[l], ssm_lam_im=ssm_lam_im[l], ssm_log_dt=ssm_log_dt[l],
                 ssm_b_re=ssm_b_re[l], ssm_b_im=ssm_b_im[l], ssm_c_re=ssm_c_re[l], ssm_c_im=ssm_c_im[l],
                 ssm_d=ssm_d[l], w_glu=w_glu[l], b_glu=b_glu[l], attn_out_norm=attn_out_norm[l],
                 ssm_out_norm=ssm_out_norm[l], w_out=w_out[l], norm_x=norm_x[l], norm_mem=norm_mem[l],
                 w_xq=w_xq[l], w_xkv=w_xkv[l], xq_norm=xq_norm[l], xk_norm=xk_norm[l], w_xo=w_xo[l],
                 norm_ffn=norm_ffn[l], w_up=w_up[l], conv_w=conv_w[l], conv_b=conv_b[l], w_down=w_down[l])
        mkv_p = memory_kv(mem_prompt, p)
        s0 = jnp.zeros((Bp, SSM_GROUPS, SSM_STATE), jnp.float32)
        cb0 = jnp.zeros((Bp, CONV_W - 1, 2 * D_FF), yp.dtype)
        yp, nkv, hr, hi, nc = decoder_layer(yp, pos_p, None, s0, s0, cb0, mkv_p, p)
        for g in range(n_g):
            kv_p[g].append(nkv[g])
        re_p.append(hr)
        im_p.append(hi)
        conv_p.append(nc)
        mem_p.append(mkv_p)
        past = (cache_kv_dil1[l], cache_kv_dil4[l], cache_kv_dil16[l])
        ys, nkv, hr, hi, nc = decoder_layer(ys, pos_s, past, state_ssm_re[l], state_ssm_im[l],
                                            state_ffn_conv[l], cache_mem_kv[l], p)
        for g in range(n_g):
            kv_s[g].append(nkv[g])
        re_s.append(hr)
        im_s.append(hi)
        conv_s.append(nc)
    kvp = [jnp.stack(a) for a in kv_p]
    kvs = [jnp.stack(a) for a in kv_s]
    return (yp, ys,
            kvp[0], kvp[1], kvp[2], jnp.stack(re_p), jnp.stack(im_p), jnp.stack(conv_p), jnp.stack(mem_p),
            kvs[0], kvs[1], kvs[2], jnp.stack(re_s), jnp.stack(im_s), jnp.stack(conv_s))


_drawn_inputs = setup_inputs


def setup_inputs(seed=0):
    import zlib

    import numpy as np

    out = dict(_drawn_inputs(seed))
    spreads = {}
    factors = {'q_norm': 4.835,
     'k_norm': 3.938,
     'ssm_lam_re': 43.22,
     'b_glu': 8.0,
     'attn_out_norm': 4.315,
     'ssm_out_norm': 8.0,
     'norm_x': 8.0,
     'norm_mem': 2.744,
     'xq_norm': 8.0,
     'xk_norm': 3.911,
     'norm_ffn': 8.192,
     'conv_b': 29.147}
    for name, (base, spread) in spreads.items():
        noise = np.random.default_rng([zlib.crc32(name.encode()), seed]).standard_normal(out[name].shape)
        drawn = base * np.exp(spread * noise) if base else spread * noise
        out[name] = __import__('jax').numpy.asarray(drawn.astype(out[name].dtype))
    for name, factor in factors.items():
        out[name] = (out[name] * factor).astype(out[name].dtype)
    return out
```

```python
import math
from contextlib import ExitStack

import numpy as np
import concourse.bass as bass
from concourse import mybir

F32 = mybir.dt.float32
F32R = mybir.dt.float32r
ALU = mybir.AluOpType
ACT = mybir.ActivationFunctionType
AX = mybir.AxisListType

P = 128
D = 1024
KT = D // P
SEQ = 1024
NT = SEQ // P
DB, DT = 8, 4
TS = DB * DT
T = SEQ + TS
TILES = NT + 1
G = 3
H = 4
E = 64
GW = H * E
AW = G * GW
SW = D - AW
WB = 256
PAST = 1024
EPS = 1e-6
NEG = -1e30
X = 4
F = 2816


def rows(t):
    return P if t < NT else TS


STRIDE = [1, 4, 8, 8]


def first_token(order, t):
    return (P * t, t // 2 + 4 * P * (t % 2), t, t)[order]


def columns(ap, order, t):
    if t == NT:
        return ap[..., SEQ:T]
    first = first_token(order, t)
    return ap[..., first:first + STRIDE[order] * (P - 1) + 1:STRIDE[order]]


def linker(eng, sem):
    count = [0]

    def link(ins):
        count[0] += 1
        ins.then_inc(sem, 1)
        eng.wait_ge(sem, count[0])
    return link


def per_head(ap, n):
    return ap.unsqueeze(2).to_broadcast([n, H, E])


def block_project(nc, I, O, S):
    XH, XL, WH, WL, wstage = S["XH"], S["XL"], S["WH"], S["WL"], S["wstage"]
    ident, gain_bc, qk_gain, rope, mask = S["ident"], S["gain_bc"], S["qk_gain"], S["rope"], S["mask"]
    qT, kT, V, U, US, att = S["qT"], S["kT"], S["V"], S["U"], S["US"], S["att"]
    qkS, vS, negm, lsum = S["qkS"], S["vS"], S["negm"], S["lsum"]
    bank = S["bank"]
    MM, TR, SC, OB = bank[0:3], bank[3:5], bank[5:7], bank[7]
    QK = [(b, t) for b in range(9) if b % 3 < 2 for t in range(TILES)]
    qk_at = {bt: n for n, bt in enumerate(QK)}

    with ExitStack() as c:
        def sb(name, shape, dt=F32):
            return c.enter_context(nc.sbuf_tensor(name, shape, dt))

        def sem(name):
            return nc.alloc_semaphore(name)

        ssq = sb("ssq", [P, 3, TILES])
        zs = sb("zs", [P, 3, GW])
        zsq = sb("zsq", [P, 2, GW])
        zn = sb("zn", [P, 3, GW])
        zt = sb("zt", [P, 2, H, 16])
        zr = sb("zr", [P, 2, len(QK), H])
        rl = sb("rl", [P, G * NT, H])
        with ExitStack() as early:
            xin = early.enter_context(nc.sbuf_tensor("xin", [P, 2, D], F32))
            junk = early.enter_context(nc.sbuf_tensor("junk", [P, D], F32))
        Sm = sb("Sm", [P, 2, H, 2 * P])
        PT = sb("PT", [P, 2, 2 * H, P])

        x_ld = [sem(f"x_ld{i}") for i in range(2)]
        x_sq = sem("x_sq")
        x_rt = sem("x_rt")
        x_n = sem("x_n")
        x_tr = sem("x_tr")
        x_hi = sem("x_hi")
        x_lo = sem("x_lo")
        w_ld = sem("w_ld")
        w_hi = sem("w_hi")
        w_lo = sem("w_lo")
        mm = sem("mm")
        ev = sem("ev")
        z_sq = sem("z_sq")
        z_ms = sem("z_ms")
        z_rt = sem("z_rt")
        z_n = sem("z_n")
        z_tr = sem("z_tr")
        z_T = sem("z_T")
        k_st = [sem(f"k_st{i}") for i in range(3)]
        v_st = sem("v_st")
        at_s = sem("at_s")
        at_mask = sem("at_mask")
        at_m = sem("at_m")
        at_e = sem("at_e")
        at_tr = sem("at_tr")
        at_pa = sem("at_pa")
        at_pb = sem("at_pb")
        at_pv = sem("at_pv")
        at_o = sem("at_o")
        tab = sem("tab")
        c_dve = sem("c_dve")
        c_act = sem("c_act")
        zero = sem("zero")

        norm_at = {b * TILES + t + 1: q for q, (b, t) in enumerate(QK)}
        take_at = {b * TILES + t + 2: q for q, (b, t) in enumerate(QK)}

        def wcols(b):
            return (b % 3) * AW + (b // 3) * GW if b < 9 else 3 * AW

        def key_tiles(g, i):
            return [i - 1, i] if (g == 0 and i > 0) or (g == 1 and i % 2) else [i]

        start = [TILES * (3 * (a // NT) + 2) + 1 + 2 * (a % NT) for a in range(G * NT)]
        LAST = start[-1] + 4

        def due(s, after):
            return [a for a in range(G * NT) if start[a] + after == s]

        ab = []
        for a in range(G * NT):
            ab.append(len(key_tiles(a // NT, a % NT)))
        a_before = [sum(ab[:a]) for a in range(G * NT + 1)]
        b_before = [sum(x == 2 for x in ab[:a]) for a in range(G * NT + 1)]

        blk = c.enter_context(nc.Block())

        @blk.sync
        def _(sp):
            for i in range(TILES):
                if i >= 2:
                    sp.wait_ge(x_tr, 2 * (i - 1))
                src = I["x_prompt"][0, P * i:P * i + P, :] if i < NT else \
                    I["x_sample"].rearrange("b t d -> (b t) d")
                sp.dma_start(xin[:rows(i), i % 2, :], src).then_inc(x_ld[i % 2], 16)
                if i == 0:
                    for dst, src in S["tables"]:
                        sp.dma_start(dst, src).then_inc(tab, 16)
                if i == 1:
                    for b in range(1):
                        sp.dma_start(wstage[:], I["w_in"][0, :, wcols(b):wcols(b) + WB]
                                     .rearrange("(k p) n -> p k n", p=P)).then_inc(w_ld, 16)
            for b in range(1, 10):
                sp.wait_ge(w_lo, b)
                sp.dma_start(wstage[:], I["w_in"][0, :, wcols(b):wcols(b) + WB]
                             .rearrange("(k p) n -> p k n", p=P)).then_inc(w_ld, 16)

        @blk.gpsimd
        def _(pool):
            nc.gpsimd.memset(S["eps"][:], EPS).then_inc(zero, 1)
            stored = [0, 0, 0]
            vs = 0
            late = []
            for b in range(9):
                g, kind = b // 3, b % 3
                for t in range(TILES):
                    s, n = b * TILES + t, rows(t)
                    if kind < 2:
                        q = qk_at[b, t]
                        pool.wait_ge(ev, s + 1)
                        if q >= 2:
                            pool.wait_ge(z_ms, q - 1)
                        nc.gpsimd.tensor_tensor(zsq[:n, q % 2], zs[:n, q % 3], zs[:n, q % 3], ALU.mult)\
                            .then_inc(z_sq, 1)
                    for dst, src, j in late:
                        pool.wait_ge(z_n, j + 1)
                        pool.dma_start(dst, src).then_inc(k_st[j % 3], 16)
                        stored[j % 3] += 16
                    late = []
                    if kind == 1:
                        late = [(dst, zn[lo:hi, q % 3], q) for dst, lo, hi in cache_rows(O, g, t, 0)]
                    if kind == 2:
                        for dst, lo, hi in cache_rows(O, g, t, 1):
                            pool.wait_ge(ev, s + 1)
                            pool.dma_start(dst, V[lo:hi, t] if t < NT else vS[lo:hi, g]).then_inc(v_st, 16)
                            vs += 16
            for i in range(3):
                pool.wait_ge(k_st[i], stored[i])
            pool.wait_ge(v_st, vs)

        k_stores = [0] * len(QK)
        for q, (b, t) in enumerate(QK):
            k_stores[q] = sum(16 * len(cache_rows(O, QK[r][0] // 3, QK[r][1], 0))
                              for r in range(q) if r % 3 == q % 3 and QK[r][0] % 3 == 1)
        v_stores = [sum(16 * len(cache_rows(O, gg, t, 1)) for gg in range(g) for t in range(TILES))
                    for g in range(G + 1)]

        def split_weights_act(act, b):
            act.wait_ge(w_ld, 16 * (b + 1))
            if b >= 2:
                act.wait_ge(mm, (b - 1) * TILES)
            nc.scalar.activation(WH[:, b % 2], wstage[:], ACT.Copy).then_inc(w_hi, 1)

        @blk.scalar
        def _(act):
            link = linker(act, c_act)
            nc.scalar.preload_act_table_set("natural_log_exp_and_others")
            act.wait_ge(zero, 1)

            def rsqrt_of_mean(sums, out, width):
                n = sums.shape[0]
                link(nc.scalar.activation(out, sums, ACT.Ln, scale=1.0 / width, bias=S["eps"][:n]))
                return nc.scalar.activation(out, out, ACT.Exp, scale=-0.5)

            for i in range(TILES + 1):
                if i < TILES:
                    n = rows(i)
                    act.wait_ge(x_ld[i % 2], 16 * (i // 2 + 1))
                    if i:
                        act.wait_ge(x_sq, i)
                    nc.scalar.activation(junk[:n], xin[:n, i % 2], ACT.Square,
                                         accum_out=ssq[:n, 0, i:i + 1]).then_inc(x_sq, 1)
                    act.wait_ge(x_sq, i + 1)
                    rsqrt_of_mean(ssq[:n, 0, i:i + 1], ssq[:n, 1, i:i + 1], D).then_inc(x_rt, 1)
                if i > 0:
                    n = rows(i - 1)
                    for half in range(2):
                        act.wait_ge(x_tr, 2 * (i - 1) + half + 1)
                        nc.scalar.activation(XH[:, 4 * half:4 * half + 4, P * (i - 1):P * (i - 1) + n],
                                             TR[half][:, 0:4 * P].rearrange("p (k n) -> p k n", k=4)[:, :, :n],
                                             ACT.Copy).then_inc(x_hi, 1)
                if i == 2:
                    split_weights_act(act, 0)
            split_weights_act(act, 1)

            def attend(a):
                g, i = a // NT, a % NT
                nk = P * len(key_tiles(g, i))
                act.wait_ge(at_m, a + 1)
                for h in range(H):
                    last = nc.scalar.activation(Sm[:, a % 2, h, :nk], Sm[:, a % 2, h, :nk], ACT.Exp,
                                                bias=negm[:, a, h:h + 1], accum_out=lsum[:, a, h:h + 1])
                last.then_inc(at_e, 1)

            def take_probabilities(a):
                act.wait_ge(at_tr, a_before[a] + 1)
                if a >= 2:
                    act.wait_ge(at_pv, a - 1)
                nc.scalar.activation(PT[:, a % 2, 0:4, :], TR[0][:, :].rearrange("p (k n) -> p k n", k=4),
                                     ACT.Copy).then_inc(at_pa, 1)

            def take_q_or_k(q):
                b, t = QK[q]
                g, n = b // 3, rows(t)
                act.wait_ge(z_tr, q + 1)
                src = TR[q % 2][:, 0:2 * P].rearrange("p (k n) -> p k n", k=2)[:, :, :n]
                dst = (qT, kT)[b % 3][:, :, P * t:P * t + n] if t < NT else qkS[:, g, b % 3]
                nc.scalar.activation(dst, src, ACT.Copy).then_inc(z_T, 1)

            for s in range(LAST):
                b, t = s // TILES, s % TILES
                g, kind, n = b // 3, b % 3, rows(t)
                if b < 10:
                    src = MM[s % 3][:n, 0:WB]
                    if b == 9:
                        dst = U[:, :, t] if t < NT else US[:, :].rearrange("p (g h) -> p g h", g=16)
                        src = src.rearrange("p (g h) -> p g h", g=16)
                    elif kind < 2:
                        q = qk_at[b, t]
                        if q >= 3:
                            act.wait_ge(z_n, q - 2)
                            act.wait_ge(z_sq, q - 2)
                        dst = zs[:n, q % 3]
                    else:
                        if t == 0 and g:
                            act.wait_ge(v_st, v_stores[g])
                            act.wait_ge(at_pv, NT * g)
                        dst = V[:n, t] if t < NT else vS[:n, g]
                    act.wait_ge(mm, s + 1)
                    nc.scalar.activation(dst, src, ACT.Copy).then_inc(ev, 1)
                    if s in take_at:
                        take_q_or_k(take_at[s])
                    if s in norm_at:
                        q = norm_at[s]
                        n_q = rows(QK[q][1])
                        act.wait_ge(z_ms, q + 1)
                        rsqrt_of_mean(zr[:n_q, 0, q], zr[:n_q, 1, q], E).then_inc(z_rt, 1)
                for a in due(s, 1):
                    attend(a)
                for a in due(s, 2):
                    take_probabilities(a)
                if t == 2 and 1 <= b < 9:
                    split_weights_act(act, b + 1)

        @blk.vector
        def _(dve):
            link = linker(dve, c_dve)
            dve.wait_ge(tab, 16 * len(S["tables"]))
            link(nc.vector.tensor_scalar(qk_gain[:, 0], qk_gain[:, 0], E ** -0.5, None, ALU.mult))

            def split_weights(b):
                dve.wait_ge(w_hi, b + 1)
                nc.vector.tensor_tensor(WL[:, b % 2], wstage[:], WH[:, b % 2].bitcast(F32), ALU.subtract)\
                    .then_inc(w_lo, 1)

            for i in range(TILES + 1):
                if i < TILES:
                    n = rows(i)
                    dve.wait_ge(x_rt, i + 1)
                    nc.vector.scalar_tensor_tensor(xin[:n, i % 2], xin[:n, i % 2], ssq[:n, 1, i:i + 1],
                                                   gain_bc[:n], ALU.mult, ALU.mult).then_inc(x_n, 1)
                if i > 0:
                    n = rows(i - 1)
                    for half in range(2):
                        dve.wait_ge(x_hi, 2 * (i - 1) + half + 1)
                        ks, ts = slice(4 * half, 4 * half + 4), slice(P * (i - 1), P * (i - 1) + n)
                        nc.vector.tensor_tensor(XL[:, ks, ts],
                                                TR[half][:, 0:4 * P].rearrange("p (k n) -> p k n", k=4)[:, :, :n],
                                                XH[:, ks, ts].bitcast(F32), ALU.subtract).then_inc(x_lo, 1)
                if i == 2:
                    split_weights(0)
            split_weights(1)

            def sum_squares(q):
                n = rows(QK[q][1])
                dve.wait_ge(z_sq, q + 1)
                nc.vector.tensor_reduce(zr[:n, 0, q], zsq[:n, q % 2].rearrange("p (h e) -> p h e", h=H),
                                        AX.X, ALU.add).then_inc(z_ms, 1)

            def norm_and_rotate(q):
                b, t = QK[q]
                g, kind, n = b // 3, b % 3, rows(t)
                z = zn[:n, q % 3].rearrange("p (h e) -> p h e", h=H)
                dve.wait_ge(z_rt, q + 1)
                if q >= 3:
                    dve.wait_ge(z_tr, q - 2)
                    if k_stores[q]:
                        dve.wait_ge(k_st[q % 3], k_stores[q])
                link(nc.vector.tensor_tensor(z, zs[:n, q % 3].rearrange("p (h e) -> p h e", h=H),
                                             per_head(zr[:n, 1, q], n), ALU.mult))
                link(nc.vector.tensor_tensor(z, z, qk_gain[:n, kind].unsqueeze(1).to_broadcast([n, H, E]),
                                             ALU.mult))
                r = rope[:n, g * NT + t if t < NT else G * NT]
                cos, sin = r[:, 0:16], r[:, 16:32]
                nc.vector.tensor_tensor(zt[:n, 0], z[:, :, 0:16], cos.unsqueeze(1).to_broadcast([n, H, 16]),
                                        ALU.mult)
                nc.vector.tensor_tensor(zt[:n, 1, :, 0:8], z[:, :, 8:16],
                                        sin[:, 0:8].unsqueeze(1).to_broadcast([n, H, 8]), ALU.mult)
                link(nc.vector.tensor_tensor(zt[:n, 1, :, 8:16], z[:, :, 0:8],
                                             sin[:, 8:16].unsqueeze(1).to_broadcast([n, H, 8]), ALU.mult))
                nc.vector.tensor_tensor(z[:, :, 0:16], zt[:n, 0], zt[:n, 1], ALU.add).then_inc(z_n, 1)

            def mask_and_max(a):
                g, i = a // NT, a % NT
                nk = P * len(key_tiles(g, i))
                m = mask[:, 0:2 * P] if nk == 2 * P else (mask[:, P:2 * P] if g < 2 else mask[:, 2 * P:3 * P])
                dve.wait_ge(at_s, a + 1)
                if a >= 2:
                    dve.wait_ge(at_tr, a_before[a - 1])
                for j in range(2):
                    ins = nc.vector.tensor_tensor(
                        Sm[:, a % 2, j::2, :nk], SC[j][:, :].rearrange("p (h n) -> p h n", h=2)[:, :, :nk],
                        m.unsqueeze(1).to_broadcast([P, 2, nk]), ALU.add)
                    if j == 0:
                        link(ins)
                ins.then_inc(at_mask, 1)
                dve.wait_ge(at_mask, a + 1)
                nc.vector.tensor_reduce(negm[:, a], Sm[:, a % 2, :, :nk], AX.X, ALU.max, negate=True)\
                    .then_inc(at_m, 1)

            def take_probabilities(a):
                if ab[a] == 2:
                    dve.wait_ge(at_tr, a_before[a + 1])
                    if a >= 2:
                        dve.wait_ge(at_pv, a - 1)
                    nc.vector.tensor_copy(PT[:, a % 2, 4:8, :], TR[1][:, :].rearrange("p (k n) -> p k n", k=4))\
                        .then_inc(at_pb, 1)

            def take_output(a):
                dve.wait_ge(at_e, a + 1)
                link(nc.vector.reciprocal(rl[:, a], lsum[:, a]))
                dve.wait_ge(at_pv, a + 1)
                nc.vector.tensor_tensor(att[:, a].rearrange("p (h e) -> p h e", h=H),
                                        OB[:, 0:GW].rearrange("p (h e) -> p h e", h=H),
                                        per_head(rl[:, a], P), ALU.mult).then_inc(at_o, 1)

            for s in range(LAST):
                b, t = s // TILES, s % TILES
                if (b, t) in qk_at:
                    sum_squares(qk_at[b, t])
                if s in norm_at:
                    norm_and_rotate(norm_at[s])
                for a in due(s, 3):
                    take_output(a)
                for a in due(s, 0):
                    mask_and_max(a)
                for a in due(s, 2):
                    take_probabilities(a)
                if t == 2 and 1 <= b < 9:
                    split_weights(b + 1)

        @blk.tensor
        def _(pe):
            last_reader = [None, None]

            def claim(j, sem_, value):
                if last_reader[j]:
                    pe.wait_ge(*last_reader[j])
                last_reader[j] = (sem_, value)

            pe.wait_ge(tab, 16 * len(S["tables"]))
            for i in range(TILES):
                n = rows(i)
                pe.wait_ge(x_n, i + 1)
                for half in range(2):
                    claim(half, x_lo, 2 * i + half + 1)
                    for k in range(4):
                        ks = 4 * half + k
                        ins = nc.tensor.transpose(TR[half][:, P * k:P * k + n],
                                                  xin[:n, i % 2, P * ks:P * ks + P], ident[:n, :n])
                    ins.then_inc(x_tr, 1)

            def transpose_qk(q):
                n = rows(QK[q][1])
                pe.wait_ge(z_n, q + 1)
                claim(q % 2, z_T, q + 1)
                for k in range(2):
                    ins = nc.tensor.transpose(TR[q % 2][:, P * k:P * k + n], zn[:n, q % 3, P * k:P * k + P],
                                              ident[:n, :n])
                ins.then_inc(z_tr, 1)

            def scores(a):
                g, i = a // NT, a % NT
                kt = key_tiles(g, i)
                nk = P * len(kt)
                if i == 0:
                    pe.wait_ge(z_T, 2 * TILES * (g + 1))
                if a:
                    pe.wait_ge(at_mask, a)
                for h in (0, 1, 2, 3):
                    e0 = E * (h % 2)
                    ins = nc.tensor.matmul(SC[h % 2][:, 2 * P * (h // 2):2 * P * (h // 2) + nk],
                                           qT[e0:e0 + E, h // 2, P * i:P * i + P],
                                           kT[e0:e0 + E, h // 2, P * kt[0]:P * kt[0] + nk],
                                           start=True, stop=True)
                ins.then_inc(at_s, 1)

            def transpose_p(a):
                nc_ = ab[a]
                pe.wait_ge(at_e, a + 1)
                for j in range(nc_):
                    claim(j, (at_pa, at_pb)[j], a + 1 if j == 0 else b_before[a + 1])
                    for x in range(4):
                        idx = 4 * j + x
                        h, ch = idx // nc_, idx % nc_
                        ins = nc.tensor.transpose(TR[j][:, P * x:P * x + P],
                                                  Sm[:, a % 2, h, P * ch:P * ch + P], ident[:, :])
                    ins.then_inc(at_tr, 1)

            def weigh(a):
                g, i = a // NT, a % NT
                kt = key_tiles(g, i)
                pe.wait_ge(ev, TILES * (3 * g + 2) + i + 1)
                pe.wait_ge(at_pa, a + 1)
                if b_before[a + 1]:
                    pe.wait_ge(at_pb, b_before[a + 1])
                if a:
                    pe.wait_ge(at_o, a)
                for h in range(H):
                    for ch, kt_ in enumerate(kt):
                        ins = nc.tensor.matmul(OB[:, E * h:E * h + E], PT[:, a % 2, h * len(kt) + ch],
                                               V[:, kt_, E * h:E * h + E],
                                               start=ch == 0, stop=ch == len(kt) - 1)
                ins.then_inc(at_pv, 1)

            for s in range(LAST):
                b, t = s // TILES, s % TILES
                g, n = b // 3, rows(t)
                if b < 10:
                    if t == 0:
                        pe.wait_ge(w_lo, b + 1)
                    if b == 0:
                        pe.wait_ge(x_lo, 2 * (t + 1))
                    if s >= 3:
                        pe.wait_ge(ev, s - 2)
                    for k in range(KT):
                        xh, xl = columns(XH[:, k], g, t), columns(XL[:, k], g, t)
                        for j, (x, w) in enumerate(((xh, WH), (xh, WL), (xl, WH))):
                            ins = nc.tensor.matmul(MM[s % 3][:n, 0:WB], x, w[:, b % 2, k],
                                                   start=k == 0 and j == 0, stop=k == KT - 1 and j == 2)
                    ins.then_inc(mm, 1)
                    if s in take_at:
                        transpose_qk(take_at[s])
                for a in due(s, 3):
                    weigh(a)
                for a in due(s, 0):
                    scores(a)
                for a in due(s, 2):
                    transpose_p(a)


def block_ssm(nc, I, O, S):
    ident, gain_bc, U, US, ysb = S["ident"], S["gain_bc"], S["U"], S["US"], S["ysb"]
    bank = S["bank"]
    (BpR, BpI, ER, EI, XR, XI, HR, HI, ta, tb, BAR, BAI) = S["ssm_over"]
    CH, GH = 8, 8
    NC = SEQ // CH
    INV_2PI = 1.0 / (2 * math.pi)
    MAGIC = 1.5 * 2.0 ** 23
    PI_A, PI_B, PI_C = 6.28125, 0.0019350051879882812, 3.019916050e-7
    assert abs(PI_A + PI_B + PI_C - 2 * math.pi) < 1e-11

    with ExitStack() as c:
        def sb(name, shape, dt=F32):
            return c.enter_context(nc.sbuf_tensor(name, shape, dt))

        def sem(name):
            return nc.alloc_semaphore("s2_" + name)

        lamR, lamI, dt_ = sb("lamR", [P, GH]), sb("lamI", [P, GH]), sb("dt_", [P, GH])
        Bin = sb("Bin", [P, 2, GH, 16])
        Cin = sb("Cin", [16, 2, 16, 64])
        Dbc = sb("Dbc", [P, SW])
        bglu = sb("bglu", [P, SW])
        wglu = sb("wglu", [P, 2, SW])
        USp = sb("USp", [DB, 16, CH, 16])
        sm = sb("sm", [P, 24, GH])
        PR, PI = sb("PR", [P, 9, GH]), sb("PI", [P, 9, GH])
        QR, QI = sb("QR", [P, 8, GH]), sb("QI", [P, 8, GH])
        CI_ = sb("CI_", [P, 2, GH, 16])
        H0 = sb("H0", [P, 2, GH, DB])
        CAR, CAI, WBR, WBI, TZ, UT, Sin = S["ssm_mats"]
        MZ = S["MZ"]
        UTs = sb("UTs", [P, 16, DB])
        FR = sb("FR", [P, 2, GH, 9])
        hout = sb("hout", [9, 2, D])
        YS8 = sb("YS8", [DB, DT, SW])
        nrm = sb("nrm", [P, 3, TILES])

        ld = sem("ld")
        ld_us = sem("ld_us")
        us_zero = sem("us_zero")
        p_exp = sem("p_exp")
        p_ang = sem("p_ang")
        p_sin = sem("p_sin")
        p_unit = sem("p_unit")
        tz_zero, tz_st = sem("tz_zero"), sem("tz_st")
        t_in = sem("t_in")
        t_c = sem("t_c")
        bb = sem("bb")
        t_b = sem("t_b")
        wb = sem("wb")
        tz_p, tz = sem("tz_p"), sem("tz")
        u_p, u_t = sem("u_p"), sem("u_t")
        us_p = sem("us_p")
        l_p = sem("l_p")
        l_r = sem("l_r")
        e_tab = sem("e_tab")
        ud = sem("ud")
        h_ok = sem("h_ok")
        f_p, f_s, f_o = sem("f_p"), sem("f_s"), sem("f_o")
        y_p = sem("y_p")
        ys_c, ys_d = sem("ys_c"), sem("ys_d")
        y_ok, z_ok = sem("y_ok"), sem("z_ok")
        zt_p, zt_c, gl_p, gl_s = sem("zt_p"), sem("zt_c"), sem("gl_p"), sem("gl_s")
        sg, so, so_q, so_m, so_r, so_n = (sem(x) for x in ("sg", "so", "so_q", "so_m", "so_r", "so_n"))
        c_dve, c_act, c_pool = sem("c_dve"), sem("c_act"), sem("c_pool")
        n_ld = 20
        zT = sb("zT", [P, 2, 2, P])
        glS = sb("glS", [TS, SW])

        def gate(j):
            return (XR if j < 4 else XI)[:, (2 * (j % 4)):(2 * (j % 4)) + 2, :].rearrange("p a b -> p (a b)") \
                if j < NT else glS[:]

        blk = c.enter_context(nc.Block())

        @blk.sync
        def _(sp):
            n = 0
            for gl_ in range(2):
                ps = slice(64 * gl_, 64 * gl_ + 64)
                for dst, name in ((lamR, "ssm_lam_re"), (lamI, "ssm_lam_im")):
                    sp.dma_start(dst[ps], I[name][0].rearrange("(g l) p -> l p g", l=2)[gl_],
                                 allow_slow_non_contiguous=True).then_inc(ld, 16)
                sp.dma_start(dt_[ps], I["ssm_log_dt"][0].rearrange("(g l) -> l g", l=2)[gl_]
                             .partition_broadcast(64), allow_slow_non_contiguous=True).then_inc(ld, 16)
                for j, name in enumerate(("ssm_b_re", "ssm_b_im")):
                    sp.dma_start(Bin[ps, j], I[name][0].rearrange("(g l) p h -> l p g h", l=2)[gl_])\
                        .then_inc(ld, 16)
                n += 5
            for j, (cn, sn) in enumerate((("ssm_c_re", "state_ssm_re"), ("ssm_c_im", "state_ssm_im"))):
                sp.dma_start(Cin[:, j], I[cn][0].rearrange("g h p -> h g p")).then_inc(ld, 16)
                sp.dma_start(Sin[:, j], I[sn][0].rearrange("b g p -> b (g p)")).then_inc(ld, 16)
                n += 2
            sp.dma_start(Dbc[:], I["ssm_d"][0].rearrange("g h -> (g h)").partition_broadcast(P)).then_inc(ld, 16)
            sp.dma_start(bglu[:], I["b_glu"][0].partition_broadcast(P)).then_inc(ld, 16)
            sp.dma_start(wglu[:], I["w_glu"][0].rearrange("(k p) n -> p k n", p=P)).then_inc(ld, 16)
            sp.dma_start(gain_bc[:, 0:AW], I["attn_out_norm"][0].partition_broadcast(P)).then_inc(ld, 16)
            sp.dma_start(gain_bc[:, AW:D], I["ssm_out_norm"][0].partition_broadcast(P)).then_inc(ld, 16)
            n += 5
            assert n == n_ld - 1
            sp.wait_ge(us_zero, 1)
            for i in range(DT):
                sp.dma_start(USp[:, :, 4 + i, :], US[i:TS:DT].rearrange("b (g h) -> b g h", g=16))\
                    .then_inc(ld_us, 16)
            sp.wait_ge(tz, 4)
            sp.wait_ge(tz_zero, 1)
            for j in range(CH):
                sp.dma_start(TZ[16 * j:16 * j + 16, :, 16 * j:P], MZ[:, :, 0:P - 16 * j]).then_inc(tz_st, 16)
            sp.wait_ge(ys_c, 2)
            for i in range(DT):
                sp.dma_start(ysb[i:TS:DT, NT], YS8[:, i]).then_inc(ys_d, 16)
            sp.wait_ge(f_s, 4)
            for j, name in enumerate(("ssm_re", "ssm_im")):
                sp.dma_start(O[name + "_s"][0].rearrange("b g p -> b (g p)"), hout[0:DB, j]).then_inc(f_o, 16)
                sp.dma_start(O[name + "_p"][0].rearrange("b g p -> b (g p)"), hout[DB:DB + 1, j]).then_inc(f_o, 16)
            sp.wait_ge(f_o, 64)

        @blk.gpsimd
        def _(pool):
            link = linker(pool, c_pool)
            nc.gpsimd.memset(USp[:], 0.0).then_inc(us_zero, 1)
            nc.gpsimd.memset(TZ[:], 0.0).then_inc(tz_zero, 1)
            pool.wait_ge(ld, 16 * (n_ld - 1))
            d = Dbc[:].rearrange("p (g h) -> p g h", g=16)
            for a in range(2):
                gs = slice(8 * a, 8 * a + 8)
                nc.gpsimd.tensor_tensor((ta, tb)[a][:].rearrange("p g (j h) -> p g j h", j=8), U[:, gs],
                                        d[:, gs].unsqueeze(2).to_broadcast([P, 8, CH, 16]), ALU.mult)\
                    .then_inc(ud, 1)
            link(nc.gpsimd.memset(ER[:, :, 0:1], 1.0))
            link(nc.gpsimd.memset(EI[:, :, 0:1], 0.0))
            t = XR[:, :, 0:64], XR[:, :, 64:128], XI[:, :, 0:64], XI[:, :, 64:128]

            def times(oR, oI, aR, aI, bR, bI, n):
                x = [y[:, :, 0:n] for y in t]
                nc.gpsimd.tensor_tensor(x[0], aR, bR, ALU.mult)
                nc.gpsimd.tensor_tensor(x[1], aI, bI, ALU.mult)
                nc.gpsimd.tensor_tensor(x[2], aR, bI, ALU.mult)
                link(nc.gpsimd.tensor_tensor(x[3], aI, bR, ALU.mult))
                nc.gpsimd.tensor_tensor(oR, x[0], x[1], ALU.subtract)
                link(nc.gpsimd.tensor_tensor(oI, x[2], x[3], ALU.add))

            pool.wait_ge(p_unit, 1)
            w = [sm[:, k].unsqueeze(2) for k in (16, 17)]
            v = [sm[:, k].unsqueeze(2) for k in (18, 19)]
            times(v[0], v[1], w[0], w[1], w[0], w[1], 1)
            times(w[0], w[1], v[0], v[1], v[0], v[1], 1)
            times(ER[:, :, 1:2], EI[:, :, 1:2], w[0], w[1], w[0], w[1], 1)
            m = 2
            while m < NC:
                half = ER[:, :, m // 2:m // 2 + 1], EI[:, :, m // 2:m // 2 + 1]
                times(v[0], v[1], *half, *half, 1)
                b = [x.to_broadcast([P, GH, m]) for x in v]
                times(ER[:, :, m:2 * m], EI[:, :, m:2 * m], ER[:, :, 0:m], EI[:, :, 0:m], *b, m)
                m *= 2
            pool.sem_inc(e_tab, 1)

        @blk.scalar
        def _(act):
            act.wait_ge(ld, 16 * (n_ld - 1))
            link = linker(act, c_act)
            link(nc.scalar.activation(dt_[:], dt_[:], ACT.Exp))
            act.wait_ge(p_exp, 1)
            nc.scalar.activation(sm[:, 1], sm[:, 0], ACT.Exp).then_inc(p_exp, 1)
            act.wait_ge(p_ang, 1)
            nc.scalar.activation(sm[:, 16], sm[:, 5], ACT.Sin).then_inc(p_sin, 1)
            nc.scalar.activation(sm[:, 17], sm[:, 4], ACT.Sin).then_inc(p_sin, 1)
            act.wait_ge(t_in, 1)
            for j in range(2):
                nc.scalar.activation(CI_[:, j], bank[j][:, 0:P].rearrange("p (g h) -> p g h", g=GH), ACT.Copy)
            nc.scalar.activation(H0[:, :, :, :].rearrange("p a g b -> p (a g b)"), bank[2][:, 0:P], ACT.Copy)\
                .then_inc(t_c, 1)
            for q in range(4):
                act.wait_ge(u_p, q + 1)
                nc.scalar.activation(UT[:, 4 * q:4 * q + 4], bank[3 + q][:].rearrange("p (g n) -> p g n", g=4),
                                     ACT.Copy).then_inc(u_t, 1)
            act.wait_ge(us_p, 1)
            nc.scalar.activation(UTs[:], bank[7][:, 0:P].rearrange("p (g n) -> p g n", g=16), ACT.Copy)\
                .then_inc(u_t, 1)
            for q in range(4):
                act.wait_ge(t_b, q + 1)
                nc.scalar.activation((WBR, WBI)[q // 2][:, 4 * (q % 2):4 * (q % 2) + 4],
                                     bank[3 + q][:].rearrange("p (g n) -> p g n", g=4), ACT.Copy).then_inc(wb, 1)
            for q in range(4):
                act.wait_ge(tz_p, q + 1)
                gs = 8 * (q % 2) + q // 2
                nc.scalar.activation(MZ[:, gs:gs + 7:2],
                                     bank[(0, 1, 2, 7)[q]][0:16].rearrange("p (g n) -> p g n", g=4),
                                     ACT.Copy).then_inc(tz, 1)
            for q in range(4):
                act.wait_ge(f_p, q + 1)
                nc.scalar.activation(hout[:, q // 2, 512 * (q % 2):512 * (q % 2) + 512], bank[3 + q][0:9],
                                     ACT.Copy).then_inc(f_s, 1)
            for l in range(2):
                act.wait_ge(y_p, 5 + l)
                nc.scalar.activation(YS8[:].rearrange("b i (g l h) -> b l g i h", g=GH, l=2)[:, l],
                                     bank[5 + l][0:DB].rearrange("b (g i h) -> b g i h", g=GH, i=DT), ACT.Copy)\
                    .then_inc(ys_c, 1)
            act.wait_ge(y_ok, 5)
            nc.scalar.activation(ysb[:, 0:NT], ysb[:, 0:NT], ACT.Gelu_apprx_tanh)
            nc.scalar.activation(ysb[0:TS, NT], ysb[0:TS, NT], ACT.Gelu_apprx_tanh).then_inc(z_ok, 1)
            for j in range(TILES):
                n = rows(j)
                act.wait_ge(zt_p, j + 1)
                if j >= 2:
                    act.wait_ge(gl_p, j - 1)
                nc.scalar.activation(zT[:, j % 2, :, :n],
                                     bank[j % 2][:, 0:2 * P].rearrange("p (k n) -> p k n", k=2)[:, :, :n],
                                     ACT.Copy).then_inc(zt_c, 1)
            for j in range(TILES):
                act.wait_ge(gl_s, j + 1)
                nc.scalar.activation(gate(j)[:rows(j)], gate(j)[:rows(j)], ACT.Sigmoid).then_inc(sg, 1)
            for j in range(TILES):
                n = rows(j)
                act.wait_ge(so, j + 1)
                nc.scalar.activation(gate(j)[:n], ysb[:n, j], ACT.Square, accum_out=nrm[:n, 0, j:j + 1])\
                    .then_inc(so_q, 1)
            act.wait_ge(so_m, 2)
            nc.scalar.activation(nrm[:, 2, 0:NT], nrm[:, 1, 0:NT], ACT.Sqrt)
            nc.scalar.activation(nrm[0:TS, 2, NT:], nrm[0:TS, 1, NT:], ACT.Sqrt).then_inc(so_r, 1)

        @blk.vector
        def _(dve):
            link = linker(dve, c_dve)

            def tt(o, a, b, op=ALU.mult):
                link(nc.vector.tensor_tensor(o, a, b, op))

            def ts(o, a, s1, s2, op0, op1=None):
                link(nc.vector.tensor_scalar(o, a, s1, s2, op0, *([op1] if op1 else [])))

            x = [sm[:, k] for k in range(24)]
            dve.wait_ge(c_act, 1)
            nc.vector.tensor_tensor(x[0], lamR[:], dt_[:], ALU.mult).then_inc(p_exp, 1)
            tt(x[2], lamI[:], dt_[:])
            ts(x[3], x[2], INV_2PI, MAGIC, ALU.mult, ALU.add)
            ts(x[3], x[3], MAGIC, None, ALU.subtract)
            for part in (PI_A, PI_B, PI_C):
                link(nc.vector.scalar_tensor_tensor(x[2], x[3], -part, x[2], ALU.mult, ALU.add))
            lim = 3.1415925
            ts(x[4], x[2], lim, -lim, ALU.min, ALU.max)
            ts(x[5], x[4], -1.0, None, ALU.mult)
            tt(x[5], x[5], x[4], ALU.max)
            nc.vector.tensor_scalar(x[5], x[5], -1.0, math.pi / 2, ALU.mult, ALU.add).then_inc(p_ang, 1)
            dve.wait_ge(p_sin, 2)
            dve.wait_ge(p_exp, 2)
            link(nc.vector.memset(PR[:, 0], 1.0))
            link(nc.vector.memset(PI[:, 0], 0.0))
            tt(PR[:, 1], x[1], x[16])
            nc.vector.tensor_tensor(PI[:, 1], x[1], x[17], ALU.mult).then_inc(p_unit, 1)
            dve.wait_ge(p_unit, 1)

            def times(oR, oI, aR, aI, bR, bI, t):
                nc.vector.tensor_tensor(t[0], aR, bR, ALU.mult)
                nc.vector.tensor_tensor(t[1], aI, bI, ALU.mult)
                nc.vector.tensor_tensor(t[2], aR, bI, ALU.mult)
                tt(t[3], aI, bR)
                nc.vector.tensor_tensor(oR, t[0], t[1], ALU.subtract)
                tt(oI, t[2], t[3], ALU.add)

            for m in (1, 2, 4):
                tmp = [BAR[:, k, 0:8 * m].rearrange("p (m g) -> p m g", g=GH) for k in range(4)]
                b = [q[:, m:m + 1].to_broadcast([P, m, GH]) for q in (PR, PI)]
                times(PR[:, m + 1:2 * m + 1], PI[:, m + 1:2 * m + 1], PR[:, 1:m + 1], PI[:, 1:m + 1], *b, tmp)
            for m in range(8):
                nc.vector.tensor_copy(QR[:, m], PR[:, 7 - m])
                link(nc.vector.tensor_copy(QI[:, m], PI[:, 7 - m]))
            tt(x[6], x[1], x[1])
            tt(x[6], x[6], x[6])
            tt(x[6], x[6], x[6])
            ts(x[7], PR[:, 1], 1.0, None, ALU.subtract)
            tt(x[8], lamR[:], lamR[:])
            tt(x[9], lamI[:], lamI[:])
            tt(x[8], x[8], x[9], ALU.add)
            link(nc.vector.reciprocal(x[8], x[8]))
            tt(x[9], x[7], lamR[:])
            tt(x[10], PI[:, 1], lamI[:])
            tt(x[9], x[9], x[10], ALU.add)
            tt(x[9], x[9], x[8])
            tt(x[10], PI[:, 1], lamR[:])
            tt(x[11], x[7], lamI[:])
            tt(x[10], x[10], x[11], ALU.subtract)
            tt(x[10], x[10], x[8])
            cb = [x[k].unsqueeze(2).to_broadcast([P, GH, 16]) for k in (9, 10)]
            tmp = [BAR[:, k].rearrange("p (g h) -> p g h", g=GH) for k in range(4)]
            bp = BpR[:], BpI[:]
            times(bp[0], bp[1], *cb, Bin[:, 0], Bin[:, 1], tmp)
            q = [y[:].rearrange("p j g -> p g j").unsqueeze(3).to_broadcast([P, GH, CH, 16]) for y in (QR, QI)]
            bx = [y.unsqueeze(2).to_broadcast([P, GH, CH, 16]) for y in bp]
            v4 = [y[:].rearrange("p g (j h) -> p g j h", j=CH) for y in (BAR, BAI, S["t1"])]
            tt(v4[0], q[0], bx[0])
            tt(v4[2], q[1], bx[1])
            tt(v4[0], v4[0], v4[2], ALU.subtract)
            tt(v4[1], q[0], bx[1])
            tt(v4[2], q[1], bx[0])
            nc.vector.tensor_tensor(v4[1], v4[1], v4[2], ALU.add).then_inc(bb, 1)
            dve.wait_ge(t_c, 1)
            pw = [y[:].rearrange("p d g -> p g d").unsqueeze(3).to_broadcast([P, GH, 9, 16]) for y in (PR, PI)]
            cx = [CI_[:, j].unsqueeze(2).to_broadcast([P, GH, 9, 16]) for j in range(2)]
            scratch = S["tH"][:, 0:GH * 9 * 16].rearrange("p (g d h) -> p g d h", g=GH, d=9)
            flat = [y[:].rearrange("p g d h -> p (g d h)") for y in (CAR, CAI)]
            tt(CAR[:], pw[0], cx[0])
            tt(scratch, pw[1], cx[1])
            tt(CAR[:], CAR[:], scratch, ALU.subtract)
            tt(CAI[:], pw[0], cx[1])
            tt(scratch, pw[1], cx[0])
            link(nc.vector.scalar_tensor_tensor(flat[1], flat[1], -1.0, S["tH"][:, 0:GH * 9 * 16],
                                                ALU.mult, ALU.subtract))
            dve.sem_inc(bb, 1)
            dve.wait_ge(e_tab, 1)
            dve.wait_ge(l_p, 5)
            for a in range(2):
                gs = slice(4 * a, 4 * a + 4)
                L = [bank[3 + 2 * j + a][:].rearrange("p (g n) -> p g n", g=4) for j in range(2)]
                tt(XR[:, gs], ER[:, gs], L[0])
                tt(BAR[:, gs], EI[:, gs], L[1])
                tt(XR[:, gs], XR[:, gs], BAR[:, gs], ALU.add)
                tt(XI[:, gs], ER[:, gs], L[1])
                tt(BAR[:, gs], EI[:, gs], L[0])
                tt(XI[:, gs], XI[:, gs], BAR[:, gs], ALU.subtract)
            a4 = [y[:, 4].unsqueeze(2).to_broadcast([P, GH, DB]) for y in (PR, PI)]
            t2 = [BAR[:, k, 0:64].rearrange("p (g b) -> p g b", g=GH) for k in range(4)]
            times(FR[:, 0, :, 0:DB], FR[:, 1, :, 0:DB], *a4, H0[:, 0], H0[:, 1], t2)
            LS = bank[7][:, 256:256 + P].rearrange("p (a g b) -> p a g b", a=2, g=GH)
            link(nc.vector.tensor_tensor(FR[:, :, :, 0:DB], FR[:, :, :, 0:DB], LS, ALU.add))
            dve.sem_inc(l_r, 1)
            for gh in range(GH):
                r8 = x[6][:, gh:gh + 1].to_broadcast([P, NC])
                nc.vector.tensor_tensor_scan(BAR[:, gh], r8, XR[:, gh], 0.0, ALU.mult, ALU.add)
                link(nc.vector.tensor_tensor_scan(BAI[:, gh], r8, XI[:, gh], 0.0, ALU.mult, ALU.add))
            link(nc.vector.memset(HR[:, :, 0:1], 0.0))
            link(nc.vector.memset(HI[:, :, 0:1], 0.0))
            tt(HR[:, :, 1:NC + 1], ER[:], BAR[:])
            tt(XR[:], EI[:], BAI[:])
            tt(HR[:, :, 1:NC + 1], HR[:, :, 1:NC + 1], XR[:], ALU.subtract)
            tt(HI[:, :, 1:NC + 1], ER[:], BAI[:])
            tt(XR[:], EI[:], BAR[:])
            tt(HI[:, :, 1:NC + 1], HI[:, :, 1:NC + 1], XR[:], ALU.add)
            nc.vector.tensor_copy(FR[:, 0, :, DB:DB + 1], HR[:, :, NC:NC + 1])
            nc.vector.tensor_copy(FR[:, 1, :, DB:DB + 1], HI[:, :, NC:NC + 1]).then_inc(h_ok, 1)
            dve.wait_ge(ud, 2)
            for q_ in range(4):
                l, a = q_ // 2, q_ % 2
                dve.wait_ge(y_p, q_ + 1)
                out = ysb[:, 0:NT].rearrange("p j (g l h) -> p l g j h", g=GH, l=2)[:, l, 4 * a:4 * a + 4]
                u_ = (ta, tb)[a][:].rearrange("p (g l) (j h) -> p l g j h", l=2, h=16)[:, l]
                nc.vector.tensor_tensor(out, bank[(0, 1, 2, 7)[q_]][:].rearrange("p (g j h) -> p g j h", g=4, j=CH),
                                        u_, ALU.add).then_inc(y_ok, 1)
            tt(glS[:], US[:], Dbc[0:TS])
            dve.wait_ge(ys_d, 16 * DT)
            nc.vector.tensor_tensor(ysb[0:TS, NT], ysb[0:TS, NT], glS[:], ALU.add).then_inc(y_ok, 1)
            for j in range(TILES):
                n = rows(j)
                dve.wait_ge(gl_p, j + 1)
                nc.vector.tensor_tensor(gate(j)[:n], bank[2 + j % 2][:n, 0:SW], bglu[:n], ALU.add)\
                    .then_inc(gl_s, 1)
            for j in range(TILES):
                n = rows(j)
                dve.wait_ge(sg, j + 1)
                nc.vector.tensor_tensor(ysb[:n, j], ysb[:n, j], gate(j)[:n], ALU.mult).then_inc(so, 1)
            dve.wait_ge(so_q, TILES)
            for n, js in ((P, slice(0, NT)), (TS, slice(NT, TILES))):
                nc.vector.tensor_scalar(nrm[:n, 1, js], nrm[:n, 0, js], 1.0 / SW, EPS, ALU.mult, ALU.add)\
                    .then_inc(so_m, 1)
            dve.wait_ge(so_r, 1)
            for n, js in ((P, slice(0, NT)), (TS, slice(NT, TILES))):
                link(nc.vector.reciprocal(nrm[:n, 1, js], nrm[:n, 2, js]))
            for j in range(TILES):
                n = rows(j)
                nc.vector.scalar_tensor_tensor(ysb[:n, j], ysb[:n, j], nrm[:n, 1, j:j + 1], gain_bc[:n, AW:D],
                                               ALU.mult, ALU.mult).then_inc(so_n, 1)

        @blk.tensor
        def _(pe):
            pe.wait_ge(ld, 16 * (n_ld - 1))
            for gh in range(GH):
                for j in range(2):
                    nc.tensor.transpose(bank[j][:, 16 * gh:16 * gh + 16],
                                        Cin[:, j, 2 * gh:2 * gh + 2].rearrange("h l p -> h (l p)"), ident[:16, :16])
                    ins = nc.tensor.transpose(bank[2][:, 64 * j + 8 * gh:64 * j + 8 * gh + 8],
                                              Sin[:, j, P * gh:P * gh + P], ident[:DB, :DB])
            ins.then_inc(t_in, 1)
            for q in range(4):
                for g in range(4):
                    ins = nc.tensor.transpose(bank[3 + q][:, P * g:P * g + P],
                                              U[:, 4 * q + g].rearrange("c j h -> c (j h)"), ident[:])
                ins.then_inc(u_p, 1)
            pe.wait_ge(ld_us, 16 * DT)
            for g in range(16):
                ins = nc.tensor.transpose(bank[7][:, 8 * g:8 * g + 8], USp[:, g].rearrange("b j h -> b (j h)"),
                                          ident[:DB, :DB])
            ins.then_inc(us_p, 1)
            pe.wait_ge(bb, 1)
            for q in range(4):
                pe.wait_ge(u_t, q + 1)
                for g in range(4):
                    ins = nc.tensor.transpose(bank[3 + q][:, P * g:P * g + P],
                                              (BAR, BAI)[q // 2][:, 4 * (q % 2) + g], ident[:])
                ins.then_inc(t_b, 1)
            pe.wait_ge(t_c, 1)
            pe.wait_ge(bb, 2)
            pe.wait_ge(u_t, 5)
            for q in range(4):
                l, ps = q // 2, slice(64 * (q // 2), 64 * (q // 2) + 64)
                for g in range(4):
                    gh = 4 * (q % 2) + g
                    for j, (bp, ca) in enumerate(((BpR, CAR), (BpI, CAI))):
                        ins = nc.tensor.matmul(bank[(0, 1, 2, 7)[q]][0:16, P * g:P * g + P], bp[ps, gh],
                                               ca[ps, gh, 0:CH].rearrange("p d h -> p (d h)"),
                                               start=j == 0, stop=j == 1)
                ins.then_inc(tz_p, 1)
            for q in range(4):
                pe.wait_ge(wb, q + 1)
            for q in range(4):
                W = (WBR, WBI)[q // 2]
                for g in range(4):
                    gh = 4 * (q % 2) + g
                    for l in range(2):
                        ins = nc.tensor.matmul(bank[3 + q][64 * l:64 * l + 64, P * g:P * g + P],
                                               W[:, gh, 64 * l:64 * l + 64], UT[:, 2 * gh + l],
                                               start=True, stop=True)
                ins.then_inc(l_p, 1)
            pe.wait_ge(tz, 4)
            for j, W in enumerate((WBR, WBI)):
                for gh in range(GH):
                    for l in range(2):
                        ins = nc.tensor.matmul(bank[7][64 * l:64 * l + 64, 256 + 64 * j + 8 * gh:264 + 64 * j + 8 * gh],
                                               W[:, gh, 64 * l:64 * l + 64], UTs[:, 2 * gh + l],
                                               start=True, stop=True)
            ins.then_inc(l_p, 1)
            pe.wait_ge(l_r, 1)
            pe.wait_ge(h_ok, 1)
            for q in range(4):
                for g in range(4):
                    ins = nc.tensor.transpose(bank[3 + q][0:9, P * g:P * g + P], FR[:, q // 2, 4 * (q % 2) + g],
                                              ident[:])
                ins.then_inc(f_p, 1)
            pe.wait_ge(tz_st, 16 * CH)
            for q in range(4):
                l, ps = q // 2, slice(64 * (q // 2), 64 * (q // 2) + 64)
                for g in range(4):
                    gh = 4 * (q % 2) + g
                    out = bank[(0, 1, 2, 7)[q]][:, P * g:P * g + P]
                    nc.tensor.matmul(out, UT[:, 2 * gh + l], TZ[:, 2 * gh + l], start=True, stop=False)
                    nc.tensor.matmul(out, HR[ps, gh, 0:NC], CAR[ps, gh, 1:9].rearrange("p d h -> p (d h)"),
                                     start=False, stop=False)
                    ins = nc.tensor.matmul(out, HI[ps, gh, 0:NC], CAI[ps, gh, 1:9].rearrange("p d h -> p (d h)"),
                                           start=False, stop=True)
                ins.then_inc(y_p, 1)
            pe.wait_ge(f_s, 4)
            for l in range(2):
                ps = slice(64 * l, 64 * l + 64)
                for gh in range(GH):
                    out = bank[5 + l][0:DB, 64 * gh:64 * gh + 64]
                    nc.tensor.matmul(out, UTs[:, 2 * gh + l], TZ[:, 2 * gh + l, 64:P], start=True, stop=False)
                    for j, ca in enumerate((CAR, CAI)):
                        ins = nc.tensor.matmul(out, H0[ps, j, gh], ca[ps, gh, 1:5].rearrange("p d h -> p (d h)"),
                                               start=False, stop=j == 1)
                ins.then_inc(y_p, 1)
            pe.wait_ge(z_ok, 1)

            def gate_product(j):
                n = rows(j)
                pe.wait_ge(zt_c, j + 1)
                if j >= 2:
                    pe.wait_ge(gl_s, j - 1)
                for k in range(2):
                    ins = nc.tensor.matmul(bank[2 + j % 2][:n, 0:SW], zT[:, j % 2, k, :n], wglu[:, k],
                                           start=k == 0, stop=k == 1)
                ins.then_inc(gl_p, 1)

            for j in range(TILES):
                n = rows(j)
                if j >= 2:
                    pe.wait_ge(zt_c, j - 1)
                for k in range(2):
                    ins = nc.tensor.transpose(bank[j % 2][:, P * k:P * k + n], ysb[:n, j, P * k:P * k + P],
                                              ident[:n, :n])
                ins.then_inc(zt_p, 1)
                if j:
                    gate_product(j - 1)
            gate_product(NT)


def block_sample(nc, I, O, S):
    ident, gain_bc, qkS, vS, attS, smask = (S[x] for x in ("ident", "gain_bc", "qkS", "vS", "attS", "smask"))
    bank = S["bank"]
    NTL = [1, 4, 2]
    TOK = [4, 1, 2]
    NKS = P + TS
    RING = 3
    loads = [(kv, g, b) for kv in range(2) for g in range(G) for b in range(DB)]
    units = [(g, b, i) for g in range(G) for b in range(DB) for i in range(NTL[g])]
    g_end = [8, 40, 56]

    with ExitStack() as c:
        def sb(name, shape, dt=F32):
            return c.enter_context(nc.sbuf_tensor(name, shape, dt))

        def sem(name):
            return nc.alloc_semaphore("s3_" + name)

        ring = sb("ring", [P, RING, 4, GW])
        kTc = sb("kTc", [P, 4, 2, P])
        Qbd = sb("Qbd", [P, G, 2, 2, TS])
        sT = sb("sT", [P, G, 2, P])
        Pm = sb("Pm", [P, G, NKS])
        sc = sb("sc", [P, 8, G])
        PTc = sb("PTc", [P, G, P])
        PTn = sb("PTn", [TS, G, P])
        oS = sb("oS", [P, 2 * G, TS])
        nrm = sb("nrm_s", [TS, 4])
        junk = sb("junk_s", [TS, AW])

        r_ld = [sem(f"r_ld{i}") for i in range(RING)]
        m_ld = sem("m_ld")
        q_zero, q_bd = sem("q_zero"), sem("q_bd")
        k_p = sem("k_p")
        k_a, k_d = sem("k_a"), sem("k_d")
        s_p = sem("s_p")
        s_n = sem("s_n")
        s_c, s_b = sem("s_c"), sem("s_b")
        mx, ex, ln, al, ae, pr = (sem(x) for x in ("mx", "ex", "ln", "al", "ae", "pr"))
        pt_p, pt_c = sem("pt_p"), sem("pt_c")
        v_p = sem("v_p")
        o_c, o_p, o_s = sem("o_c"), sem("o_p"), sem("o_s")
        n_q, n_m, n_r = sem("n_q"), sem("n_m"), sem("n_r")
        c_dve = sem("c_dve")

        def ring_waits(eng, j):
            n = sum(2 if loads[x][1] == 2 else 1 for x in range(j % RING, j + 1, RING))
            eng.wait_ge(r_ld[j % RING], 16 * n)

        def load_of(kv, g, b):
            return (kv * G + g) * DB + b

        units_to = [sum(NTL[g] for _, g, _b in loads[:j]) for j in range(len(loads) + 1)]
        blk = c.enter_context(nc.Block())

        @blk.sync
        def _(sp):
            sp.dma_start(smask[:], I["c_smask"]).then_inc(m_ld, 16)
            for j, (kv, g, b) in enumerate(loads):
                if j >= RING:
                    k = units_to[j - RING + 1]
                    sp.wait_ge(k_p if k <= 56 else v_p, k if k <= 56 else k - 56)
                cache = I[f"cache_kv_dil{(1, 4, 16)[g]}"][0, b]
                if g == 0:
                    sp.dma_start(ring[:, j % RING, 0], cache[:, kv].rearrange("s h e -> s (h e)"))\
                        .then_inc(r_ld[j % RING], 16)
                elif g == 1:
                    sp.dma_start(ring[:, j % RING], cache.rearrange("(s r) v h e -> s r v (h e)", r=4)[:, :, kv])\
                        .then_inc(r_ld[j % RING], 16)
                else:
                    for r in range(2):
                        sp.dma_start(ring[64 * r:64 * r + 64, j % RING, 0:2],
                                     cache.rearrange("(s r) v h e -> s r v (h e)", r=16)[:, r:4:2, kv])\
                            .then_inc(r_ld[j % RING], 16)

        @blk.scalar
        def _(act):
            def take_keys(u):
                act.wait_ge(k_p, u + 1)
                if u >= 4:
                    act.wait_ge(s_p, u - 3)
                nc.scalar.activation(kTc[:, u % 4], bank[3 + u % 2][:, 0:2 * P].rearrange("p (k n) -> p k n", k=2),
                                     ACT.Copy).then_inc(k_a, 1)

            for u in range(0, 56, 2):
                take_keys(u)
            for g in range(G):
                act.wait_ge(s_p, g_end[g])
                act.wait_ge(s_n, g + 1)
                nc.scalar.activation(sT[:, g, 0], bank[g][:, 0:P], ACT.Copy)
                nc.scalar.activation(sT[0:TS, g, 1], bank[g][0:TS, P:2 * P], ACT.Copy).then_inc(s_c, 1)
            act.wait_ge(mx, 1)
            for g in range(G):
                ins = nc.scalar.activation(Pm[:, g], Pm[:, g], ACT.Exp, bias=sc[:, 0, g:g + 1],
                                           accum_out=sc[:, 1, g:g + 1])
            ins.then_inc(ex, 1)
            act.wait_ge(ex, 1)
            nc.scalar.activation(sc[:, 2], sc[:, 1], ACT.Ln).then_inc(ln, 1)
            act.wait_ge(al, 1)
            nc.scalar.activation(sc[:, 4], sc[:, 3], ACT.Exp, accum_out=sc[:, 5, 0:1]).then_inc(ae, 1)
            act.wait_ge(pt_p, 1)
            nc.scalar.activation(PTc[:], bank[6][:, 0:3 * P].rearrange("p (g n) -> p g n", g=G), ACT.Copy)
            nc.scalar.activation(PTn[:], bank[7][0:TS, 0:3 * P].rearrange("p (g n) -> p g n", g=G), ACT.Copy)\
                .then_inc(pt_c, 1)
            for g in range(G):
                act.wait_ge(v_p, g_end[g])
                for hp in range(2):
                    for hh in range(2):
                        ps = slice(64 * hh, 64 * hh + 64)
                        ins = nc.scalar.activation(oS[ps, 2 * g + hp], bank[2 * g + hp][ps, TS * hh:TS * hh + TS],
                                                   ACT.Copy)
                ins.then_inc(o_c, 1)
            act.wait_ge(o_p, 1)
            nc.scalar.activation(attS[:, 0:512], bank[6][0:TS, :], ACT.Copy)
            nc.scalar.activation(attS[:, 512:AW], bank[7][0:TS, 0:256], ACT.Copy).then_inc(o_s, 1)
            act.wait_ge(o_s, 1)
            nc.scalar.activation(junk[:], attS[:], ACT.Square, accum_out=nrm[:, 0:1]).then_inc(n_q, 1)
            act.wait_ge(n_m, 1)
            nc.scalar.activation(nrm[:, 2:3], nrm[:, 1:2], ACT.Sqrt).then_inc(n_r, 1)

        @blk.vector
        def _(dve):
            link = linker(dve, c_dve)
            nc.vector.memset(Qbd[:], 0.0).then_inc(q_zero, 1)
            dve.wait_ge(q_zero, 1)
            for hh in range(2):
                ps = slice(64 * hh, 64 * hh + 64)
                nc.vector.tensor_copy(Qbd[ps, :, :, hh], qkS[ps, :, 0]).then_inc(q_bd, 1)
            for u in range(1, 56, 2):
                dve.wait_ge(k_p, u + 1)
                if u >= 4:
                    dve.wait_ge(s_p, u - 3)
                nc.vector.tensor_copy(kTc[:, u % 4], bank[3 + u % 2][:, 0:2 * P].rearrange("p (k n) -> p k n", k=2))\
                    .then_inc(k_d, 1)
            dve.wait_ge(s_b, 1)
            dve.wait_ge(m_ld, 16)
            link(nc.vector.tensor_tensor(Pm[:], bank[5][:, 0:G * NKS].rearrange("p (g n) -> p g n", g=G), smask[:],
                                         ALU.add))
            nc.vector.tensor_reduce(sc[:, 0], Pm[:], AX.X, ALU.max, negate=True).then_inc(mx, 1)
            dve.wait_ge(ln, 1)
            link(nc.vector.tensor_tensor(sc[:, 2], sc[:, 2], sc[:, 0], ALU.subtract))
            link(nc.vector.tensor_reduce(sc[:, 6, 0:1], sc[:, 2], AX.X, ALU.max))
            nc.vector.tensor_scalar(sc[:, 3], sc[:, 2], sc[:, 6, 0:1], None, ALU.subtract).then_inc(al, 1)
            dve.wait_ge(ae, 1)
            link(nc.vector.tensor_scalar(sc[:, 6], sc[:, 1], sc[:, 5, 0:1], None, ALU.mult))
            link(nc.vector.reciprocal(sc[:, 7], sc[:, 6]))
            link(nc.vector.tensor_tensor(sc[:, 7], sc[:, 7], sc[:, 4], ALU.mult))
            nc.vector.tensor_tensor(Pm[:], Pm[:], sc[:, 7].unsqueeze(2).to_broadcast([P, G, NKS]), ALU.mult)\
                .then_inc(pr, 1)
            dve.wait_ge(n_q, 1)
            nc.vector.tensor_scalar(nrm[:, 1:2], nrm[:, 0:1], 1.0 / AW, EPS, ALU.mult, ALU.add).then_inc(n_m, 1)
            dve.wait_ge(n_r, 1)
            link(nc.vector.reciprocal(nrm[:, 3:4], nrm[:, 2:3]))
            link(nc.vector.scalar_tensor_tensor(attS[:], attS[:], nrm[:, 3:4], gain_bc[0:TS, 0:AW],
                                                ALU.mult, ALU.mult))

        @blk.tensor
        def _(pe):
            def tokens(g, b, i):
                return slice(DT * b + TOK[g] * i, DT * b + TOK[g] * (i + 1))

            def transpose_keys(u):
                g, b, i = units[u]
                j = load_of(0, g, b)
                if i == 0:
                    ring_waits(pe, j)
                if u >= 2:
                    pe.wait_ge(k_d if u % 2 else k_a, u // 2)
                for k in range(2):
                    ins = nc.tensor.transpose(bank[3 + u % 2][:, P * k:P * k + P],
                                              ring[:, j % RING, i, P * k:P * k + P], ident[:])
                ins.then_inc(k_p, 1)

            def scores(u):
                g, b, i = units[u]
                pe.wait_ge(k_d if u % 2 else k_a, u // 2 + 1)
                for hp in range(2):
                    out = bank[g][:, 64 * hp:64 * hp + 64].rearrange("p (h n) -> p h n", h=2)[:, :, tokens(g, b, i)]
                    ins = nc.tensor.matmul(out, kTc[:, u % 4, hp], Qbd[:, g, hp, :, tokens(g, b, i)],
                                           start=True, stop=True)
                ins.then_inc(s_p, 1)

            pe.wait_ge(q_bd, 2)
            for g in range(G):
                for hp in range(2):
                    ins = nc.tensor.matmul(bank[g][0:TS, P + 64 * hp:P + 64 * hp + 64], qkS[:, g, 1, hp],
                                           Qbd[:, g, hp].rearrange("p h n -> p (h n)"), start=True, stop=True)
                ins.then_inc(s_n, 1)
            for u in range(57):
                if u < 56:
                    transpose_keys(u)
                if u:
                    scores(u - 1)
            for g in range(G):
                pe.wait_ge(s_c, g + 1)
                nc.tensor.transpose(bank[5][:, NKS * g:NKS * g + P], sT[:, g, 0], ident[:])
                ins = nc.tensor.transpose(bank[5][:, NKS * g + P:NKS * g + NKS], sT[0:TS, g, 1], ident[:TS, :TS])
            ins.then_inc(s_b, 1)
            pe.wait_ge(pr, 1)
            for g in range(G):
                nc.tensor.transpose(bank[6][:, P * g:P * g + P], Pm[:, g, 0:P], ident[:])
                ins = nc.tensor.transpose(bank[7][0:TS, P * g:P * g + P], Pm[:, g, P:NKS], ident[:])
            ins.then_inc(pt_p, 1)
            pe.wait_ge(pt_c, 1)
            for g in range(G):
                for hp in range(2):
                    nc.tensor.matmul(bank[2 * g + hp][:, 0:64], vS[:, g, P * hp:P * hp + P],
                                     PTn[:, g, 64 * hp:64 * hp + 64], start=True, stop=False)
                for b in range(DB):
                    j = load_of(1, g, b)
                    ring_waits(pe, j)
                    for i in range(NTL[g]):
                        for hp in range(2):
                            out = bank[2 * g + hp][:, 0:64].rearrange("p (h n) -> p h n", h=2)
                            w = PTc[:, g, 64 * hp:64 * hp + 64].rearrange("p (h n) -> p h n", h=2)
                            ins = nc.tensor.matmul(out[:, :, tokens(g, b, i)], ring[:, j % RING, i, P * hp:P * hp + P],
                                                   w[:, :, tokens(g, b, i)], start=False,
                                                   stop=b == DB - 1 and i == NTL[g] - 1)
                        ins.then_inc(v_p, 1)
            pe.wait_ge(o_c, 3)
            for k in range(2 * G):
                ins = nc.tensor.transpose(bank[6 + k // 4][0:TS, P * (k % 4):P * (k % 4) + P], oS[:, k], ident[:])
            ins.then_inc(o_p, 1)


def block_mix(nc, I, O, S):
    ident, gain_bc, att, attS, ysb = (S[x] for x in ("ident", "gain_bc", "att", "attS", "ysb"))
    XH, XL, negm, lsum = S["XH"], S["XL"], S["negm"], S["lsum"]
    bank, stat = S["bank"], S["stat"]
    A = G * NT
    with ExitStack() as c:
        def sb(name, shape, dt=F32):
            return c.enter_context(nc.sbuf_tensor(name, shape, dt))

        def sem(name):
            return nc.alloc_semaphore("s4_" + name)

        sq = sb("sq", [P, NT, GW])
        st = sb("st", [P, A, 2, H])
        al = sb("al", [P, A, G, 2, H])
        w1 = sb("w1", [P, A, G, H])
        w2 = sb("w2", [P, A, H])
        w3 = sb("w3", [P, A])
        s_sq, s_rd = sem("sq"), sem("rd")
        ln, st_ok, st_w, st_r = sem("ln"), sem("st_ok"), sem("st_w"), sem("st_r")
        sub, ex, ms, rt = sem("sub"), sem("ex"), sem("ms"), sem("rt")
        a_n, t_p, t_h, t_l = sem("a_n"), sem("t_p"), sem("t_h"), sem("t_l")
        c_dve = sem("c_dve")
        blk = c.enter_context(nc.Block())
        work = [("y", t) for t in range(TILES)] + [("s", g) for g in range(G)] + [("a", a) for a in range(A)]

        def place(X, w):
            kind, i = w
            if kind == "y":
                return columns(X[:, 6:8], 3, i), rows(i)
            if kind == "s":
                return X[:, 2 * i:2 * i + 2, SEQ:T], TS
            g, t = i // NT, i % NT
            return columns(X[:, 2 * g:2 * g + 2], g, t), P

        def by_token(g):
            if g == 0:
                return stat.rearrange("(t p) v -> p t v", p=P)
            if g == 1:
                return None
            return stat.rearrange("(p t) v -> p t v", t=NT)

        def stat_dmas(eng, g, tile, g2, to_dram, sem_):
            n = 0
            vs = slice(8 * g2, 8 * g2 + 8) if g2 is not None else slice(0, 24)
            parts = [(by_token(g)[:, :, vs], slice(g * NT, g * NT + NT))] if g != 1 else \
                [(stat.rearrange("(h p r) v -> p h r v", h=2, r=4)[:, h, :, vs], slice(NT + h, 2 * NT, 2))
                 for h in range(2)]
            for dram, ts in parts:
                x = tile[:, ts]
                eng.dma_start(*((dram, x) if to_dram else (x, dram))).then_inc(sem_, 16)
                n += 1
            return n

        @blk.sync
        def _(sp):
            sp.wait_ge(st_ok, 1)
            n = 0
            for g in range(G):
                n += stat_dmas(sp, g, st[:].rearrange("p a x h -> p a (x h)"), g, True, st_w)
            sp.wait_ge(st_w, 16 * n)
            for g in range(G):
                stat_dmas(sp, g, al[:].rearrange("p a g x h -> p a (g x h)"), None, False, st_r)

        @blk.gpsimd
        def _(pool):
            for g in range(G):
                if g:
                    pool.wait_ge(s_rd, g)
                x = att[:, g * NT:g * NT + NT]
                nc.gpsimd.tensor_tensor(sq[:], x, x, ALU.mult).then_inc(s_sq, 1)

        @blk.scalar
        def _(act):
            nc.scalar.activation(st[:, :, 0], lsum[:], ACT.Ln).then_inc(ln, 1)
            act.wait_ge(sub, 1)
            nc.scalar.activation(w1[:], w1[:], ACT.Exp).then_inc(ex, 1)

            def take(k):
                act.wait_ge(t_p, k + 1)
                dst, n = place(XH, work[k])
                src = bank[k % 4][:, 0:2 * P].rearrange("p (k n) -> p k n", k=2)[:, :, :n]
                nc.scalar.activation(dst, src, ACT.Copy).then_inc(t_h, 1)

            for k in range(len(work)):
                if k == TILES + G:
                    act.wait_ge(ms, 1)
                    nc.scalar.activation(w3[:], w3[:], ACT.Sqrt).then_inc(rt, 1)
                take(k)

        @blk.vector
        def _(dve):
            link = linker(dve, c_dve)
            dve.wait_ge(ln, 1)
            for g in range(G):
                dve.wait_ge(s_sq, g + 1)
                nc.vector.tensor_reduce(st[:, g * NT:g * NT + NT, 1], sq[:].rearrange("p t (h e) -> p t h e", h=H),
                                        AX.X, ALU.add).then_inc(s_rd, 1)
            nc.vector.tensor_tensor(st[:, :, 0], st[:, :, 0], negm[:], ALU.subtract).then_inc(st_ok, 1)

            def take(k):
                dve.wait_ge(t_h, k + 1)
                dst, n = place(XL, work[k])
                hi, _ = place(XH, work[k])
                src = bank[k % 4][:, 0:2 * P].rearrange("p (k n) -> p k n", k=2)[:, :, :n]
                nc.vector.tensor_tensor(dst, src, hi.bitcast(F32), ALU.subtract).then_inc(t_l, 1)

            dve.wait_ge(st_r, 16 * 4)
            lse = [al[:, :, g, 0] for g in range(G)]
            link(nc.vector.tensor_tensor(w2[:], lse[0], lse[1], ALU.max))
            link(nc.vector.tensor_tensor(w2[:], w2[:], lse[2], ALU.max))
            for g in range(G):
                ins = nc.vector.tensor_tensor(w1[:, :, g], lse[g], w2[:], ALU.subtract)
            ins.then_inc(sub, 1)
            dve.wait_ge(ex, 1)
            link(nc.vector.tensor_tensor(w2[:], w1[:, :, 0], w1[:, :, 1], ALU.add))
            link(nc.vector.tensor_tensor(w2[:], w2[:], w1[:, :, 2], ALU.add))
            link(nc.vector.reciprocal(w2[:], w2[:]))
            for g in range(G):
                link(nc.vector.tensor_tensor(w1[:, :, g], w1[:, :, g], w2[:], ALU.mult))
            for g in range(G):
                link(nc.vector.tensor_tensor(al[:, :, g, 0], w1[:, :, g], w1[:, :, g], ALU.mult))
                link(nc.vector.tensor_tensor(al[:, :, g, 1], al[:, :, g, 1], al[:, :, g, 0], ALU.mult))
            link(nc.vector.tensor_tensor(w2[:], al[:, :, 0, 1], al[:, :, 1, 1], ALU.add))
            link(nc.vector.tensor_tensor(w2[:], w2[:], al[:, :, 2, 1], ALU.add))
            link(nc.vector.tensor_reduce(w3[:], w2[:], AX.X, ALU.add))
            nc.vector.tensor_scalar(w3[:], w3[:], 1.0 / AW, EPS, ALU.mult, ALU.add).then_inc(ms, 1)
            for k in range(TILES + G):
                take(k)
            dve.wait_ge(rt, 1)
            link(nc.vector.reciprocal(w3[:], w3[:]))
            for g in range(G):
                ts = slice(g * NT, g * NT + NT)
                link(nc.vector.tensor_tensor(w2[:, ts], w1[:, ts, g], w3[:, ts].unsqueeze(2).to_broadcast([P, NT, H]),
                                             ALU.mult))

            def scale(a):
                g = a // NT
                x = att[:, a].rearrange("p (h e) -> p h e", h=H)
                link(nc.vector.tensor_tensor(x, x, per_head(w2[:, a], P), ALU.mult))
                nc.vector.tensor_tensor(att[:, a], att[:, a], gain_bc[:, GW * g:GW * g + GW], ALU.mult)\
                    .then_inc(a_n, 1)

            for a in range(A + 1):
                if a < A:
                    scale(a)
                if a:
                    take(TILES + G + a - 1)

        @blk.tensor
        def _(pe):
            for k, (kind, i) in enumerate(work):
                if k >= 4:
                    pe.wait_ge(t_l, k - 3)
                if kind == "a":
                    pe.wait_ge(a_n, i + 1)
                n = place(XH, work[k])[1]
                src = {"y": lambda: ysb[:n, i], "s": lambda: attS[:, GW * i:GW * i + GW], "a": lambda: att[:, i]}[kind]()
                for x in range(2):
                    ins = nc.tensor.transpose(bank[k % 4][:, P * x:P * x + n], src[:, P * x:P * x + P],
                                              ident[:n, :n])
                ins.then_inc(t_p, 1)


def block_dense(nc, I, O, S, stages):
    XH, XL, WH, WL, wstage = S["XH"], S["XL"], S["WH"], S["WL"], S["wstage"]
    ident, gain_bc, hres = S["ident"], S["gain_bc"], S["hres"]
    bank = S["bank"]
    MM, TR, KT_ = bank[0:3], bank[3:5], bank[5:7]
    weights = {"m": "w_xkv", "o": "w_out", "q": "w_xq", "x": "w_xo"}
    NM = 2
    blocks = [(st, j) for st in stages for j in range(8 if st == "m" else 4)]
    steps = [(st, j, t, b) for b, (st, j) in enumerate(blocks) for t in range(NM if st == "m" else TILES)]
    has_m = "m" in stages
    normed = [s for s, (st, j, t, b) in enumerate(steps) if st == "q" or st == "m" and j < 4]
    norm_at = {s: n for n, s in enumerate(normed)}
    block_end = [max(s for s, x in enumerate(steps) if x[3] == b) + 1 for b in range(len(blocks))]
    by_dve = [sum(steps[r][0] != "m" or steps[r][1] < 4 for r in range(s)) for s in range(len(steps) + 1)]
    by_act = [s - by_dve[s] for s in range(len(steps) + 1)]
    preps = ([("m", i) for i in range(NM)] if has_m else []) + [("h", i) for i in range(TILES)]
    h0 = len(preps) - TILES

    def rows_of(kind, i):
        return P if kind == "m" else rows(i)

    with ExitStack() as c:
        def sb(name, shape, dt=F32):
            return c.enter_context(nc.sbuf_tensor(name + stages, shape, dt))

        def sem(name):
            return nc.alloc_semaphore(f"d{stages}_" + name)

        xn = sb("xn", [P, 2, D])
        kn = sb("kn", [P, 2, WB])
        ssq = sb("ssq", [P, 3, len(preps)])
        zr = sb("zr", [P, 3, max(1, len(normed))])

        ld = sem("ld")
        x_ld = sem("x_ld")
        w_ld, w_hi, w_lo = sem("w_ld"), sem("w_hi"), sem("w_lo")
        p_sq, p_ms, p_rt, p_n = sem("p_sq"), sem("p_ms"), sem("p_rt"), sem("p_n")
        p_tr, p_hi, p_lo = sem("p_tr"), sem("p_hi"), sem("p_lo")
        mm = sem("mm")
        ev_a, ev_d = sem("ev_a"), sem("ev_d")
        n_q, n_m, n_r, n_t, n_T = sem("n_q"), sem("n_m"), sem("n_r"), sem("n_t"), sem("n_T")
        k_st, v_st = [sem("k_st0"), sem("k_st1")], sem("v_st")
        c_dve = sem("c_dve")
        n_x = 2 if "o" in stages else 0
        n_ld = 16 * len(S["loads" + stages])

        def after_step(s):
            st, j, t, b = steps[s]
            return [t] if st in "ox" and j == 3 else []

        blk = c.enter_context(nc.Block())

        @blk.sync
        def _(sp):
            for dst, src in S["loads" + stages]:
                sp.dma_start(dst, src).then_inc(ld, 16)
            for b, (st, j) in enumerate(blocks):
                if b:
                    sp.wait_ge(w_lo, b)
                sp.dma_start(wstage[:], I[weights[st]][0, :, WB * j:WB * j + WB]
                             .rearrange("(k p) n -> p k n", p=P)).then_inc(w_ld, 16)
                if b == 0 and n_x:
                    sp.dma_start(hres[:, 0:NT], I["x_prompt"][0].rearrange("(t p) d -> p t d", p=P)).then_inc(x_ld, 16)
                    sp.dma_start(hres[0:TS, NT], I["x_sample"].rearrange("b t d -> (b t) d")).then_inc(x_ld, 16)

        @blk.gpsimd
        def _(pool):
            if has_m:
                kv = O["mem_kv_p"][0, 0]
                ks, vs = [0, 0], 0
                for s, (st, j, t, b) in enumerate(steps):
                    if st != "m":
                        break
                    dst = kv[P * t:P * t + P, j // 4, j % 4]
                    if j < 4:
                        n = norm_at[s]
                        pool.wait_ge(ev_d, n + 1)
                        pool.dma_start(dst, kn[:, n % 2]).then_inc(k_st[n % 2], 16)
                        ks[n % 2] += 16
                    else:
                        vs += 1
                        pool.wait_ge(ev_a, vs)
                        pool.dma_start(dst, S["Vm"][:, t, WB * (j - 4):WB * (j - 3)]).then_inc(v_st, 16)
                pool.wait_ge(k_st[0], ks[0])
                pool.wait_ge(k_st[1], ks[1])
                pool.wait_ge(v_st, 16 * vs)

        def source(kind, i):
            return S["mraw"][:, i] if kind == "m" else hres[:rows(i), i]

        def parts(kind, i, hi):
            if kind == "m":
                return (S["MH"] if hi else S["ML"])[:, :, P * i:P * i + P]
            return (XH if hi else XL)[:, :, P * i:P * i + rows(i)]

        @blk.scalar
        def _(act):
            def split_weights(b):
                act.wait_ge(w_ld, 16 * (b + 1))
                if b >= 2:
                    act.wait_ge(mm, block_end[b - 2])
                nc.scalar.activation(WH[:, b % 2], wstage[:], ACT.Copy).then_inc(w_hi, 1)

            def prep_square(p):
                kind, i = preps[p]
                n = rows_of(kind, i)
                if p >= 2:
                    act.wait_ge(p_tr, 2 * (p - 1))
                nc.scalar.activation(xn[:n, p % 2], source(kind, i), ACT.Square, accum_out=ssq[:n, 0, p:p + 1])\
                    .then_inc(p_sq, 1)
                act.wait_ge(p_ms, p + 1)
                nc.scalar.activation(ssq[:n, 2, p:p + 1], ssq[:n, 1, p:p + 1], ACT.Sqrt).then_inc(p_rt, 1)

            def prep_high(p):
                kind, i = preps[p]
                n = rows_of(kind, i)
                for half in range(2):
                    act.wait_ge(p_tr, 2 * p + half + 1)
                    nc.scalar.activation(parts(kind, i, True)[:, 4 * half:4 * half + 4],
                                         TR[half][:].rearrange("p (k n) -> p k n", k=4)[:, :, :n],
                                         ACT.Copy).then_inc(p_hi, 1)

            def take_transposed(n):
                st, j, t, b = steps[normed[n]]
                act.wait_ge(n_t, n + 1)
                src = KT_[n % 2][:, 0:2 * P].rearrange("p (k n) -> p k n", k=2)
                if st == "m":
                    dst = S["kmT"][:, 2 * j:2 * j + 2, P * t:P * t + P]
                else:
                    src = src[:, :, :rows(t)]
                    dst = S["qxT"][:, 2 * j:2 * j + 2, P * t:P * t + rows(t)]
                nc.scalar.activation(dst, src, ACT.Copy).then_inc(n_T, 1)

            act.wait_ge(ld, n_ld)
            split_weights(0)
            if has_m:
                for p in range(NM):
                    prep_square(p)
                    prep_high(p)
            split_weights(1)
            pending = []
            for s, (st, j, t, b) in enumerate(steps):
                n_rows = P if st == "m" else rows(t)
                if st == "m" and j >= 4:
                    act.wait_ge(mm, s + 1)
                    nc.scalar.activation(S["Vm"][:, t, WB * (j - 4):WB * (j - 3)], MM[s % 3][:, 0:WB], ACT.Copy)\
                        .then_inc(ev_a, 1)
                elif s in norm_at:
                    n = norm_at[s]
                    act.wait_ge(mm, s + 1)
                    if n >= 2:
                        act.wait_ge(n_t, n - 1)
                        if has_m:
                            act.wait_ge(k_st[n % 2], 16 * min(NM * 2, n // 2))
                    nc.scalar.activation(kn[:n_rows, n % 2], MM[s % 3][:n_rows, 0:WB], ACT.Square,
                                         accum_out=zr[:n_rows, 0, n:n + 1]).then_inc(n_q, 1)
                    act.wait_ge(n_m, n + 1)
                    nc.scalar.activation(zr[:n_rows, 2, n:n + 1], zr[:n_rows, 1, n:n + 1], ACT.Sqrt).then_inc(n_r, 1)
                    if n:
                        take_transposed(n - 1)
                for i in after_step(s):
                    act.wait_ge(ev_d, by_dve[s + 1])
                    prep_square(h0 + i)
                    if i:
                        prep_high(h0 + i - 1)
                    if i == NT:
                        prep_high(h0 + i)
                if (t == 2 or st == "m" and t == 1) and 1 <= b < len(blocks) - 1:
                    split_weights(b + 1)
            if normed:
                take_transposed(len(normed) - 1)

        @blk.vector
        def _(dve):
            link = linker(dve, c_dve)

            def split_weights(b):
                dve.wait_ge(w_hi, b + 1)
                nc.vector.tensor_tensor(WL[:, b % 2], wstage[:], WH[:, b % 2].bitcast(F32), ALU.subtract)\
                    .then_inc(w_lo, 1)

            def prep_norm(p):
                kind, i = preps[p]
                n = rows_of(kind, i)
                dve.wait_ge(p_sq, p + 1)
                nc.vector.tensor_scalar(ssq[:n, 1, p:p + 1], ssq[:n, 0, p:p + 1], 1.0 / D, EPS,
                                        ALU.mult, ALU.add).then_inc(p_ms, 1)
                dve.wait_ge(p_rt, p + 1)
                link(nc.vector.reciprocal(ssq[:n, 1, p:p + 1], ssq[:n, 2, p:p + 1]))
                gain = S["gain_m"] if kind == "m" else gain_bc
                nc.vector.scalar_tensor_tensor(xn[:n, p % 2], source(kind, i), ssq[:n, 1, p:p + 1],
                                               gain[:n], ALU.mult, ALU.mult).then_inc(p_n, 1)

            def prep_low(p):
                kind, i = preps[p]
                n = rows_of(kind, i)
                for half in range(2):
                    dve.wait_ge(p_hi, 2 * p + half + 1)
                    ks = slice(4 * half, 4 * half + 4)
                    nc.vector.tensor_tensor(parts(kind, i, False)[:, ks],
                                            TR[half][:].rearrange("p (k n) -> p k n", k=4)[:, :, :n],
                                            parts(kind, i, True)[:, ks].bitcast(F32), ALU.subtract).then_inc(p_lo, 1)

            dve.wait_ge(ld, n_ld)
            split_weights(0)
            if has_m:
                for p in range(NM):
                    prep_norm(p)
                    prep_low(p)
            split_weights(1)
            first_o = True
            for s, (st, j, t, b) in enumerate(steps):
                n_rows = P if st == "m" else rows(t)
                src = MM[s % 3][:n_rows, 0:WB]
                if st in "ox":
                    if first_o and n_x:
                        dve.wait_ge(x_ld, 32)
                    first_o = False
                    dve.wait_ge(mm, s + 1)
                    dst = hres[:n_rows, t, WB * j:WB * j + WB]
                    nc.vector.tensor_tensor(dst, dst, src, ALU.add).then_inc(ev_d, 1)
                elif s in norm_at:
                    n = norm_at[s]
                    width = 1.0 / WB
                    dve.wait_ge(n_q, n + 1)
                    nc.vector.tensor_scalar(zr[:n_rows, 1, n:n + 1], zr[:n_rows, 0, n:n + 1], width, EPS,
                                            ALU.mult, ALU.add).then_inc(n_m, 1)
                    dve.wait_ge(n_r, n + 1)
                    link(nc.vector.reciprocal(zr[:n_rows, 1, n:n + 1], zr[:n_rows, 2, n:n + 1]))
                    gain = S["gain_xk"] if st == "m" else S["gain_xq"]
                    nc.vector.scalar_tensor_tensor(kn[:n_rows, n % 2], src, zr[:n_rows, 1, n:n + 1], gain[:n_rows],
                                                   ALU.mult, ALU.mult).then_inc(ev_d, 1)
                for i in after_step(s):
                    prep_norm(h0 + i)
                    if i:
                        prep_low(h0 + i - 1)
                    if i == NT:
                        prep_low(h0 + i)
                if (t == 2 or st == "m" and t == 1) and 1 <= b < len(blocks) - 1:
                    split_weights(b + 1)

        @blk.tensor
        def _(pe):
            def prep_transpose(p):
                kind, i = preps[p]
                n = rows_of(kind, i)
                pe.wait_ge(p_n, p + 1)
                for half in range(2):
                    if p:
                        pe.wait_ge(p_lo, 2 * p + half - 1)
                    for k in range(4):
                        ks = 4 * half + k
                        ins = nc.tensor.transpose(TR[half][:, P * k:P * k + n], xn[:n, p % 2, P * ks:P * ks + P],
                                                  ident[:n, :n])
                    ins.then_inc(p_tr, 1)

            def transpose_normed(n):
                st, j, t, b = steps[normed[n]]
                r = P if st == "m" else rows(t)
                pe.wait_ge(ev_d, by_dve[normed[n] + 1])
                if n >= 2:
                    pe.wait_ge(n_T, n - 1)
                for k in range(2):
                    ins = nc.tensor.transpose(KT_[n % 2][:, P * k:P * k + r], kn[:r, n % 2, P * k:P * k + P],
                                              ident[:r, :r])
                ins.then_inc(n_t, 1)

            pe.wait_ge(ld, n_ld)
            if has_m:
                for p in range(NM):
                    prep_transpose(p)
            for s, (st, j, t, b) in enumerate(steps):
                r = P if st == "m" else rows(t)
                if s == 0 or steps[s - 1][3] != b:
                    pe.wait_ge(w_lo, b + 1)
                if s >= 3:
                    q = steps[s - 3]
                    if q[0] == "m" and q[1] >= 4:
                        pe.wait_ge(ev_a, by_act[s - 2])
                    else:
                        pe.wait_ge(ev_d, by_dve[s - 2])
                if st == "m":
                    xh, xl = S["MH"], S["ML"]
                    pe.wait_ge(p_lo, 2 * (t + 1))
                else:
                    xh, xl = XH, XL
                    if st == "q" and j == 0:
                        pe.wait_ge(p_lo, 2 * (h0 + t + 1))
                cols = slice(P * t, P * t + r)
                for k in range(KT):
                    for i, (x, w) in enumerate(((xh, WH), (xh, WL), (xl, WH))):
                        ins = nc.tensor.matmul(MM[s % 3][:r, 0:WB], x[:, k, cols], w[:, b % 2, k],
                                               start=k == 0 and i == 0, stop=k == KT - 1 and i == 2)
                ins.then_inc(mm, 1)
                if s in norm_at and norm_at[s] >= 1:
                    transpose_normed(norm_at[s] - 1)
                if st in "ox" and j == 3:
                    if t:
                        prep_transpose(h0 + t - 1)
                    if t == NT:
                        prep_transpose(h0 + t)
            if normed:
                transpose_normed(len(normed) - 1)


def block_cross(nc, I, O, S):
    ident, qxT, kmT, Vm, XH, XL = (S[x] for x in ("ident", "qxT", "kmT", "Vm", "XH", "XL"))
    ring, kTx, sTx, Pm, PT = S["cross_over"]
    bank = S["bank"]
    SC, TRB, OO, TRK = bank[0:2], bank[2:4], bank[4:6], bank[6]
    NU = NT * X + 1
    RING = 6
    loads = [(kv, b, h) for kv in range(2) for b in range(DB) for h in range(X)]
    NL = DB * X
    with ExitStack() as c:
        def sem(name):
            return nc.alloc_semaphore("s6_" + name)

        st = c.enter_context(nc.sbuf_tensor("st6", [P, 4, NU], F32))
        r_ld = [sem(f"r_ld{i}") for i in range(RING)]
        sp_, mx, ex, pn = sem("s"), sem("mx"), sem("ex"), sem("pn")
        tp, tc, op, oh, ol = sem("tp"), sem("tc"), sem("op"), sem("oh"), sem("ol")
        kp, kc, ks, vp = sem("kp"), sem("kc"), sem("ks"), sem("vp")
        sc_ = sem("sc")
        c_dve = sem("c_dve")
        blk = c.enter_context(nc.Block())

        def out_place(Xt, u):
            if u == NU - 1:
                return Xt[:, :, SEQ:T]
            i, h = u // X, u % X
            return Xt[:, 2 * h:2 * h + 2, P * i:P * i + P]

        def out_bank(u):
            if u == NU - 1:
                return OO[u % 2][:, 0:8 * TS].rearrange("p (k n) -> p k n", k=8)
            return OO[u % 2][:, 0:2 * P].rearrange("p (k n) -> p k n", k=2)

        @blk.sync
        def _(sp):
            for j, (kv, b, h) in enumerate(loads):
                if j >= RING:
                    k = j - RING + 1
                    sp.wait_ge(kp if k <= NL else vp, k if k <= NL else k - NL)
                sp.dma_start(ring[:, j % RING], I["cache_mem_kv"][0, b, :, kv, h].rearrange("(m p) e -> p m e", p=P))\
                    .then_inc(r_ld[j % RING], 16)

        @blk.scalar
        def _(act):
            def take_output(u):
                act.wait_ge(op, u + 1)
                nc.scalar.activation(out_place(XH, u), out_bank(u), ACT.Copy).then_inc(oh, 1)

            def exps(u):
                act.wait_ge(mx, u + 1)
                if u >= 2:
                    act.wait_ge(tp, u - 1)
                nc.scalar.activation(Pm[:, u % 2], SC[u % 2][:, 0:2 * P], ACT.Exp, bias=st[:, 1, u:u + 1],
                                     scale=1.0 / 16, accum_out=st[:, 2, u:u + 1]).then_inc(ex, 1)

            def take_keys(j):
                act.wait_ge(kp, j + 1)
                if j >= 2:
                    act.wait_ge(ks, j - 1)
                nc.scalar.activation(kTx[:, j % 2], TRK[:].rearrange("p (e m) -> p e m", e=2), ACT.Copy)\
                    .then_inc(kc, 1)

            for u in range(NU - 1):
                take_keys(u)
                exps(u)
                if u >= 2:
                    take_output(u - 2)
            act.wait_ge(ks, NL)
            nc.scalar.activation(sTx[:], bank[7][:, 0:2 * P], ACT.Copy).then_inc(sc_, 1)
            exps(NU - 1)
            for u in range(NU - 3, NU):
                take_output(u)

        @blk.vector
        def _(dve):
            link = linker(dve, c_dve)

            def maxima(u):
                dve.wait_ge(sp_, u + 1)
                link(nc.vector.tensor_reduce(st[:, 0, u:u + 1], SC[u % 2][:, 0:2 * P], AX.X, ALU.max, negate=True))
                nc.vector.tensor_scalar(st[:, 1, u:u + 1], st[:, 0, u:u + 1], 1.0 / 16, None, ALU.mult).then_inc(mx, 1)

            def normalise(u):
                dve.wait_ge(ex, u + 1)
                link(nc.vector.reciprocal(st[:, 3, u:u + 1], st[:, 2, u:u + 1]))
                nc.vector.tensor_scalar(Pm[:, u % 2], Pm[:, u % 2], st[:, 3, u:u + 1], None, ALU.mult).then_inc(pn, 1)

            def take_probabilities(u):
                dve.wait_ge(tp, u + 1)
                if u >= 2:
                    dve.wait_ge(op, u - 1)
                nc.vector.tensor_copy(PT[:, u % 2], TRB[u % 2][:, 0:2 * P].rearrange("p (m n) -> p m n", m=2))\
                    .then_inc(tc, 1)

            def take_output(u):
                dve.wait_ge(oh, u + 1)
                nc.vector.tensor_tensor(out_place(XL, u), out_bank(u), out_place(XH, u).bitcast(F32), ALU.subtract)\
                    .then_inc(ol, 1)

            for u in range(NU + 2):
                if u < NU:
                    maxima(u)
                    normalise(u)
                if 0 < u <= NU:
                    take_probabilities(u - 1)
                if u >= 2:
                    take_output(u - 2)

        @blk.tensor
        def _(pe):
            def scores(u):
                i, h = u // X, u % X
                if u >= 2:
                    pe.wait_ge(ex, u - 1)
                for e in range(2):
                    ins = nc.tensor.matmul(SC[u % 2][:, 0:2 * P], qxT[:, 2 * h + e, P * i:P * i + P],
                                           kmT[:, 2 * h + e], start=e == 0, stop=e == 1)
                ins.then_inc(sp_, 1)

            def transpose_p(u):
                pe.wait_ge(pn, u + 1)
                if u >= 2:
                    pe.wait_ge(tc, u - 1)
                for m in range(2):
                    ins = nc.tensor.transpose(TRB[u % 2][:, P * m:P * m + P], Pm[:, u % 2, P * m:P * m + P], ident[:])
                ins.then_inc(tp, 1)

            def weigh(u):
                i, h = u // X, u % X
                pe.wait_ge(tc, u + 1)
                if u >= 2:
                    pe.wait_ge(ol, u - 1)
                for e in range(2):
                    for m in range(2):
                        col = 2 * P * h + P * e
                        ins = nc.tensor.matmul(OO[u % 2][:, P * e:P * e + P], Vm[:, m, col:col + P],
                                               PT[:, u % 2, m], start=m == 0, stop=m == 1)
                ins.then_inc(op, 1)

            def keys(j):
                pe.wait_ge(r_ld[j % RING], 16 * (j // RING + 1))
                if j:
                    pe.wait_ge(kc, j)
                for e in range(2):
                    for m in range(2):
                        ins = nc.tensor.transpose(TRK[:, 2 * P * e + P * m:2 * P * e + P * m + P],
                                                  ring[:, j % RING, m, P * e:P * e + P], ident[:])
                ins.then_inc(kp, 1)

            def sample_scores(j):
                _, b, h = loads[j]
                pe.wait_ge(kc, j + 1)
                for m in range(2):
                    col = P * m + TS * h + DT * b
                    for e in range(2):
                        ins = nc.tensor.matmul(bank[7][:, col:col + DT], kTx[:, j % 2, e, P * m:P * m + P],
                                               qxT[:, 2 * h + e, SEQ + DT * b:SEQ + DT * b + DT],
                                               start=e == 0, stop=e == 1)
                ins.then_inc(ks, 1)

            for u in range(NU - 1):
                keys(u)
                scores(u)
                if u:
                    sample_scores(u - 1)
                    transpose_p(u - 1)
                if u >= 2:
                    weigh(u - 2)
            sample_scores(NL - 1)
            u = NU - 1
            pe.wait_ge(sc_, 1)
            pe.wait_ge(ex, u - 1)
            for m in range(2):
                ins = nc.tensor.transpose(SC[u % 2][:, P * m:P * m + P], sTx[:, P * m:P * m + P], ident[:])
            ins.then_inc(sp_, 1)
            transpose_p(u - 1)
            weigh(u - 2)
            weigh(u - 1)
            transpose_p(u)
            pe.wait_ge(tc, u + 1)
            pe.wait_ge(ol, u - 1)
            for j in range(NL):
                _, b, h = loads[NL + j]
                pe.wait_ge(r_ld[(NL + j) % RING], 16 * ((NL + j) // RING + 1))
                for e in range(2):
                    col = TS * (2 * h + e) + DT * b
                    for m in range(2):
                        ins = nc.tensor.matmul(OO[u % 2][:, col:col + DT], ring[:, (NL + j) % RING, m, P * e:P * e + P],
                                               PT[:, u % 2, m, TS * h + DT * b:TS * h + DT * b + DT],
                                               start=m == 0, stop=m == 1)
                ins.then_inc(vp if j < NL - 1 else op, 1)


def block_ffn(nc, I, O, S):
    XH, XL, WH, WL, wstage, ident, hres = (S[x] for x in ("XH", "XL", "WH", "WL", "wstage", "ident", "hres"))
    bank = S["bank"]
    NF = F // P
    TURNS = NF // 2
    W = 2 + SEQ + DB * (2 + DT)
    NW = W - 2
    CH = T // 3
    UNITS = 2 * TILES
    with ExitStack() as c:
        def sb(name, shape, dt=F32):
            return c.enter_context(nc.sbuf_tensor(name, shape, dt))

        def sem(name):
            return nc.alloc_semaphore("s8_" + name)

        AH, AL = sb("AH", [P, 2, T], F32R), sb("AL", [P, 2, T], F32R)
        DH, DL = sb("DH", [P, 2, D], F32R), sb("DL", [P, 2, D], F32R)
        dstage = sb("dstage", [P, D])
        UB = sb("UB", [P, 2, W])
        cv = sb("cv", [P, 2, NW])
        par = sb("par", [P, 2, P])
        pT = sb("pT", [P, 2, 20])
        last = sb("last", [P, 2, 18])
        co = sb("co", [18, 2, P])

        up_ld, dn_ld, par_ld = sem("up_ld"), sem("dn_ld"), sem("par_ld")
        w_hi, w_lo, d_hi, d_lo = sem("w_hi"), sem("w_lo"), sem("d_hi"), sem("d_lo")
        par_p, par_c = sem("par_p"), sem("par_c")
        cached = sem("cached")
        up = sem("up")
        ub = sem("ub")
        tap = sem("tap")
        conv = sem("conv")
        silu, prod = sem("silu"), sem("prod")
        a_hi, a_lo = sem("a_hi"), sem("a_lo")
        lst, co_p, co_c, co_st = sem("lst"), sem("co_p"), sem("co_c"), sem("co_st")
        dn = sem("dn")
        y = sem("y")
        y_st = sem("y_st")
        zero = sem("zero")
        c_dve = sem("c_dve")
        blk = c.enter_context(nc.Block())
        tail = cv[:, 0, SEQ:].rearrange("p (b n) -> p b n", b=DB)[:, :, 2:]
        w_up = I["w_up"][0].rearrange("(k p) (g c) -> p k g c", p=P, g=2)
        seqs = UB[:, :, 2 + SEQ:W].rearrange("p g (b n) -> p g b n", b=DB)

        @blk.sync
        def _(sp):
            def tile(f, first):
                cols = bass.ds(f * P, P)
                if not first:
                    sp.wait_ge(w_lo, f)
                for g in range(2):
                    sp.dma_start(wstage[:, :, P * g:P * g + P], w_up[:, :, g, cols]).then_inc(up_ld, 16)
                if first:
                    sp.wait_ge(zero, 1)
                else:
                    sp.wait_ge(par_p, f)
                for lo, hi, src in ((0, 16, I["state_ffn_conv"][0].rearrange("b r (g c) -> (b r) g c", g=2)),
                                    (16, 19, I["conv_w"][0].rearrange("r (g c) -> r g c", g=2)),
                                    (19, 20, I["conv_b"].rearrange("r (g c) -> r g c", g=2))):
                    sp.dma_start(par[lo:hi], src[:, :, cols]).then_inc(par_ld, 16)
                if not first:
                    sp.wait_ge(d_lo, f)
                sp.dma_start(dstage[:], I["w_down"][0, cols]).then_inc(dn_ld, 16)

            tile(0, True)
            with sp.Fori(1, NF) as f:
                tile(f, False)
            for t in range(TILES):
                sp.wait_ge(y, (TURNS - 1) * UNITS + 2 * t + 2)
                dst = O["yp"][0, P * t:P * t + P] if t < NT else O["ys"].rearrange("b t d -> (b t) d")
                sp.dma_start(dst, hres[:rows(t), t]).then_inc(y_st, 16)
            sp.wait_ge(y_st, 16 * TILES)

        @blk.gpsimd
        def _(pool):
            def store(f, value):
                cols = bass.ds(f * P, P)
                pool.wait_ge(co_c, value)
                pool.dma_start(O["conv_p"][0, 0].rearrange("r (g c) -> r g c", g=2)[:, :, cols], co[0:2])\
                    .then_inc(co_st, 16)
                pool.dma_start(O["conv_s"][0].rearrange("b r (g c) -> (b r) g c", g=2)[:, :, cols], co[2:18])\
                    .then_inc(co_st, 16)

            store(0, 1)
            with pool.Fori(1, NF) as f:
                store(f, f + 1)
            pool.wait_ge(co_st, 32 * NF)

        @blk.scalar
        def _(act):
            def split_up(f, slot, free):
                act.wait_ge(up_ld, f * 32 + 32)
                if free:
                    act.wait_ge(up, f * 2 - 2)
                nc.scalar.activation(WH[:, slot], wstage[:], ACT.Copy).then_inc(w_hi, 1)

            def split_down(f, slot, free):
                act.wait_ge(dn_ld, f * 16 + 16)
                if free is not None:
                    act.wait_ge(dn, free)
                nc.scalar.activation(DH[:, slot], dstage[:], ACT.Copy).then_inc(d_hi, 1)

            def tile(f, slot, first, free, more):
                if more:
                    split_up(f + 1, 1 - slot, not first)
                act.wait_ge(cached, f + 1)
                for g in range(2):
                    act.wait_ge(up, f * 2 + g + 1)
                    for j in range(2):
                        nc.scalar.activation(UB[:, g, 2 + CH * j:2 + CH * j + CH], bank[3 * g + j][:, 0:CH], ACT.Copy)
                    n = SEQ - 2 * CH
                    nc.scalar.activation(UB[:, g, 2 + 2 * CH:2 + SEQ], bank[3 * g + 2][:, 0:n], ACT.Copy)
                    nc.scalar.activation(seqs[:, g, :, 2:],
                                         bank[3 * g + 2][:, n:CH].rearrange("p (b n) -> p b n", b=DB), ACT.Copy)\
                        .then_inc(ub, 1)
                    act.wait_ge(ub, f * 2 + g + 1)
                    if not first and g == 0:
                        act.wait_ge(a_lo, f)
                    nc.scalar.activation(cv[:, g], UB[:, g, 2:], ACT.Identity, scale=pT[:, g, 18:19],
                                         bias=pT[:, g, 19:20]).then_inc(tap, 1)
                act.wait_ge(conv, f * 2 + 1)
                nc.scalar.activation(cv[:, 0], cv[:, 0], ACT.Silu).then_inc(silu, 1)
                act.wait_ge(prod, f + 1)
                if free is not None:
                    act.wait_ge(dn, free)
                nc.scalar.activation(AH[:, slot, 0:SEQ], cv[:, 0, 0:SEQ], ACT.Copy)
                nc.scalar.activation(AH[:, slot, SEQ:T].rearrange("p (b n) -> p b n", b=DB),
                                     tail, ACT.Copy).then_inc(a_hi, 1)
                split_down(f, slot, free)

            split_up(0, 0, False)

            def turn(n, first, more):
                tile(n * 2, 0, first, None if first else n * UNITS, True)
                tile(n * 2 + 1, 1, False, None if first else n * UNITS, more)

            turn(0, True, True)
            with act.Fori(1, TURNS - 1) as n:
                turn(n, False, True)
            turn(TURNS - 1, False, False)

        @blk.vector
        def _(dve):
            nc.vector.memset(par[:], 0.0)
            nc.vector.memset(UB[:, :, 0:2], 0.0).then_inc(zero, 1)
            dve.wait_ge(zero, 1)

            def split_up(f, slot):
                dve.wait_ge(w_hi, f + 1)
                nc.vector.tensor_tensor(WL[:, slot], wstage[:], WH[:, slot].bitcast(F32), ALU.subtract)\
                    .then_inc(w_lo, 1)

            def params(f, first):
                if not first:
                    dve.wait_ge(lst, f)
                    dve.wait_ge(conv, f * 2)
                dve.wait_ge(par_p, f + 1)
                ps = bank[6][:, 0:2 * P].rearrange("p (g n) -> p g n", g=2)[:, :, 0:20]
                nc.vector.tensor_copy(pT[:], ps).then_inc(par_c, 1)
                dve.wait_ge(par_c, f + 1)
                for g in range(2):
                    ins = nc.vector.tensor_copy(seqs[:, g, :, 0:2], pT[:, g, 0:16].rearrange("p (b n) -> p b n", b=DB))
                ins.then_inc(cached, 1)

            def convolve(f, g, part):
                if part == 0:
                    dve.wait_ge(tap, f * 2 + g + 1)
                    nc.vector.scalar_tensor_tensor(cv[:, g], UB[:, g, 1:W - 1], pT[:, g, 17:18], cv[:, g],
                                                   ALU.mult, ALU.add).then_inc(c_dve, 1)
                else:
                    dve.wait_ge(c_dve, f * 2 + g + 1)
                    nc.vector.scalar_tensor_tensor(cv[:, g], UB[:, g, 0:W - 2], pT[:, g, 16:17], cv[:, g],
                                                   ALU.mult, ALU.add).then_inc(conv, 1)

            def columns(f, first):
                if not first:
                    dve.wait_ge(co_p, f)
                nc.vector.tensor_copy(last[:, :, 0:2], UB[:, :, SEQ:SEQ + 2])
                for g in range(2):
                    ins = nc.vector.tensor_copy(last[:, g, 2:18].rearrange("p (b n) -> p b n", b=DB),
                                                seqs[:, g, :, DT:DT + 2])
                ins.then_inc(lst, 1)

            def product(f):
                dve.wait_ge(silu, f + 1)
                dve.wait_ge(conv, f * 2 + 2)
                nc.vector.tensor_tensor(cv[:, 0], cv[:, 0], cv[:, 1], ALU.mult).then_inc(prod, 1)

            def low(f, slot):
                dve.wait_ge(a_hi, f + 1)
                nc.vector.tensor_tensor(AL[:, slot, 0:SEQ], cv[:, 0, 0:SEQ], AH[:, slot, 0:SEQ].bitcast(F32),
                                        ALU.subtract)
                nc.vector.tensor_tensor(AL[:, slot, SEQ:T].rearrange("p (b n) -> p b n", b=DB), tail,
                                        AH[:, slot, SEQ:T].rearrange("p (b n) -> p b n", b=DB).bitcast(F32),
                                        ALU.subtract).then_inc(a_lo, 1)
                dve.wait_ge(d_hi, f + 1)
                nc.vector.tensor_tensor(DL[:, slot], dstage[:], DH[:, slot].bitcast(F32), ALU.subtract)\
                    .then_inc(d_lo, 1)

            def columns_out(f, first):
                dve.wait_ge(co_p, f + 1)
                if not first:
                    dve.wait_ge(co_st, f * 32)
                nc.vector.tensor_copy(co[:], bank[7][0:18, 0:2 * P].rearrange("p (g n) -> p g n", g=2))\
                    .then_inc(co_c, 1)

            def add_down(n, lo, hi):
                for u in range(lo, hi):
                    t, half = u // 2, u % 2
                    dst = hres[:rows(t), t, 512 * half:512 * half + 512]
                    dve.wait_ge(dn, n * UNITS + u + 1)
                    nc.vector.tensor_tensor(dst, dst, bank[6 + u % 2][:rows(t)], ALU.add).then_inc(y, 1)

            split_up(0, 0)
            params(0, True)

            def turn(n, first, more):
                f = n * 2

                def adds(lo, hi):
                    if not first:
                        add_down(n - 1, lo, hi)

                split_up(f + 1, 1)
                convolve(f, 0, 0)
                convolve(f, 0, 1)
                if not first:
                    columns_out(f - 1, False)
                adds(0, 4)
                convolve(f, 1, 0)
                adds(4, 6)
                convolve(f, 1, 1)
                adds(6, 8)
                columns(f, first)
                adds(8, 11)
                product(f)
                adds(11, UNITS)
                params(f + 1, False)
                low(f, 0)
                columns_out(f, first)
                if more:
                    split_up(f + 2, 0)
                for g in range(2):
                    convolve(f + 1, g, 0)
                    convolve(f + 1, g, 1)
                columns(f + 1, False)
                product(f + 1)
                low(f + 1, 1)
                if more:
                    params(f + 2, False)

            turn(0, True, True)
            with dve.Fori(1, TURNS - 1) as n:
                turn(n, False, True)
            turn(TURNS - 1, False, False)
            columns_out(NF - 1, False)
            add_down(TURNS - 1, 0, UNITS)

        @blk.tensor
        def _(pe):
            def params(f):
                pe.wait_ge(par_ld, f * 48 + 48)
                for g in range(2):
                    ins = nc.tensor.transpose(bank[6][:, P * g:P * g + P], par[:, g], ident[:])
                ins.then_inc(par_p, 1)

            def up_project(f, slot, first):
                pe.wait_ge(w_lo, f + 1)
                for g in range(2):
                    if not first:
                        pe.wait_ge(ub, f * 2 + g - 1)
                    for j in range(3):
                        for k in range(KT):
                            for i, (w, x) in enumerate(((WH, XH), (WH, XL), (WL, XH))):
                                ins = nc.tensor.matmul(bank[3 * g + j][:, 0:CH], w[:, slot, k, P * g:P * g + P],
                                                       x[:, k, CH * j:CH * j + CH],
                                                       start=k == 0 and i == 0, stop=k == KT - 1 and i == 2)
                    ins.then_inc(up, 1)

            def columns_out(f):
                pe.wait_ge(lst, f + 1)
                for g in range(2):
                    ins = nc.tensor.transpose(bank[7][0:18, P * g:P * g + P], last[:, g], ident[:])
                ins.then_inc(co_p, 1)

            def down_project(n):
                pe.wait_ge(a_lo, n * 2 + 2)
                pe.wait_ge(d_lo, n * 2 + 2)
                pe.wait_ge(co_c, n * 2 + 2)
                for u in range(UNITS):
                    t, half = u // 2, u % 2
                    r = rows(t)
                    if u >= 2:
                        pe.wait_ge(y, n * UNITS + u - 1)
                    for s in range(2):
                        for i, (x, w) in enumerate(((AH, DH), (AH, DL), (AL, DH))):
                            ins = nc.tensor.matmul(bank[6 + u % 2][:r, :], x[:, s, P * t:P * t + r],
                                                   w[:, s, 512 * half:512 * half + 512],
                                                   start=s == 0 and i == 0, stop=s == 1 and i == 2)
                    ins.then_inc(dn, 1)

            def turn(n, first, more):
                f = n * 2
                up_project(f, 0, first)
                if not first:
                    columns_out(f - 1)
                    pe.wait_ge(par_c, f + 1)
                    down_project(n - 1)
                    pe.wait_ge(y, n * UNITS)
                params(f + 1)
                columns_out(f)
                up_project(f + 1, 1, False)
                if more:
                    pe.wait_ge(par_c, f + 2)
                    params(f + 2)
                    pe.wait_ge(co_c, f + 1)

            params(0)
            pe.wait_ge(par_c, 1)
            turn(0, True, True)
            with pe.Fori(1, TURNS - 1) as n:
                turn(n, False, True)
            turn(TURNS - 1, False, False)
            pe.wait_ge(co_c, NF - 1)
            columns_out(NF - 1)
            pe.wait_ge(par_c, NF)
            down_project(TURNS - 1)


def cache_rows(O, g, t, kv):
    if t == NT:
        return [(O[f"kv_s{g}"][0, :, :, kv].rearrange("b t h e -> (b t) (h e)"), 0, TS)]
    dst = O[f"kv_p{g}"][0, 0, :, kv].rearrange("n h e -> n (h e)")
    if g == 0:
        return [(dst, 0, P)] if t == NT - 1 else []
    if g == 1:
        return [(dst[t // 2:t // 2 + 4 * (P - 1) + 1:4], 0, P)] if t % 2 else []
    return [(dst[t:t + 8 * (P - 1) + 1:8], 0, P)]


OUTS = [("yp", (1, SEQ, D)), ("ys", (DB, DT, D)),
        ("kv_p0", (1, 1, 128, 2, H, E)), ("kv_p1", (1, 1, 512, 2, H, E)), ("kv_p2", (1, 1, 1024, 2, H, E)),
        ("ssm_re_p", (1, 1, 16, 64)), ("ssm_im_p", (1, 1, 16, 64)), ("conv_p", (1, 1, 2, 5632)),
        ("mem_kv_p", (1, 1, 256, 2, 4, 256)),
        ("kv_s0", (1, DB, DT, 2, H, E)), ("kv_s1", (1, DB, DT, 2, H, E)), ("kv_s2", (1, DB, DT, 2, H, E)),
        ("ssm_re_s", (1, DB, 16, 64)), ("ssm_im_s", (1, DB, 16, 64)), ("conv_s", (1, DB, 2, 5632))]


def build(nc, I, O):
    before = nc.snapshot_sems()
    with ExitStack() as c:
        def sb(name, shape, dt=F32):
            return c.enter_context(nc.sbuf_tensor(name, shape, dt))

        S = {"stat": nc.dram_tensor("stat", (SEQ, 2 * G * H), F32, kind="Internal").ap()}
        S["bank"] = [c.enter_context(nc.psum_tensor(f"bank{i}", [P, 512], F32)) for i in range(8)]
        S["ident"] = sb("ident", [P, P])
        S["gain_bc"] = sb("gain_bc", [P, D])
        S["eps"] = sb("eps", [P, 1])
        with ExitStack() as o:
            def so(name, shape):
                return o.enter_context(nc.sbuf_tensor(name, shape, F32))

            S["ssm_over"] = (so("BpR", [P, 8, 16]), so("BpI", [P, 8, 16]), so("ER", [P, 8, P]), so("EI", [P, 8, P]),
                             so("XR", [P, 8, P]), so("XI", [P, 8, P]), so("HR", [P, 8, P + 1]),
                             so("HI", [P, 8, P + 1]), so("ta", [P, 8, P]), so("tb", [P, 8, P]),
                             so("BAR", [P, 8, P]), so("BAI", [P, 8, P]))
            S["MZ"] = so("MZ", [16, 16, P])
            S["t1"] = so("t1", [P, 8, P])
            S["tH"] = so("tH", [P, 8 * 9 * 16])
            S["ssm_mats"] = (so("CAR", [P, 8, 9, 16]), so("CAI", [P, 8, 9, 16]), so("WBR", [P, 8, P]),
                             so("WBI", [P, 8, P]), so("TZ", [P, 16, P]), so("UT", [P, 16, P]), so("Sin", [DB, 2, D]))
        with ExitStack() as o:
            def co(name, shape):
                return o.enter_context(nc.sbuf_tensor(name, shape, F32))

            S["cross_over"] = (co("ring6", [P, 6, 2, 2 * P]), co("kTx", [P, 2, 2, 2 * P]), co("sTx", [P, 2 * P]),
                               co("Pm6", [P, 2, 2 * P]), co("PT6", [P, 2, 2, P]))
        S["wstage"] = sb("wstage", [P, KT, WB])
        S["WH"] = sb("WH", [P, 2, KT, WB], F32R)
        S["WL"] = sb("WL", [P, 2, KT, WB], F32R)
        S["XH"] = sb("XH", [P, KT, T], F32R)
        S["XL"] = sb("XL", [P, KT, T], F32R)
        with ExitStack() as a:
            def sa(name, shape, dt=F32):
                return a.enter_context(nc.sbuf_tensor(name, shape, dt))

            S["mask"] = sa("mask", [P, 3 * P])
            S["rope"] = sa("rope", [P, G * NT + 1, 32])
            S["qk_gain"] = sa("qk_gain", [P, 2, E])
            S["U"] = sa("U", [P, 16, NT, 16])
            S["US"] = sa("US", [TS, SW])
            S["att"] = sa("att", [P, G * NT, GW])
            S["qkS"] = sa("qkS", [P, G, 2, 2, TS])
            S["vS"] = sa("vS", [TS, G, GW])
            S["negm"] = sa("negm", [P, G * NT, H])
            S["lsum"] = sa("lsum", [P, G * NT, H])
            S["tables"] = [(S["ident"][:], I["c_ident"]), (S["mask"][:], I["c_mask"]),
                           (S["rope"][:], I["c_rope"]), (S["gain_bc"][:], I["norm_mix"][0].partition_broadcast(P)),
                           (S["qk_gain"][:, 0], I["q_norm"][0].partition_broadcast(P)),
                           (S["qk_gain"][:, 1], I["k_norm"][0].partition_broadcast(P))]
            with ExitStack() as b:
                S["qT"] = b.enter_context(nc.sbuf_tensor("qT", [P, 2, SEQ], F32))
                S["kT"] = b.enter_context(nc.sbuf_tensor("kT", [P, 2, SEQ], F32))
                S["V"] = b.enter_context(nc.sbuf_tensor("V", [P, NT, GW], F32))
                block_project(nc, I, O, S)
            S["ysb"] = sa("ysb", [P, TILES, SW])
            block_ssm(nc, I, O, S)
            S["attS"] = sa("attS", [TS, AW])
            S["smask"] = sa("smask", [P, G, P + TS])
            block_sample(nc, I, O, S)
            block_mix(nc, I, O, S)
        nc.clear_and_free_semaphores(nc.allocated_since(before))
        nc.all_engine_barrier()
        S["hres"] = sb("hres", [P, TILES, D])
        with ExitStack() as b:
            def sb_(name, shape):
                return b.enter_context(nc.sbuf_tensor(name, shape, F32))

            S["kmT"], S["Vm"] = sb_("kmT", [P, KT, 2 * P]), sb_("Vm", [P, 2, D])
            S["gain_xq"] = sb_("gain_xq", [P, WB])
            with ExitStack() as m:
                def sm(name, shape, dt=F32):
                    return m.enter_context(nc.sbuf_tensor(name, shape, dt))

                S["MH"], S["ML"] = sm("MH", [P, KT, 2 * P], F32R), sm("ML", [P, KT, 2 * P], F32R)
                S["mraw"], S["gain_m"], S["gain_xk"] = sm("mraw", [P, 2, D]), sm("gain_m", [P, D]), sm("gain_xk", [P, WB])
            S["qxT"] = sb_("qxT", [P, KT, T])
            S["loadsmoq"] = [(S["gain_bc"][:], I["norm_x"][0].partition_broadcast(P)),
                             (S["gain_m"][:], I["norm_mem"][0].partition_broadcast(P)),
                             (S["gain_xk"][:], I["xk_norm"][0].partition_broadcast(P)),
                             (S["gain_xq"][:], I["xq_norm"][0].partition_broadcast(P)),
                             (S["mraw"][:], I["mem_prompt"][0].rearrange("(t p) d -> p t d", p=P))]
            block_dense(nc, I, O, S, "moq")
            block_cross(nc, I, O, S)
            S["loadsx"] = [(S["gain_bc"][:], I["norm_ffn"][0].partition_broadcast(P))]
        block_dense(nc, I, O, S, "x")
        block_ffn(nc, I, O, S)


def shape_constants():
    q, k = np.arange(P)[:, None], np.arange(P)[None, :]
    prev = np.where(k >= q, 0, NEG)
    own = np.where(k <= q, 0, NEG)
    pair = np.where((k % 2 == q % 2) & (k <= q), 0, NEG)
    mask = np.concatenate([prev, own, pair], 1).astype(np.float32)
    pos = np.zeros((P, G * NT + 1), np.int64)
    for g in range(G):
        for t in range(NT):
            pos[:, g * NT + t] = first_token(g, t) + STRIDE[g] * np.arange(P)
    pos[:TS, G * NT] = PAST + np.arange(TS) % DT
    inv = np.power(np.float32(500000.0), -np.arange(8, dtype=np.float32) * np.float32(2.0) / np.float32(16))
    ang = pos.astype(np.float32)[:, :, None] * inv.astype(np.float32)
    cos, sin = np.cos(ang), np.sin(ang)
    rope = np.concatenate([cos, cos, -sin, sin], 2).astype(np.float32)
    b, t = (np.arange(P) % TS // DT)[:, None], (np.arange(P) % DT)[:, None]
    key, nb, ni = np.arange(P)[None, :], np.arange(TS)[None, :] // DT, np.arange(TS)[None, :] % DT
    ok = [np.concatenate([key >= t, (nb == b) & (ni <= t)], 1),
          np.concatenate([(key >= 0) & (t >= 0), (nb == b) & (ni == t)], 1),
          np.concatenate([key // 64 == t % 2, (nb == b) & (ni == t)], 1)]
    smask = np.stack([np.where(x, 0, NEG) for x in ok], 1).astype(np.float32)
    return {"c_smask": smask, "c_ident": np.eye(P, dtype=np.float32), "c_mask": mask, "c_rope": rope}


def kernel(**inputs):
    import numpy as _np
    import concourse.bacc as _bacc
    from concourse import mybir as _mybir
    from concourse.bass_utils import run_bass_kernel_spmd as _run

    nc = _bacc.Bacc("TRN2", target_bir_lowering=False, num_devices=1)
    arrays, I, O = {}, {}, {}
    for name, a in [*inputs.items(), *shape_constants().items()]:
        a = _np.ascontiguousarray(a)
        arrays[name] = a
        I[name] = nc.dram_tensor(name, a.shape, _mybir.dt.from_np(a.dtype), kind="ExternalInput").ap()
    for name, shape in OUTS:
        O[name] = nc.dram_tensor("out_" + name, shape, F32, kind="ExternalOutput").ap()
    build(nc, I, O)
    r = _run(nc, [arrays], core_ids=[0])
    return tuple(r.results[0]["out_" + name] for name, _ in OUTS)
```

```python
import math
from contextlib import ExitStack

import numpy as np
import concourse.bass as bass
from concourse import mybir

F32 = mybir.dt.float32
F32R = mybir.dt.float32r
ALU = mybir.AluOpType
ACT = mybir.ActivationFunctionType
AX = mybir.AxisListType

P = 128
D = 1024
KT = D // P
SEQ = 1024
NT = SEQ // P
DB, DT = 8, 4
TS = DB * DT
T = SEQ + TS
TILES = NT + 1
G = 3
H = 4
E = 64
GW = H * E
AW = G * GW
SW = D - AW
WB = 256
PAST = 1024
EPS = 1e-6
NEG = -1e30
X = 4
F = 2816


def rows(t):
    return P if t < NT else TS


STRIDE = [1, 4, 8, 8]


def first_token(order, t):
    return (P * t, t // 2 + 4 * P * (t % 2), t, t)[order]


def columns(ap, order, t):
    if t == NT:
        return ap[..., SEQ:T]
    first = first_token(order, t)
    return ap[..., first:first + STRIDE[order] * (P - 1) + 1:STRIDE[order]]


def linker(eng, sem):
    count = [0]

    def link(ins):
        count[0] += 1
        ins.then_inc(sem, 1)
        eng.wait_ge(sem, count[0])
    return link


def refine_rsqrt(nc, link, sums, r, tmp, width):
    link(nc.vector.tensor_scalar(tmp, sums, -0.5 / width, -0.5 * EPS, ALU.mult, ALU.add))
    link(nc.vector.tensor_tensor(tmp, tmp, r, ALU.mult))
    link(nc.vector.tensor_tensor(tmp, tmp, r, ALU.mult))
    link(nc.vector.scalar_tensor_tensor(r, tmp, 1.5, r, ALU.add, ALU.mult))


def per_head(ap, n):
    return ap.unsqueeze(2).to_broadcast([n, H, E])


def block_project(nc, I, O, S):
    XH, XL, WH, WL, wstage = S["XH"], S["XL"], S["WH"], S["WL"], S["wstage"]
    ident, gain_bc, qk_gain, rope, mask = S["ident"], S["gain_bc"], S["qk_gain"], S["rope"], S["mask"]
    qT, kT, V, U, US, att = S["qT"], S["kT"], S["V"], S["U"], S["US"], S["att"]
    qkS, vS, negm, lsum = S["qkS"], S["vS"], S["negm"], S["lsum"]
    bank = S["bank"]
    MM, TR, SC, OB = bank[0:3], bank[3:5], bank[5:7], bank[7]
    QK = [(b, t) for b in range(9) if b % 3 < 2 for t in range(TILES)]
    qk_at = {bt: n for n, bt in enumerate(QK)}

    with ExitStack() as c:
        def sb(name, shape, dt=F32):
            return c.enter_context(nc.sbuf_tensor(name, shape, dt))

        def sem(name):
            return nc.alloc_semaphore(name)

        ssq = sb("ssq", [P, 3, TILES])
        zs = sb("zs", [P, 3, GW])
        zsq = sb("zsq", [P, 2, GW])
        zn = sb("zn", [P, 4, GW])
        zt = sb("zt", [P, 2, H, 16])
        zr = sb("zr", [P, 3, len(QK), H])
        rl = sb("rl", [P, G * NT, H])
        with ExitStack() as early:
            xin = early.enter_context(nc.sbuf_tensor("xin", [P, 2, D], F32))
            junk = early.enter_context(nc.sbuf_tensor("junk", [P, D], F32))
        Sm = sb("Sm", [P, 2, H, 2 * P])
        PT = sb("PT", [P, 2, 2 * H, P])

        x_ld = [sem(f"x_ld{i}") for i in range(2)]
        x_sq = sem("x_sq")
        x_rt = sem("x_rt")
        x_n = sem("x_n")
        x_tr = sem("x_tr")
        x_hi = sem("x_hi")
        x_lo = sem("x_lo")
        w_ld = sem("w_ld")
        w_hi = sem("w_hi")
        w_lo = sem("w_lo")
        mm = sem("mm")
        ev = sem("ev")
        z_sq = sem("z_sq")
        z_ms = sem("z_ms")
        z_rt = sem("z_rt")
        z_s = sem("z_s")
        z_n = sem("z_n")
        z_tr = sem("z_tr")
        z_T = sem("z_T")
        k_st = [sem(f"k_st{i}") for i in range(4)]
        v_st = sem("v_st")
        at_s = sem("at_s")
        at_mask = sem("at_mask")
        at_m = sem("at_m")
        at_e = sem("at_e")
        at_tr = sem("at_tr")
        at_pa = sem("at_pa")
        at_pb = sem("at_pb")
        at_pv = sem("at_pv")
        at_o = sem("at_o")
        tab = sem("tab")
        c_dve = sem("c_dve")
        c_act, c_pool = sem("c_act"), sem("c_pool")
        zero = sem("zero")

        norm_at = {b * TILES + t + 1: q for q, (b, t) in enumerate(QK)}
        take_at = {b * TILES + t + 3: q for q, (b, t) in enumerate(QK)}

        def wcols(b):
            return (b % 3) * AW + (b // 3) * GW if b < 9 else 3 * AW

        def key_tiles(g, i):
            return [i - 1, i] if (g == 0 and i > 0) or (g == 1 and i % 2) else [i]

        start = [TILES * (3 * (a // NT) + 2) + 2 + 2 * (a % NT) for a in range(G * NT)]
        LAST = start[-1] + 4

        def due(s, after):
            return [a for a in range(G * NT) if start[a] + after == s]

        ab = []
        for a in range(G * NT):
            ab.append(len(key_tiles(a // NT, a % NT)))
        a_before = [sum(ab[:a]) for a in range(G * NT + 1)]
        b_before = [sum(x == 2 for x in ab[:a]) for a in range(G * NT + 1)]

        k_step = {b * TILES + t: q for q, (b, t) in enumerate(QK) if b % 3 == 1}
        k_stores = [0] * len(QK)
        for q, (b, t) in enumerate(QK):
            k_stores[q] = sum(16 * len(cache_rows(O, QK[r][0] // 3, QK[r][1], 0))
                              for r in range(q) if r % 4 == q % 4 and QK[r][0] % 3 == 1)

        blk = c.enter_context(nc.Block())

        @blk.sync
        def _(sp):
            def load_weights(b):
                if b:
                    sp.wait_ge(w_lo, b)
                sp.dma_start(wstage[:], I["w_in"][0, :, wcols(b):wcols(b) + WB]
                             .rearrange("(k p) n -> p k n", p=P)).then_inc(w_ld, 16)

            for i in range(TILES):
                if i >= 2:
                    sp.wait_ge(x_tr, 2 * (i - 1))
                src = I["x_prompt"][0, P * i:P * i + P, :] if i < NT else \
                    I["x_sample"].rearrange("b t d -> (b t) d")
                sp.dma_start(xin[:rows(i), i % 2, :], src).then_inc(x_ld[i % 2], 16)
                if i == 0:
                    for dst, src in S["tables"]:
                        sp.dma_start(dst, src).then_inc(tab, 16)
                if i in (1, 4):
                    load_weights(i // 4)
            stored, vs = [0] * 4, 0
            for s in range(9 * TILES + 1):
                b, t = s // TILES, s % TILES
                if s - 1 in k_step:
                    q = k_step[s - 1]
                    for dst, lo, hi in cache_rows(O, QK[q][0] // 3, QK[q][1], 0):
                        sp.wait_ge(z_n, q + 1)
                        sp.dma_start(dst, zn[lo:hi, q % 4]).then_inc(k_st[q % 4], 16)
                        stored[q % 4] += 16
                if b % 3 == 2 and b < 9:
                    for dst, lo, hi in cache_rows(O, b // 3, t, 1):
                        sp.wait_ge(ev, s + 1)
                        sp.dma_start(dst, V[lo:hi, t] if t < NT else vS[lo:hi, b // 3]).then_inc(v_st, 16)
                        vs += 16
                if t == 3 and b < 8:
                    load_weights(b + 2)
            for i in range(4):
                sp.wait_ge(k_st[i], stored[i])
            sp.wait_ge(v_st, vs)

        @blk.gpsimd
        def _(pool):
            nc.gpsimd.memset(S["eps"][:], EPS).then_inc(zero, 1)
            link = linker(pool, c_pool)

            def scale(q):
                b, t = QK[q]
                n = rows(t)
                pool.wait_ge(z_rt, q + 1)
                sums, r, tmp = (zr[:n, x, q] for x in range(3))
                link(nc.gpsimd.tensor_scalar(tmp, sums, -0.5 / E, -0.5 * EPS, ALU.mult, ALU.add))
                link(nc.gpsimd.tensor_tensor(tmp, tmp, r, ALU.mult))
                link(nc.gpsimd.tensor_tensor(tmp, tmp, r, ALU.mult))
                link(nc.gpsimd.tensor_scalar(tmp, tmp, 1.5, None, ALU.add))
                link(nc.gpsimd.tensor_tensor(r, r, tmp, ALU.mult))
                if q >= 4:
                    pool.wait_ge(z_tr, q - 3)
                    if k_stores[q]:
                        pool.wait_ge(k_st[q % 4], k_stores[q])
                nc.gpsimd.tensor_tensor(zn[:n, q % 4].rearrange("p (h e) -> p h e", h=H),
                                        zs[:n, q % 3].rearrange("p (h e) -> p h e", h=H),
                                        per_head(zr[:n, 1, q], n), ALU.mult).then_inc(z_s, 1)

            for s in range(9 * TILES):
                b, t = s // TILES, s % TILES
                n = rows(t)
                if (b, t) in qk_at:
                    q = qk_at[b, t]
                    pool.wait_ge(ev, s + 1)
                    if q >= 2:
                        pool.wait_ge(z_ms, q - 1)
                    nc.gpsimd.tensor_tensor(zsq[:n, q % 2], zs[:n, q % 3], zs[:n, q % 3], ALU.mult)\
                        .then_inc(z_sq, 1)
                if s in norm_at:
                    scale(norm_at[s])

        v_stores = [sum(16 * len(cache_rows(O, gg, t, 1)) for gg in range(g) for t in range(TILES))
                    for g in range(G + 1)]

        def split_weights_act(act, b):
            act.wait_ge(w_ld, 16 * (b + 1))
            if b >= 2:
                act.wait_ge(mm, (b - 1) * TILES)
            nc.scalar.activation(WH[:, b % 2], wstage[:], ACT.Copy).then_inc(w_hi, 1)

        @blk.scalar
        def _(act):
            link = linker(act, c_act)
            nc.scalar.preload_act_table_set("natural_log_exp_and_others")
            act.wait_ge(zero, 1)

            def rsqrt_of_mean(sums, out, width):
                n = sums.shape[0]
                link(nc.scalar.activation(out, sums, ACT.Ln, scale=1.0 / width, bias=S["eps"][:n]))
                return nc.scalar.activation(out, out, ACT.Exp, scale=-0.5)

            def prepare(i):
                if i < TILES:
                    n = rows(i)
                    act.wait_ge(x_ld[i % 2], 16 * (i // 2 + 1))
                    if i:
                        act.wait_ge(x_sq, i)
                    nc.scalar.activation(junk[:n], xin[:n, i % 2], ACT.Square,
                                         accum_out=ssq[:n, 0, i:i + 1]).then_inc(x_sq, 1)
                    act.wait_ge(x_sq, i + 1)
                    rsqrt_of_mean(ssq[:n, 0, i:i + 1], ssq[:n, 1, i:i + 1], D).then_inc(x_rt, 1)
                if 0 < i <= TILES:
                    n = rows(i - 1)
                    for half in range(2):
                        act.wait_ge(x_tr, 2 * (i - 1) + half + 1)
                        nc.scalar.activation(XH[:, 4 * half:4 * half + 4, P * (i - 1):P * (i - 1) + n],
                                             TR[half][:, 0:4 * P].rearrange("p (k n) -> p k n", k=4)[:, :, :n],
                                             ACT.Copy).then_inc(x_hi, 1)
            prepare(0)
            prepare(1)
            split_weights_act(act, 0)

            def attend(a):
                g, i = a // NT, a % NT
                nk = P * len(key_tiles(g, i))
                act.wait_ge(at_m, a + 1)
                for h in range(H):
                    last = nc.scalar.activation(Sm[:, a % 2, h, :nk], Sm[:, a % 2, h, :nk], ACT.Exp,
                                                bias=negm[:, a, h:h + 1], accum_out=lsum[:, a, h:h + 1])
                last.then_inc(at_e, 1)

            def take_probabilities(a):
                act.wait_ge(at_tr, a_before[a] + 1)
                if a >= 2:
                    act.wait_ge(at_pv, a - 1)
                nc.scalar.activation(PT[:, a % 2, 0:4, :], TR[0][:, :].rearrange("p (k n) -> p k n", k=4),
                                     ACT.Copy).then_inc(at_pa, 1)

            def take_q_or_k(q):
                b, t = QK[q]
                g, n = b // 3, rows(t)
                act.wait_ge(z_tr, q + 1)
                src = TR[q % 2][:, 0:2 * P].rearrange("p (k n) -> p k n", k=2)[:, :, :n]
                dst = (qT, kT)[b % 3][:, :, P * t:P * t + n] if t < NT else qkS[:, g, b % 3]
                nc.scalar.activation(dst, src, ACT.Copy).then_inc(z_T, 1)

            for s in range(LAST):
                b, t = s // TILES, s % TILES
                g, kind, n = b // 3, b % 3, rows(t)
                if b == 0:
                    prepare(t + 2)
                if b < 10:
                    src = MM[s % 3][:n, 0:WB]
                    if b == 9:
                        dst = U[:, :, t] if t < NT else US[:, :].rearrange("p (g h) -> p g h", g=16)
                        src = src.rearrange("p (g h) -> p g h", g=16)
                    elif kind < 2:
                        q = qk_at[b, t]
                        if q >= 3:
                            act.wait_ge(z_n, q - 2)
                            act.wait_ge(z_sq, q - 2)
                        dst = zs[:n, q % 3]
                    else:
                        if t == 0 and g:
                            act.wait_ge(v_st, v_stores[g])
                            act.wait_ge(at_pv, NT * g)
                        dst = V[:n, t] if t < NT else vS[:n, g]
                    act.wait_ge(mm, s + 1)
                    nc.scalar.activation(dst, src, ACT.Copy).then_inc(ev, 1)
                    if s in take_at:
                        take_q_or_k(take_at[s])
                    if s in norm_at:
                        q = norm_at[s]
                        n_q = rows(QK[q][1])
                        act.wait_ge(z_ms, q + 1)
                        rsqrt_of_mean(zr[:n_q, 0, q], zr[:n_q, 1, q], E).then_inc(z_rt, 1)
                for a in due(s, 1):
                    attend(a)
                for a in due(s, 2):
                    take_probabilities(a)
                if t == 2 and b < 9:
                    split_weights_act(act, b + 1)

        @blk.vector
        def _(dve):
            link = linker(dve, c_dve)
            dve.wait_ge(tab, 16 * len(S["tables"]))
            link(nc.vector.tensor_scalar(qk_gain[:, 0], qk_gain[:, 0], E ** -0.5, None, ALU.mult))

            def split_weights(b):
                dve.wait_ge(w_hi, b + 1)
                nc.vector.tensor_tensor(WL[:, b % 2], wstage[:], WH[:, b % 2].bitcast(F32), ALU.subtract)\
                    .then_inc(w_lo, 1)

            def prepare(i):
                if i < TILES:
                    n = rows(i)
                    dve.wait_ge(x_rt, i + 1)
                    refine_rsqrt(nc, link, ssq[:n, 0, i:i + 1], ssq[:n, 1, i:i + 1], ssq[:n, 2, i:i + 1], D)
                    nc.vector.scalar_tensor_tensor(xin[:n, i % 2], xin[:n, i % 2], ssq[:n, 1, i:i + 1],
                                                   gain_bc[:n], ALU.mult, ALU.mult).then_inc(x_n, 1)
                if 0 < i <= TILES:
                    n = rows(i - 1)
                    for half in range(2):
                        dve.wait_ge(x_hi, 2 * (i - 1) + half + 1)
                        ks, ts = slice(4 * half, 4 * half + 4), slice(P * (i - 1), P * (i - 1) + n)
                        nc.vector.tensor_tensor(XL[:, ks, ts],
                                                TR[half][:, 0:4 * P].rearrange("p (k n) -> p k n", k=4)[:, :, :n],
                                                XH[:, ks, ts].bitcast(F32), ALU.subtract).then_inc(x_lo, 1)
            prepare(0)
            prepare(1)
            split_weights(0)

            def sum_squares(q):
                n = rows(QK[q][1])
                dve.wait_ge(z_sq, q + 1)
                nc.vector.tensor_reduce(zr[:n, 0, q], zsq[:n, q % 2].rearrange("p (h e) -> p h e", h=H),
                                        AX.X, ALU.add).then_inc(z_ms, 1)

            def norm_and_rotate(q):
                b, t = QK[q]
                g, kind, n = b // 3, b % 3, rows(t)
                z = zn[:n, q % 4].rearrange("p (h e) -> p h e", h=H)
                dve.wait_ge(z_s, q + 1)
                link(nc.vector.tensor_tensor(z, z, qk_gain[:n, kind].unsqueeze(1).to_broadcast([n, H, E]),
                                             ALU.mult))
                r = rope[:n, g * NT + t if t < NT else G * NT]
                cos, sin = r[:, 0:16], r[:, 16:32]
                nc.vector.tensor_tensor(zt[:n, 0], z[:, :, 0:16], cos.unsqueeze(1).to_broadcast([n, H, 16]),
                                        ALU.mult)
                nc.vector.tensor_tensor(zt[:n, 1, :, 0:8], z[:, :, 8:16],
                                        sin[:, 0:8].unsqueeze(1).to_broadcast([n, H, 8]), ALU.mult)
                link(nc.vector.tensor_tensor(zt[:n, 1, :, 8:16], z[:, :, 0:8],
                                             sin[:, 8:16].unsqueeze(1).to_broadcast([n, H, 8]), ALU.mult))
                nc.vector.tensor_tensor(z[:, :, 0:16], zt[:n, 0], zt[:n, 1], ALU.add).then_inc(z_n, 1)

            def mask_and_max(a):
                g, i = a // NT, a % NT
                nk = P * len(key_tiles(g, i))
                m = mask[:, 0:2 * P] if nk == 2 * P else (mask[:, P:2 * P] if g < 2 else mask[:, 2 * P:3 * P])
                dve.wait_ge(at_s, a + 1)
                if a >= 2:
                    dve.wait_ge(at_tr, a_before[a - 1])
                for j in range(2):
                    ins = nc.vector.tensor_tensor(
                        Sm[:, a % 2, j::2, :nk], SC[j][:, :].rearrange("p (h n) -> p h n", h=2)[:, :, :nk],
                        m.unsqueeze(1).to_broadcast([P, 2, nk]), ALU.add)
                    if j == 0:
                        link(ins)
                ins.then_inc(at_mask, 1)
                dve.wait_ge(at_mask, a + 1)
                nc.vector.tensor_reduce(negm[:, a], Sm[:, a % 2, :, :nk], AX.X, ALU.max, negate=True)\
                    .then_inc(at_m, 1)

            def take_probabilities(a):
                if ab[a] == 2:
                    dve.wait_ge(at_tr, a_before[a + 1])
                    if a >= 2:
                        dve.wait_ge(at_pv, a - 1)
                    nc.vector.tensor_copy(PT[:, a % 2, 4:8, :], TR[1][:, :].rearrange("p (k n) -> p k n", k=4))\
                        .then_inc(at_pb, 1)

            def take_output(a):
                dve.wait_ge(at_e, a + 1)
                link(nc.vector.reciprocal(rl[:, a], lsum[:, a]))
                dve.wait_ge(at_pv, a + 1)
                nc.vector.tensor_tensor(att[:, a].rearrange("p (h e) -> p h e", h=H),
                                        OB[:, 0:GW].rearrange("p (h e) -> p h e", h=H),
                                        per_head(rl[:, a], P), ALU.mult).then_inc(at_o, 1)

            for s in range(LAST):
                b, t = s // TILES, s % TILES
                if b == 0:
                    prepare(t + 2)
                if (b, t) in qk_at:
                    sum_squares(qk_at[b, t])
                if s in norm_at:
                    norm_and_rotate(norm_at[s])
                for a in due(s, 3):
                    take_output(a)
                for a in due(s, 0):
                    mask_and_max(a)
                for a in due(s, 2):
                    take_probabilities(a)
                if t == 2 and b < 9:
                    split_weights(b + 1)

        @blk.tensor
        def _(pe):
            last_reader = [None, None]

            def claim(j, sem_, value):
                if last_reader[j]:
                    pe.wait_ge(*last_reader[j])
                last_reader[j] = (sem_, value)

            pe.wait_ge(tab, 16 * len(S["tables"]))

            def transpose_x(i):
                n = rows(i)
                pe.wait_ge(x_n, i + 1)
                for half in range(2):
                    claim(half, x_lo, 2 * i + half + 1)
                    for k in range(4):
                        ks = 4 * half + k
                        ins = nc.tensor.transpose(TR[half][:, P * k:P * k + n],
                                                  xin[:n, i % 2, P * ks:P * ks + P], ident[:n, :n])
                    ins.then_inc(x_tr, 1)

            transpose_x(0)

            def transpose_qk(q):
                n = rows(QK[q][1])
                pe.wait_ge(z_n, q + 1)
                claim(q % 2, z_T, q + 1)
                for k in range(2):
                    ins = nc.tensor.transpose(TR[q % 2][:, P * k:P * k + n], zn[:n, q % 4, P * k:P * k + P],
                                              ident[:n, :n])
                ins.then_inc(z_tr, 1)

            def scores(a):
                g, i = a // NT, a % NT
                kt = key_tiles(g, i)
                nk = P * len(kt)
                if i == 0:
                    pe.wait_ge(z_T, 2 * TILES * (g + 1))
                if a:
                    pe.wait_ge(at_mask, a)
                for h in (0, 1, 2, 3):
                    e0 = E * (h % 2)
                    ins = nc.tensor.matmul(SC[h % 2][:, 2 * P * (h // 2):2 * P * (h // 2) + nk],
                                           qT[e0:e0 + E, h // 2, P * i:P * i + P],
                                           kT[e0:e0 + E, h // 2, P * kt[0]:P * kt[0] + nk],
                                           start=True, stop=True)
                ins.then_inc(at_s, 1)

            def transpose_p(a):
                nc_ = ab[a]
                pe.wait_ge(at_e, a + 1)
                for j in range(nc_):
                    claim(j, (at_pa, at_pb)[j], a + 1 if j == 0 else b_before[a + 1])
                    for x in range(4):
                        idx = 4 * j + x
                        h, ch = idx // nc_, idx % nc_
                        ins = nc.tensor.transpose(TR[j][:, P * x:P * x + P],
                                                  Sm[:, a % 2, h, P * ch:P * ch + P], ident[:, :])
                    ins.then_inc(at_tr, 1)

            def weigh(a):
                g, i = a // NT, a % NT
                kt = key_tiles(g, i)
                pe.wait_ge(ev, TILES * (3 * g + 2) + i + 1)
                pe.wait_ge(at_pa, a + 1)
                if b_before[a + 1]:
                    pe.wait_ge(at_pb, b_before[a + 1])
                if a:
                    pe.wait_ge(at_o, a)
                for h in range(H):
                    for ch, kt_ in enumerate(kt):
                        ins = nc.tensor.matmul(OB[:, E * h:E * h + E], PT[:, a % 2, h * len(kt) + ch],
                                               V[:, kt_, E * h:E * h + E],
                                               start=ch == 0, stop=ch == len(kt) - 1)
                ins.then_inc(at_pv, 1)

            for s in range(LAST):
                b, t = s // TILES, s % TILES
                g, n = b // 3, rows(t)
                if b < 10:
                    if t == 0:
                        pe.wait_ge(w_lo, b + 1)
                    if b == 0:
                        if t < NT:
                            transpose_x(t + 1)
                        pe.wait_ge(x_lo, 2 * (t + 1))
                    if s >= 3:
                        pe.wait_ge(ev, s - 2)
                    for k in range(KT):
                        xh, xl = columns(XH[:, k], g, t), columns(XL[:, k], g, t)
                        for j, (x, w) in enumerate(((xh, WH), (xh, WL), (xl, WH))):
                            ins = nc.tensor.matmul(MM[s % 3][:n, 0:WB], x, w[:, b % 2, k],
                                                   start=k == 0 and j == 0, stop=k == KT - 1 and j == 2)
                    ins.then_inc(mm, 1)
                    if s in take_at:
                        transpose_qk(take_at[s])
                for a in due(s, 3):
                    weigh(a)
                for a in due(s, 0):
                    scores(a)
                for a in due(s, 2):
                    transpose_p(a)


def block_ssm(nc, I, O, S):
    ident, gain_bc, U, US, ysb = S["ident"], S["gain_bc"], S["U"], S["US"], S["ysb"]
    bank = S["bank"]
    (BpR, BpI, ER, EI, XR, XI, HR, HI, ta, tb, BAR, BAI) = S["ssm_over"]
    CH, GH = 8, 8
    NC = SEQ // CH
    INV_2PI = 1.0 / (2 * math.pi)
    MAGIC = 1.5 * 2.0 ** 23
    PI_A, PI_B, PI_C = 6.28125, 0.0019350051879882812, 3.019916050e-7
    assert abs(PI_A + PI_B + PI_C - 2 * math.pi) < 1e-11

    with ExitStack() as c:
        def sb(name, shape, dt=F32):
            return c.enter_context(nc.sbuf_tensor(name, shape, dt))

        def sem(name):
            return nc.alloc_semaphore("s2_" + name)

        lamR, lamI, dt_ = sb("lamR", [P, GH]), sb("lamI", [P, GH]), sb("dt_", [P, GH])
        Bin = sb("Bin", [P, 2, GH, 16])
        Cin = sb("Cin", [16, 2, 16, 64])
        Dbc = sb("Dbc", [P, SW])
        bglu = sb("bglu", [P, SW])
        wglu = sb("wglu", [P, 2, SW])
        USp = sb("USp", [DB, 16, CH, 16])
        sm = sb("sm", [P, 24, GH])
        PR, PI = sb("PR", [P, 9, GH]), sb("PI", [P, 9, GH])
        QR, QI = sb("QR", [P, 8, GH]), sb("QI", [P, 8, GH])
        CI_ = sb("CI_", [P, 2, GH, 16])
        H0 = sb("H0", [P, 2, GH, DB])
        CAR, CAI, WBR, WBI, TZ, UT, Sin = S["ssm_mats"]
        MZ = S["MZ"]
        UTs = sb("UTs", [P, 16, DB])
        FR = sb("FR", [P, 2, GH, 9])
        hout = sb("hout", [9, 2, D])
        YS8 = sb("YS8", [DB, DT, SW])
        nrm = sb("nrm", [P, 3, TILES])

        ld_lam = sem("ld_lam")
        ld = sem("ld")
        ld_us = sem("ld_us")
        us_zero = sem("us_zero")
        p_exp = sem("p_exp")
        p_ang = sem("p_ang")
        p_sin = sem("p_sin")
        p_unit = sem("p_unit")
        tz_zero, tz_st = sem("tz_zero"), sem("tz_st")
        t_in = sem("t_in")
        t_c = sem("t_c")
        bb = sem("bb")
        t_b = sem("t_b")
        wb = sem("wb")
        tz_p, tz = sem("tz_p"), sem("tz")
        u_p, u_t = sem("u_p"), sem("u_t")
        us_p = sem("us_p")
        l_p = sem("l_p")
        l_r = sem("l_r")
        e_tab = sem("e_tab")
        ud = sem("ud")
        h_ok = sem("h_ok")
        f_p, f_s, f_o = sem("f_p"), sem("f_s"), sem("f_o")
        y_p = sem("y_p")
        ys_c, ys_d = sem("ys_c"), sem("ys_d")
        y_ok, z_ok = sem("y_ok"), sem("z_ok")
        zt_p, zt_c, gl_p, gl_s = sem("zt_p"), sem("zt_c"), sem("gl_p"), sem("gl_s")
        sg, so, so_q, so_m, so_r, so_n = (sem(x) for x in ("sg", "so", "so_q", "so_m", "so_r", "so_n"))
        c_dve, c_act, c_pool = sem("c_dve"), sem("c_act"), sem("c_pool")
        n_ld = 13
        zT = sb("zT", [P, 2, 2, P])
        glS = sb("glS", [TS, SW])

        def gate(j):
            return (XR if j < 4 else XI)[:, (2 * (j % 4)):(2 * (j % 4)) + 2, :].rearrange("p a b -> p (a b)") \
                if j < NT else glS[:]

        blk = c.enter_context(nc.Block())

        @blk.sync
        def _(sp):
            for gl_ in range(2):
                ps = slice(64 * gl_, 64 * gl_ + 64)
                for dst, name in ((lamR, "ssm_lam_re"), (lamI, "ssm_lam_im")):
                    sp.dma_start(dst[ps], I[name][0].rearrange("(g l) p -> l p g", l=2)[gl_],
                                 allow_slow_non_contiguous=True).then_inc(ld_lam, 16)
                sp.dma_start(dt_[ps], I["ssm_log_dt"][0].rearrange("(g l) -> l g", l=2)[gl_]
                             .partition_broadcast(64), allow_slow_non_contiguous=True).then_inc(ld_lam, 16)
            n = 0
            for gl_ in range(2):
                ps = slice(64 * gl_, 64 * gl_ + 64)
                for j, name in enumerate(("ssm_b_re", "ssm_b_im")):
                    sp.dma_start(Bin[ps, j], I[name][0].rearrange("(g l) p h -> l p g h", l=2)[gl_])\
                        .then_inc(ld, 16)
                n += 2
            for j, (cn, sn) in enumerate((("ssm_c_re", "state_ssm_re"), ("ssm_c_im", "state_ssm_im"))):
                sp.dma_start(Cin[:, j], I[cn][0].rearrange("g h p -> h g p")).then_inc(ld, 16)
                sp.dma_start(Sin[:, j], I[sn][0].rearrange("b g p -> b (g p)")).then_inc(ld, 16)
                n += 2
            sp.dma_start(Dbc[:], I["ssm_d"][0].rearrange("g h -> (g h)").partition_broadcast(P)).then_inc(ld, 16)
            sp.dma_start(bglu[:], I["b_glu"][0].partition_broadcast(P)).then_inc(ld, 16)
            sp.dma_start(wglu[:], I["w_glu"][0].rearrange("(k p) n -> p k n", p=P)).then_inc(ld, 16)
            sp.dma_start(gain_bc[:, 0:AW], I["attn_out_norm"][0].partition_broadcast(P)).then_inc(ld, 16)
            sp.dma_start(gain_bc[:, AW:D], I["ssm_out_norm"][0].partition_broadcast(P)).then_inc(ld, 16)
            n += 5
            assert n == n_ld
            sp.wait_ge(us_zero, 1)
            for i in range(DT):
                sp.dma_start(USp[:, :, 4 + i, :], US[i:TS:DT].rearrange("b (g h) -> b g h", g=16))\
                    .then_inc(ld_us, 16)
            sp.wait_ge(tz, 4)
            sp.wait_ge(tz_zero, 1)
            for j in range(CH):
                sp.dma_start(TZ[16 * j:16 * j + 16, :, 16 * j:P], MZ[:, :, 0:P - 16 * j]).then_inc(tz_st, 16)
            sp.wait_ge(ys_c, 2)
            for i in range(DT):
                sp.dma_start(ysb[i:TS:DT, NT], YS8[:, i]).then_inc(ys_d, 16)
            sp.wait_ge(f_s, 4)
            for j, name in enumerate(("ssm_re", "ssm_im")):
                sp.dma_start(O[name + "_s"][0].rearrange("b g p -> b (g p)"), hout[0:DB, j]).then_inc(f_o, 16)
                sp.dma_start(O[name + "_p"][0].rearrange("b g p -> b (g p)"), hout[DB:DB + 1, j]).then_inc(f_o, 16)
            sp.wait_ge(f_o, 64)

        @blk.gpsimd
        def _(pool):
            link = linker(pool, c_pool)
            nc.gpsimd.memset(USp[:], 0.0).then_inc(us_zero, 1)
            nc.gpsimd.memset(TZ[:], 0.0).then_inc(tz_zero, 1)
            pool.wait_ge(ld, 16 * n_ld)
            d = Dbc[:].rearrange("p (g h) -> p g h", g=16)
            for a in range(2):
                gs = slice(8 * a, 8 * a + 8)
                nc.gpsimd.tensor_tensor((ta, tb)[a][:].rearrange("p g (j h) -> p g j h", j=8), U[:, gs],
                                        d[:, gs].unsqueeze(2).to_broadcast([P, 8, CH, 16]), ALU.mult)\
                    .then_inc(ud, 1)
            link(nc.gpsimd.memset(ER[:, :, 0:1], 1.0))
            link(nc.gpsimd.memset(EI[:, :, 0:1], 0.0))
            t = XR[:, :, 0:64], XR[:, :, 64:128], XI[:, :, 0:64], XI[:, :, 64:128]

            def times(oR, oI, aR, aI, bR, bI, n):
                x = [y[:, :, 0:n] for y in t]
                nc.gpsimd.tensor_tensor(x[0], aR, bR, ALU.mult)
                nc.gpsimd.tensor_tensor(x[1], aI, bI, ALU.mult)
                nc.gpsimd.tensor_tensor(x[2], aR, bI, ALU.mult)
                link(nc.gpsimd.tensor_tensor(x[3], aI, bR, ALU.mult))
                nc.gpsimd.tensor_tensor(oR, x[0], x[1], ALU.subtract)
                link(nc.gpsimd.tensor_tensor(oI, x[2], x[3], ALU.add))

            pool.wait_ge(p_unit, 1)
            w = [sm[:, k].unsqueeze(2) for k in (16, 17)]
            v = [sm[:, k].unsqueeze(2) for k in (18, 19)]
            times(v[0], v[1], w[0], w[1], w[0], w[1], 1)
            times(w[0], w[1], v[0], v[1], v[0], v[1], 1)
            times(ER[:, :, 1:2], EI[:, :, 1:2], w[0], w[1], w[0], w[1], 1)
            m = 2
            while m < NC:
                half = ER[:, :, m // 2:m // 2 + 1], EI[:, :, m // 2:m // 2 + 1]
                times(v[0], v[1], *half, *half, 1)
                b = [x.to_broadcast([P, GH, m]) for x in v]
                times(ER[:, :, m:2 * m], EI[:, :, m:2 * m], ER[:, :, 0:m], EI[:, :, 0:m], *b, m)
                m *= 2
            pool.sem_inc(e_tab, 1)

        @blk.scalar
        def _(act):
            act.wait_ge(ld_lam, 16 * 6)
            link = linker(act, c_act)
            link(nc.scalar.activation(dt_[:], dt_[:], ACT.Exp))
            act.wait_ge(p_exp, 1)
            nc.scalar.activation(sm[:, 1], sm[:, 0], ACT.Exp).then_inc(p_exp, 1)
            act.wait_ge(p_ang, 1)
            nc.scalar.activation(sm[:, 16], sm[:, 5], ACT.Sin).then_inc(p_sin, 1)
            nc.scalar.activation(sm[:, 17], sm[:, 4], ACT.Sin).then_inc(p_sin, 1)
            act.wait_ge(t_in, 1)
            for j in range(2):
                nc.scalar.activation(CI_[:, j], bank[j][:, 0:P].rearrange("p (g h) -> p g h", g=GH), ACT.Copy)
            nc.scalar.activation(H0[:, :, :, :].rearrange("p a g b -> p (a g b)"), bank[2][:, 0:P], ACT.Copy)\
                .then_inc(t_c, 1)
            for q in range(4):
                act.wait_ge(u_p, q + 1)
                nc.scalar.activation(UT[:, 4 * q:4 * q + 4], bank[3 + q][:].rearrange("p (g n) -> p g n", g=4),
                                     ACT.Copy).then_inc(u_t, 1)
            act.wait_ge(us_p, 1)
            nc.scalar.activation(UTs[:], bank[7][:, 0:P].rearrange("p (g n) -> p g n", g=16), ACT.Copy)\
                .then_inc(u_t, 1)
            for q in range(4):
                act.wait_ge(t_b, q + 1)
                nc.scalar.activation((WBR, WBI)[q // 2][:, 4 * (q % 2):4 * (q % 2) + 4],
                                     bank[3 + q][:].rearrange("p (g n) -> p g n", g=4), ACT.Copy).then_inc(wb, 1)
            for q in range(4):
                act.wait_ge(tz_p, q + 1)
                gs = 8 * (q % 2) + q // 2
                nc.scalar.activation(MZ[:, gs:gs + 7:2],
                                     bank[(0, 1, 2, 7)[q]][0:16].rearrange("p (g n) -> p g n", g=4),
                                     ACT.Copy).then_inc(tz, 1)
            for q in range(4):
                act.wait_ge(f_p, q + 1)
                nc.scalar.activation(hout[:, q // 2, 512 * (q % 2):512 * (q % 2) + 512], bank[3 + q][0:9],
                                     ACT.Copy).then_inc(f_s, 1)
            for l in range(2):
                act.wait_ge(y_p, 5 + l)
                nc.scalar.activation(YS8[:].rearrange("b i (g l h) -> b l g i h", g=GH, l=2)[:, l],
                                     bank[5 + l][0:DB].rearrange("b (g i h) -> b g i h", g=GH, i=DT), ACT.Copy)\
                    .then_inc(ys_c, 1)
            act.wait_ge(y_ok, 5)
            nc.scalar.activation(ysb[:, 0:NT], ysb[:, 0:NT], ACT.Gelu_apprx_tanh)
            nc.scalar.activation(ysb[0:TS, NT], ysb[0:TS, NT], ACT.Gelu_apprx_tanh).then_inc(z_ok, 1)
            for j in range(TILES):
                n = rows(j)
                act.wait_ge(zt_p, j + 1)
                if j >= 2:
                    act.wait_ge(gl_p, j - 1)
                nc.scalar.activation(zT[:, j % 2, :, :n],
                                     bank[j % 2][:, 0:2 * P].rearrange("p (k n) -> p k n", k=2)[:, :, :n],
                                     ACT.Copy).then_inc(zt_c, 1)
            for j in range(TILES):
                act.wait_ge(gl_s, j + 1)
                nc.scalar.activation(gate(j)[:rows(j)], gate(j)[:rows(j)], ACT.Sigmoid).then_inc(sg, 1)
            for j in range(TILES):
                n = rows(j)
                act.wait_ge(so, j + 1)
                nc.scalar.activation(gate(j)[:n], ysb[:n, j], ACT.Square, accum_out=nrm[:n, 0, j:j + 1])\
                    .then_inc(so_q, 1)
            act.wait_ge(so_m, 2)
            nc.scalar.activation(nrm[:, 2, 0:NT], nrm[:, 1, 0:NT], ACT.Sqrt)
            nc.scalar.activation(nrm[0:TS, 2, NT:], nrm[0:TS, 1, NT:], ACT.Sqrt).then_inc(so_r, 1)

        @blk.vector
        def _(dve):
            link = linker(dve, c_dve)

            def tt(o, a, b, op=ALU.mult):
                link(nc.vector.tensor_tensor(o, a, b, op))

            def ts(o, a, s1, s2, op0, op1=None):
                link(nc.vector.tensor_scalar(o, a, s1, s2, op0, *([op1] if op1 else [])))

            x = [sm[:, k] for k in range(24)]
            dve.wait_ge(ld_lam, 16 * 6)
            dve.wait_ge(c_act, 1)
            nc.vector.tensor_tensor(x[0], lamR[:], dt_[:], ALU.mult).then_inc(p_exp, 1)
            tt(x[2], lamI[:], dt_[:])
            ts(x[3], x[2], INV_2PI, MAGIC, ALU.mult, ALU.add)
            ts(x[3], x[3], MAGIC, None, ALU.subtract)
            for part in (PI_A, PI_B, PI_C):
                link(nc.vector.scalar_tensor_tensor(x[2], x[3], -part, x[2], ALU.mult, ALU.add))
            lim = 3.1415925
            ts(x[4], x[2], lim, -lim, ALU.min, ALU.max)
            ts(x[5], x[4], -1.0, None, ALU.mult)
            tt(x[5], x[5], x[4], ALU.max)
            nc.vector.tensor_scalar(x[5], x[5], -1.0, math.pi / 2, ALU.mult, ALU.add).then_inc(p_ang, 1)
            dve.wait_ge(p_sin, 2)
            dve.wait_ge(p_exp, 2)
            link(nc.vector.memset(PR[:, 0], 1.0))
            link(nc.vector.memset(PI[:, 0], 0.0))
            tt(PR[:, 1], x[1], x[16])
            nc.vector.tensor_tensor(PI[:, 1], x[1], x[17], ALU.mult).then_inc(p_unit, 1)
            dve.wait_ge(p_unit, 1)

            def times(oR, oI, aR, aI, bR, bI, t):
                nc.vector.tensor_tensor(t[0], aR, bR, ALU.mult)
                nc.vector.tensor_tensor(t[1], aI, bI, ALU.mult)
                nc.vector.tensor_tensor(t[2], aR, bI, ALU.mult)
                tt(t[3], aI, bR)
                nc.vector.tensor_tensor(oR, t[0], t[1], ALU.subtract)
                tt(oI, t[2], t[3], ALU.add)

            for m in (1, 2, 4):
                tmp = [BAR[:, k, 0:8 * m].rearrange("p (m g) -> p m g", g=GH) for k in range(4)]
                b = [q[:, m:m + 1].to_broadcast([P, m, GH]) for q in (PR, PI)]
                times(PR[:, m + 1:2 * m + 1], PI[:, m + 1:2 * m + 1], PR[:, 1:m + 1], PI[:, 1:m + 1], *b, tmp)
            for m in range(8):
                nc.vector.tensor_copy(QR[:, m], PR[:, 7 - m])
                link(nc.vector.tensor_copy(QI[:, m], PI[:, 7 - m]))
            tt(x[6], x[1], x[1])
            tt(x[6], x[6], x[6])
            tt(x[6], x[6], x[6])
            ts(x[7], PR[:, 1], 1.0, None, ALU.subtract)
            tt(x[8], lamR[:], lamR[:])
            tt(x[9], lamI[:], lamI[:])
            tt(x[8], x[8], x[9], ALU.add)
            link(nc.vector.reciprocal(x[8], x[8]))
            tt(x[9], x[7], lamR[:])
            tt(x[10], PI[:, 1], lamI[:])
            tt(x[9], x[9], x[10], ALU.add)
            tt(x[9], x[9], x[8])
            tt(x[10], PI[:, 1], lamR[:])
            tt(x[11], x[7], lamI[:])
            tt(x[10], x[10], x[11], ALU.subtract)
            tt(x[10], x[10], x[8])
            cb = [x[k].unsqueeze(2).to_broadcast([P, GH, 16]) for k in (9, 10)]
            tmp = [BAR[:, k].rearrange("p (g h) -> p g h", g=GH) for k in range(4)]
            dve.wait_ge(ld, 16 * n_ld)
            bp = BpR[:], BpI[:]
            times(bp[0], bp[1], *cb, Bin[:, 0], Bin[:, 1], tmp)
            q = [y[:].rearrange("p j g -> p g j").unsqueeze(3).to_broadcast([P, GH, CH, 16]) for y in (QR, QI)]
            bx = [y.unsqueeze(2).to_broadcast([P, GH, CH, 16]) for y in bp]
            v4 = [y[:].rearrange("p g (j h) -> p g j h", j=CH) for y in (BAR, BAI, S["t1"])]
            tt(v4[0], q[0], bx[0])
            tt(v4[2], q[1], bx[1])
            tt(v4[0], v4[0], v4[2], ALU.subtract)
            tt(v4[1], q[0], bx[1])
            tt(v4[2], q[1], bx[0])
            nc.vector.tensor_tensor(v4[1], v4[1], v4[2], ALU.add).then_inc(bb, 1)
            dve.wait_ge(t_c, 1)
            pw = [y[:].rearrange("p d g -> p g d").unsqueeze(3).to_broadcast([P, GH, 9, 16]) for y in (PR, PI)]
            cx = [CI_[:, j].unsqueeze(2).to_broadcast([P, GH, 9, 16]) for j in range(2)]
            scratch = S["tH"][:, 0:GH * 9 * 16].rearrange("p (g d h) -> p g d h", g=GH, d=9)
            flat = [y[:].rearrange("p g d h -> p (g d h)") for y in (CAR, CAI)]
            tt(CAR[:], pw[0], cx[0])
            tt(scratch, pw[1], cx[1])
            tt(CAR[:], CAR[:], scratch, ALU.subtract)
            tt(CAI[:], pw[0], cx[1])
            tt(scratch, pw[1], cx[0])
            link(nc.vector.scalar_tensor_tensor(flat[1], flat[1], -1.0, S["tH"][:, 0:GH * 9 * 16],
                                                ALU.mult, ALU.subtract))
            dve.sem_inc(bb, 1)
            dve.wait_ge(e_tab, 1)
            dve.wait_ge(l_p, 5)
            for a in range(2):
                gs = slice(4 * a, 4 * a + 4)
                L = [bank[3 + 2 * j + a][:].rearrange("p (g n) -> p g n", g=4) for j in range(2)]
                nc.vector.tensor_tensor(XR[:, gs], ER[:, gs], L[0], ALU.mult)
                nc.vector.tensor_tensor(BAR[:, gs], EI[:, gs], L[1], ALU.mult)
                nc.vector.tensor_tensor(XI[:, gs], ER[:, gs], L[1], ALU.mult)
                tt(BAI[:, gs], EI[:, gs], L[0])
            nc.vector.tensor_tensor(XR[:], XR[:], BAR[:], ALU.add)
            tt(XI[:], XI[:], BAI[:], ALU.subtract)
            a4 = [y[:, 4].unsqueeze(2).to_broadcast([P, GH, DB]) for y in (PR, PI)]
            t2 = [BAR[:, k, 0:64].rearrange("p (g b) -> p g b", g=GH) for k in range(4)]
            times(FR[:, 0, :, 0:DB], FR[:, 1, :, 0:DB], *a4, H0[:, 0], H0[:, 1], t2)
            LS = bank[7][:, 256:256 + P].rearrange("p (a g b) -> p a g b", a=2, g=GH)
            link(nc.vector.tensor_tensor(FR[:, :, :, 0:DB], FR[:, :, :, 0:DB], LS, ALU.add))
            dve.sem_inc(l_r, 1)
            for gh in range(GH):
                r8 = x[6][:, gh:gh + 1].to_broadcast([P, NC])
                nc.vector.tensor_tensor_scan(BAR[:, gh], r8, XR[:, gh], 0.0, ALU.mult, ALU.add)
                nc.vector.tensor_tensor_scan(BAI[:, gh], r8, XI[:, gh], 0.0, ALU.mult, ALU.add)
            nc.vector.memset(HR[:, :, 0:1], 0.0)
            link(nc.vector.memset(HI[:, :, 0:1], 0.0))
            nc.vector.tensor_tensor(HR[:, :, 1:NC + 1], ER[:], BAR[:], ALU.mult)
            nc.vector.tensor_tensor(XR[:], EI[:], BAI[:], ALU.mult)
            nc.vector.tensor_tensor(HI[:, :, 1:NC + 1], ER[:], BAI[:], ALU.mult)
            tt(XI[:], EI[:], BAR[:])
            nc.vector.tensor_tensor(HR[:, :, 1:NC + 1], HR[:, :, 1:NC + 1], XR[:], ALU.subtract)
            tt(HI[:, :, 1:NC + 1], HI[:, :, 1:NC + 1], XI[:], ALU.add)
            nc.vector.tensor_copy(FR[:, 0, :, DB:DB + 1], HR[:, :, NC:NC + 1])
            nc.vector.tensor_copy(FR[:, 1, :, DB:DB + 1], HI[:, :, NC:NC + 1]).then_inc(h_ok, 1)
            dve.wait_ge(ud, 2)
            for q_ in range(4):
                l, a = q_ // 2, q_ % 2
                dve.wait_ge(y_p, q_ + 1)
                out = ysb[:, 0:NT].rearrange("p j (g l h) -> p l g j h", g=GH, l=2)[:, l, 4 * a:4 * a + 4]
                u_ = (ta, tb)[a][:].rearrange("p (g l) (j h) -> p l g j h", l=2, h=16)[:, l]
                nc.vector.tensor_tensor(out, bank[(0, 1, 2, 7)[q_]][:].rearrange("p (g j h) -> p g j h", g=4, j=CH),
                                        u_, ALU.add).then_inc(y_ok, 1)
            tt(glS[:], US[:], Dbc[0:TS])
            dve.wait_ge(ys_d, 16 * DT)
            nc.vector.tensor_tensor(ysb[0:TS, NT], ysb[0:TS, NT], glS[:], ALU.add).then_inc(y_ok, 1)
            for j in range(TILES):
                n = rows(j)
                dve.wait_ge(gl_p, j + 1)
                nc.vector.tensor_tensor(gate(j)[:n], bank[2 + j % 2][:n, 0:SW], bglu[:n], ALU.add)\
                    .then_inc(gl_s, 1)
            for j in range(TILES):
                n = rows(j)
                dve.wait_ge(sg, j + 1)
                nc.vector.tensor_tensor(ysb[:n, j], ysb[:n, j], gate(j)[:n], ALU.mult).then_inc(so, 1)
            dve.wait_ge(so_q, TILES)
            for n, js in ((P, slice(0, NT)), (TS, slice(NT, TILES))):
                nc.vector.tensor_scalar(nrm[:n, 1, js], nrm[:n, 0, js], 1.0 / SW, EPS, ALU.mult, ALU.add)\
                    .then_inc(so_m, 1)
            dve.wait_ge(so_r, 1)
            for n, js in ((P, slice(0, NT)), (TS, slice(NT, TILES))):
                link(nc.vector.reciprocal(nrm[:n, 1, js], nrm[:n, 2, js]))
            for j in range(TILES):
                n = rows(j)
                nc.vector.scalar_tensor_tensor(ysb[:n, j], ysb[:n, j], nrm[:n, 1, j:j + 1], gain_bc[:n, AW:D],
                                               ALU.mult, ALU.mult).then_inc(so_n, 1)

        @blk.tensor
        def _(pe):
            pe.wait_ge(ld, 16 * n_ld)
            for gh in range(GH):
                for j in range(2):
                    nc.tensor.transpose(bank[j][:, 16 * gh:16 * gh + 16],
                                        Cin[:, j, 2 * gh:2 * gh + 2].rearrange("h l p -> h (l p)"), ident[:16, :16])
                    ins = nc.tensor.transpose(bank[2][:, 64 * j + 8 * gh:64 * j + 8 * gh + 8],
                                              Sin[:, j, P * gh:P * gh + P], ident[:DB, :DB])
            ins.then_inc(t_in, 1)
            for q in range(4):
                for g in range(4):
                    ins = nc.tensor.transpose(bank[3 + q][:, P * g:P * g + P],
                                              U[:, 4 * q + g].rearrange("c j h -> c (j h)"), ident[:])
                ins.then_inc(u_p, 1)
            pe.wait_ge(ld_us, 16 * DT)
            for g in range(16):
                ins = nc.tensor.transpose(bank[7][:, 8 * g:8 * g + 8], USp[:, g].rearrange("b j h -> b (j h)"),
                                          ident[:DB, :DB])
            ins.then_inc(us_p, 1)
            pe.wait_ge(bb, 1)
            for q in range(4):
                pe.wait_ge(u_t, q + 1)
                for g in range(4):
                    ins = nc.tensor.transpose(bank[3 + q][:, P * g:P * g + P],
                                              (BAR, BAI)[q // 2][:, 4 * (q % 2) + g], ident[:])
                ins.then_inc(t_b, 1)
            pe.wait_ge(t_c, 1)
            pe.wait_ge(bb, 2)
            pe.wait_ge(u_t, 5)
            for q in range(4):
                l, ps = q // 2, slice(64 * (q // 2), 64 * (q // 2) + 64)
                for g in range(4):
                    gh = 4 * (q % 2) + g
                    for j, (bp, ca) in enumerate(((BpR, CAR), (BpI, CAI))):
                        ins = nc.tensor.matmul(bank[(0, 1, 2, 7)[q]][0:16, P * g:P * g + P], bp[ps, gh],
                                               ca[ps, gh, 0:CH].rearrange("p d h -> p (d h)"),
                                               start=j == 0, stop=j == 1)
                ins.then_inc(tz_p, 1)
            for q in range(4):
                pe.wait_ge(wb, q + 1)
            for q in range(4):
                W = (WBR, WBI)[q // 2]
                for g in range(4):
                    gh = 4 * (q % 2) + g
                    for l in range(2):
                        ins = nc.tensor.matmul(bank[3 + q][64 * l:64 * l + 64, P * g:P * g + P],
                                               W[:, gh, 64 * l:64 * l + 64], UT[:, 2 * gh + l],
                                               start=True, stop=True)
                ins.then_inc(l_p, 1)
            pe.wait_ge(tz, 4)
            for j, W in enumerate((WBR, WBI)):
                for gh in range(GH):
                    for l in range(2):
                        ins = nc.tensor.matmul(bank[7][64 * l:64 * l + 64, 256 + 64 * j + 8 * gh:264 + 64 * j + 8 * gh],
                                               W[:, gh, 64 * l:64 * l + 64], UTs[:, 2 * gh + l],
                                               start=True, stop=True)
            ins.then_inc(l_p, 1)
            pe.wait_ge(l_r, 1)
            pe.wait_ge(h_ok, 1)
            for q in range(4):
                for g in range(4):
                    ins = nc.tensor.transpose(bank[3 + q][0:9, P * g:P * g + P], FR[:, q // 2, 4 * (q % 2) + g],
                                              ident[:])
                ins.then_inc(f_p, 1)
            pe.wait_ge(tz_st, 16 * CH)
            for q in range(4):
                l, ps = q // 2, slice(64 * (q // 2), 64 * (q // 2) + 64)
                for g in range(4):
                    gh = 4 * (q % 2) + g
                    out = bank[(0, 1, 2, 7)[q]][:, P * g:P * g + P]
                    nc.tensor.matmul(out, UT[:, 2 * gh + l], TZ[:, 2 * gh + l], start=True, stop=False)
                    nc.tensor.matmul(out, HR[ps, gh, 0:NC], CAR[ps, gh, 1:9].rearrange("p d h -> p (d h)"),
                                     start=False, stop=False)
                    ins = nc.tensor.matmul(out, HI[ps, gh, 0:NC], CAI[ps, gh, 1:9].rearrange("p d h -> p (d h)"),
                                           start=False, stop=True)
                ins.then_inc(y_p, 1)
            pe.wait_ge(f_s, 4)
            for l in range(2):
                ps = slice(64 * l, 64 * l + 64)
                for gh in range(GH):
                    out = bank[5 + l][0:DB, 64 * gh:64 * gh + 64]
                    nc.tensor.matmul(out, UTs[:, 2 * gh + l], TZ[:, 2 * gh + l, 64:P], start=True, stop=False)
                    for j, ca in enumerate((CAR, CAI)):
                        ins = nc.tensor.matmul(out, H0[ps, j, gh], ca[ps, gh, 1:5].rearrange("p d h -> p (d h)"),
                                               start=False, stop=j == 1)
                ins.then_inc(y_p, 1)
            pe.wait_ge(z_ok, 1)

            def gate_product(j):
                n = rows(j)
                pe.wait_ge(zt_c, j + 1)
                if j >= 2:
                    pe.wait_ge(gl_s, j - 1)
                for k in range(2):
                    ins = nc.tensor.matmul(bank[2 + j % 2][:n, 0:SW], zT[:, j % 2, k, :n], wglu[:, k],
                                           start=k == 0, stop=k == 1)
                ins.then_inc(gl_p, 1)

            for j in range(TILES):
                n = rows(j)
                if j >= 2:
                    pe.wait_ge(zt_c, j - 1)
                for k in range(2):
                    ins = nc.tensor.transpose(bank[j % 2][:, P * k:P * k + n], ysb[:n, j, P * k:P * k + P],
                                              ident[:n, :n])
                ins.then_inc(zt_p, 1)
                if j:
                    gate_product(j - 1)
            gate_product(NT)


def stat_dmas(eng, stat, g, tile, g2, to_dram, sem_):
    vs = slice(8 * g2, 8 * g2 + 8) if g2 is not None else slice(0, 8 * G)
    if g == 0:
        parts = [(stat.rearrange("(t p) v -> p t v", p=P)[:, :, vs], slice(0, NT))]
    elif g == 1:
        parts = [(stat.rearrange("(h p r) v -> p h r v", h=2, r=4)[:, h, :, vs], slice(NT + h, 2 * NT, 2))
                 for h in range(2)]
    else:
        parts = [(stat.rearrange("(p t) v -> p t v", t=NT)[:, :, vs], slice(2 * NT, 3 * NT))]
    for dram, ts in parts:
        eng.dma_start(*((dram, tile[:, ts]) if to_dram else (tile[:, ts], dram))).then_inc(sem_, 16)
    return len(parts)


def block_sample(nc, I, O, S):
    ident, gain_bc, qkS, vS, attS, smask = (S[x] for x in ("ident", "gain_bc", "qkS", "vS", "attS", "smask"))
    bank, stat, stats, att, negm, lsum = (S[x] for x in ("bank", "stat", "al", "att", "negm", "lsum"))
    NTL = [1, 4, 2]
    TOK = [4, 1, 2]
    NKS = P + TS
    RING = S["ringS"].shape[1]
    loads = [(kv, g, b) for kv in range(2) for g in range(G) for b in range(DB)]
    units = [(g, b, i) for g in range(G) for b in range(DB) for i in range(NTL[g])]
    g_end = [8, 40, 56]

    with ExitStack() as c:
        def sb(name, shape, dt=F32):
            return c.enter_context(nc.sbuf_tensor(name, shape, dt))

        def sem(name):
            return nc.alloc_semaphore("s3_" + name)

        ring, kTc = S["ringS"], S["kTcS"]
        Qbd = sb("Qbd", [P, G, 2, 2, TS])
        sT = sb("sT", [P, G, 2, P])
        Pm = sb("Pm", [P, G, NKS])
        sc = sb("sc", [P, 8, G])
        PTc = sb("PTc", [P, G, P])
        PTn = sb("PTn", [TS, G, P])
        oS = sb("oS", [P, 2 * G, TS])
        nrm = sb("nrm_s", [TS, 4])
        sq = sb("sq", [P, NT, GW])
        st = sb("st", [P, G * NT, 2, H])
        junk = sb("junk_s", [TS, AW])

        r_ld = [sem(f"r_ld{i}") for i in range(RING)]
        m_ld = sem("m_ld")
        q_zero, q_bd = sem("q_zero"), sem("q_bd")
        k_p = sem("k_p")
        k_a, k_d = sem("k_a"), sem("k_d")
        s_p = sem("s_p")
        s_n = sem("s_n")
        s_c, s_b = sem("s_c"), sem("s_b")
        mx, ex, ln, al, ae, pr = (sem(x) for x in ("mx", "ex", "ln", "al", "ae", "pr"))
        pt_p, pt_c = sem("pt_p"), sem("pt_c")
        v_p = sem("v_p")
        o_c, o_p, o_s = sem("o_c"), sem("o_p"), sem("o_s")
        n_q, n_m, n_r = sem("n_q"), sem("n_m"), sem("n_r")
        c_dve = sem("c_dve")
        s_sq, s_rd = sem("sq"), sem("rd")
        lnp, st_ok, st_w, st_r = sem("lnp"), sem("st_ok"), sem("st_w"), sem("st_r")

        def ring_waits(eng, j):
            n = sum(2 if loads[x][1] == 2 else 1 for x in range(j % RING, j + 1, RING))
            eng.wait_ge(r_ld[j % RING], 16 * n)

        def load_of(kv, g, b):
            return (kv * G + g) * DB + b

        units_to = [sum(NTL[g] for _, g, _b in loads[:j]) for j in range(len(loads) + 1)]
        blk = c.enter_context(nc.Block())

        @blk.sync
        def _(sp):
            sp.dma_start(smask[:], I["c_smask"]).then_inc(m_ld, 16)
            for j, (kv, g, b) in enumerate(loads):
                if j >= RING:
                    k = units_to[j - RING + 1]
                    sp.wait_ge(k_p if k <= 56 else v_p, k if k <= 56 else k - 56)
                cache = I[f"cache_kv_dil{(1, 4, 16)[g]}"][0, b]
                if g == 0:
                    sp.dma_start(ring[:, j % RING, 0], cache[:, kv].rearrange("s h e -> s (h e)"))\
                        .then_inc(r_ld[j % RING], 16)
                elif g == 1:
                    sp.dma_start(ring[:, j % RING], cache.rearrange("(s r) v h e -> s r v (h e)", r=4)[:, :, kv])\
                        .then_inc(r_ld[j % RING], 16)
                else:
                    for r in range(2):
                        sp.dma_start(ring[64 * r:64 * r + 64, j % RING, 0:2],
                                     cache.rearrange("(s r) v h e -> s r v (h e)", r=16)[:, r:4:2, kv])\
                            .then_inc(r_ld[j % RING], 16)

        @blk.gpsimd
        def _(pool):
            for g in range(G):
                if g:
                    pool.wait_ge(s_rd, g)
                x = att[:, g * NT:g * NT + NT]
                nc.gpsimd.tensor_tensor(sq[:], x, x, ALU.mult).then_inc(s_sq, 1)
            pool.wait_ge(st_ok, 1)
            n = 0
            for g in range(G):
                n += stat_dmas(pool, stat, g, st[:].rearrange("p a x h -> p a (x h)"), g, True, st_w)
            pool.wait_ge(st_w, 16 * n)
            for g in range(G):
                stat_dmas(pool, stat, g, stats[:].rearrange("p a g x h -> p a (g x h)"), None, False, st_r)
            pool.wait_ge(st_r, 16 * n)

        @blk.scalar
        def _(act):
            nc.scalar.preload_act_table_set("natural_log_exp_and_others")
            nc.scalar.activation(st[:, :, 0], lsum[:], ACT.Ln).then_inc(lnp, 1)

            def take_keys(u):
                act.wait_ge(k_p, u + 1)
                if u >= 8:
                    act.wait_ge(s_p, u - 7)
                nc.scalar.activation(kTc[:, u % 8], bank[3 + u % 4][:, 0:2 * P].rearrange("p (k n) -> p k n", k=2),
                                     ACT.Copy).then_inc(k_a, 1)

            for u in range(0, 56, 2):
                take_keys(u)
            for g in range(G):
                act.wait_ge(s_p, g_end[g])
                act.wait_ge(s_n, g + 1)
                nc.scalar.activation(sT[:, g, 0], bank[g][:, 0:P], ACT.Copy)
                nc.scalar.activation(sT[0:TS, g, 1], bank[g][0:TS, P:2 * P], ACT.Copy).then_inc(s_c, 1)
            act.wait_ge(mx, 1)
            for g in range(G):
                ins = nc.scalar.activation(Pm[:, g], Pm[:, g], ACT.Exp, bias=sc[:, 0, g:g + 1],
                                           accum_out=sc[:, 1, g:g + 1])
            ins.then_inc(ex, 1)
            act.wait_ge(ex, 1)
            nc.scalar.activation(sc[:, 2], sc[:, 1], ACT.Ln).then_inc(ln, 1)
            act.wait_ge(al, 1)
            nc.scalar.activation(sc[:, 4], sc[:, 3], ACT.Exp, accum_out=sc[:, 5, 0:1]).then_inc(ae, 1)
            act.wait_ge(pt_p, 1)
            nc.scalar.activation(PTc[:], bank[6][:, 0:3 * P].rearrange("p (g n) -> p g n", g=G), ACT.Copy)
            nc.scalar.activation(PTn[:], bank[7][0:TS, 0:3 * P].rearrange("p (g n) -> p g n", g=G), ACT.Copy)\
                .then_inc(pt_c, 1)
            for g in range(G):
                act.wait_ge(v_p, g_end[g])
                for hp in range(2):
                    for hh in range(2):
                        ps = slice(64 * hh, 64 * hh + 64)
                        ins = nc.scalar.activation(oS[ps, 2 * g + hp], bank[2 * g + hp][ps, TS * hh:TS * hh + TS],
                                                   ACT.Copy)
                ins.then_inc(o_c, 1)
            act.wait_ge(o_p, 1)
            nc.scalar.activation(attS[:, 0:512], bank[6][0:TS, :], ACT.Copy)
            nc.scalar.activation(attS[:, 512:AW], bank[7][0:TS, 0:256], ACT.Copy).then_inc(o_s, 1)
            act.wait_ge(o_s, 1)
            nc.scalar.activation(junk[:], attS[:], ACT.Square, accum_out=nrm[:, 0:1]).then_inc(n_q, 1)
            act.wait_ge(n_m, 1)
            nc.scalar.activation(nrm[:, 2:3], nrm[:, 1:2], ACT.Sqrt).then_inc(n_r, 1)

        @blk.vector
        def _(dve):
            link = linker(dve, c_dve)
            nc.vector.memset(Qbd[:], 0.0).then_inc(q_zero, 1)
            dve.wait_ge(q_zero, 1)
            for hh in range(2):
                ps = slice(64 * hh, 64 * hh + 64)
                nc.vector.tensor_copy(Qbd[ps, :, :, hh], qkS[ps, :, 0]).then_inc(q_bd, 1)
            def sum_squares(g):
                dve.wait_ge(s_sq, g + 1)
                nc.vector.tensor_reduce(st[:, g * NT:g * NT + NT, 1], sq[:].rearrange("p t (h e) -> p t h e", h=H),
                                        AX.X, ALU.add).then_inc(s_rd, 1)

            for u in range(1, 56, 2):
                dve.wait_ge(k_p, u + 1)
                if u >= 8:
                    dve.wait_ge(s_p, u - 7)
                nc.vector.tensor_copy(kTc[:, u % 8], bank[3 + u % 4][:, 0:2 * P].rearrange("p (k n) -> p k n", k=2))\
                    .then_inc(k_d, 1)
                if u in (7, 15, 23):
                    sum_squares(u // 8)
            dve.wait_ge(lnp, 1)
            nc.vector.tensor_tensor(st[:, :, 0], st[:, :, 0], negm[:], ALU.subtract).then_inc(st_ok, 1)
            dve.wait_ge(s_b, 1)
            dve.wait_ge(m_ld, 16)
            link(nc.vector.tensor_tensor(Pm[:], bank[5][:, 0:G * NKS].rearrange("p (g n) -> p g n", g=G), smask[:],
                                         ALU.add))
            nc.vector.tensor_reduce(sc[:, 0], Pm[:], AX.X, ALU.max, negate=True).then_inc(mx, 1)
            dve.wait_ge(ln, 1)
            link(nc.vector.tensor_tensor(sc[:, 2], sc[:, 2], sc[:, 0], ALU.subtract))
            link(nc.vector.tensor_reduce(sc[:, 6, 0:1], sc[:, 2], AX.X, ALU.max))
            nc.vector.tensor_scalar(sc[:, 3], sc[:, 2], sc[:, 6, 0:1], None, ALU.subtract).then_inc(al, 1)
            dve.wait_ge(ae, 1)
            link(nc.vector.tensor_scalar(sc[:, 6], sc[:, 1], sc[:, 5, 0:1], None, ALU.mult))
            link(nc.vector.reciprocal(sc[:, 7], sc[:, 6]))
            link(nc.vector.tensor_tensor(sc[:, 7], sc[:, 7], sc[:, 4], ALU.mult))
            nc.vector.tensor_tensor(Pm[:], Pm[:], sc[:, 7].unsqueeze(2).to_broadcast([P, G, NKS]), ALU.mult)\
                .then_inc(pr, 1)
            dve.wait_ge(n_q, 1)
            nc.vector.tensor_scalar(nrm[:, 1:2], nrm[:, 0:1], 1.0 / AW, EPS, ALU.mult, ALU.add).then_inc(n_m, 1)
            dve.wait_ge(n_r, 1)
            link(nc.vector.reciprocal(nrm[:, 3:4], nrm[:, 2:3]))
            link(nc.vector.scalar_tensor_tensor(attS[:], attS[:], nrm[:, 3:4], gain_bc[0:TS, 0:AW],
                                                ALU.mult, ALU.mult))

        @blk.tensor
        def _(pe):
            def tokens(g, b, i):
                return slice(DT * b + TOK[g] * i, DT * b + TOK[g] * (i + 1))

            def transpose_keys(u):
                g, b, i = units[u]
                j = load_of(0, g, b)
                if i == 0:
                    ring_waits(pe, j)
                if u >= 4:
                    pe.wait_ge(k_d if u % 2 else k_a, u // 2 - 1)
                for k in range(2):
                    ins = nc.tensor.transpose(bank[3 + u % 4][:, P * k:P * k + P],
                                              ring[:, j % RING, i, P * k:P * k + P], ident[:])
                ins.then_inc(k_p, 1)

            def scores(u):
                g, b, i = units[u]
                pe.wait_ge(k_d if u % 2 else k_a, u // 2 + 1)
                for hp in range(2):
                    out = bank[g][:, 64 * hp:64 * hp + 64].rearrange("p (h n) -> p h n", h=2)[:, :, tokens(g, b, i)]
                    ins = nc.tensor.matmul(out, kTc[:, u % 8, hp], Qbd[:, g, hp, :, tokens(g, b, i)],
                                           start=True, stop=True)
                ins.then_inc(s_p, 1)

            pe.wait_ge(q_bd, 2)
            for g in range(G):
                for hp in range(2):
                    ins = nc.tensor.matmul(bank[g][0:TS, P + 64 * hp:P + 64 * hp + 64], qkS[:, g, 1, hp],
                                           Qbd[:, g, hp].rearrange("p h n -> p (h n)"), start=True, stop=True)
                ins.then_inc(s_n, 1)
            for u in range(59):
                if u < 56:
                    transpose_keys(u)
                if u >= 3:
                    scores(u - 3)
            for g in range(G):
                pe.wait_ge(s_c, g + 1)
                nc.tensor.transpose(bank[5][:, NKS * g:NKS * g + P], sT[:, g, 0], ident[:])
                ins = nc.tensor.transpose(bank[5][:, NKS * g + P:NKS * g + NKS], sT[0:TS, g, 1], ident[:TS, :TS])
            ins.then_inc(s_b, 1)
            pe.wait_ge(pr, 1)
            for g in range(G):
                nc.tensor.transpose(bank[6][:, P * g:P * g + P], Pm[:, g, 0:P], ident[:])
                ins = nc.tensor.transpose(bank[7][0:TS, P * g:P * g + P], Pm[:, g, P:NKS], ident[:])
            ins.then_inc(pt_p, 1)
            pe.wait_ge(pt_c, 1)
            for g in range(G):
                for hp in range(2):
                    nc.tensor.matmul(bank[2 * g + hp][:, 0:64], vS[:, g, P * hp:P * hp + P],
                                     PTn[:, g, 64 * hp:64 * hp + 64], start=True, stop=False)
                for b in range(DB):
                    j = load_of(1, g, b)
                    ring_waits(pe, j)
                    for i in range(NTL[g]):
                        for hp in range(2):
                            out = bank[2 * g + hp][:, 0:64].rearrange("p (h n) -> p h n", h=2)
                            w = PTc[:, g, 64 * hp:64 * hp + 64].rearrange("p (h n) -> p h n", h=2)
                            ins = nc.tensor.matmul(out[:, :, tokens(g, b, i)], ring[:, j % RING, i, P * hp:P * hp + P],
                                                   w[:, :, tokens(g, b, i)], start=False,
                                                   stop=b == DB - 1 and i == NTL[g] - 1)
                        ins.then_inc(v_p, 1)
            pe.wait_ge(o_c, 3)
            for k in range(2 * G):
                ins = nc.tensor.transpose(bank[6 + k // 4][0:TS, P * (k % 4):P * (k % 4) + P], oS[:, k], ident[:])
            ins.then_inc(o_p, 1)


def block_mix(nc, I, O, S):
    ident, gain_bc, att, attS, ysb = (S[x] for x in ("ident", "gain_bc", "att", "attS", "ysb"))
    XH, XL, bank = S["XH"], S["XL"], S["bank"]
    A = G * NT
    with ExitStack() as c:
        def sb(name, shape, dt=F32):
            return c.enter_context(nc.sbuf_tensor(name, shape, dt))

        def sem(name):
            return nc.alloc_semaphore("s4_" + name)

        al = S["al"]
        w1 = sb("w1", [P, A, G, H])
        w2 = sb("w2", [P, A, H])
        w3 = sb("w3", [P, A])
        sub, ex, ms, rt = sem("sub"), sem("ex"), sem("ms"), sem("rt")
        a_s = sem("a_s")
        a_n, t_p, t_h, t_l = sem("a_n"), sem("t_p"), sem("t_h"), sem("t_l")
        c_dve = sem("c_dve")
        blk = c.enter_context(nc.Block())
        work = [("y", t) for t in range(TILES)] + [("s", g) for g in range(G)] + [("a", a) for a in range(A)]

        def place(X, w):
            kind, i = w
            if kind == "y":
                return columns(X[:, 6:8], 3, i), rows(i)
            if kind == "s":
                return X[:, 2 * i:2 * i + 2, SEQ:T], TS
            g, t = i // NT, i % NT
            return columns(X[:, 2 * g:2 * g + 2], g, t), P

        @blk.sync
        def _(sp):
            sp.dma_start(S["wstage"][:], weight_block(I, "w_out", 0)).then_inc(S["w_next"], 16)

        @blk.gpsimd
        def _(pool):
            for a in range(A):
                g = a // NT
                pool.wait_ge(a_s, a + 1)
                nc.gpsimd.tensor_tensor(att[:, a], att[:, a], gain_bc[:, GW * g:GW * g + GW], ALU.mult)\
                    .then_inc(a_n, 1)

        @blk.scalar
        def _(act):
            act.wait_ge(sub, 1)
            nc.scalar.activation(w1[:], w1[:], ACT.Exp).then_inc(ex, 1)

            def take(k):
                act.wait_ge(t_p, k + 1)
                dst, n = place(XH, work[k])
                src = bank[k % 4][:, 0:2 * P].rearrange("p (k n) -> p k n", k=2)[:, :, :n]
                nc.scalar.activation(dst, src, ACT.Copy).then_inc(t_h, 1)

            for k in range(len(work)):
                if k == TILES + G:
                    act.wait_ge(ms, 1)
                    nc.scalar.activation(w3[:], w3[:], ACT.Sqrt).then_inc(rt, 1)
                take(k)

        @blk.vector
        def _(dve):
            link = linker(dve, c_dve)
            def take(k):
                dve.wait_ge(t_h, k + 1)
                dst, n = place(XL, work[k])
                hi, _ = place(XH, work[k])
                src = bank[k % 4][:, 0:2 * P].rearrange("p (k n) -> p k n", k=2)[:, :, :n]
                nc.vector.tensor_tensor(dst, src, hi.bitcast(F32), ALU.subtract).then_inc(t_l, 1)

            lse = [al[:, :, g, 0] for g in range(G)]
            link(nc.vector.tensor_tensor(w2[:], lse[0], lse[1], ALU.max))
            link(nc.vector.tensor_tensor(w2[:], w2[:], lse[2], ALU.max))
            for g in range(G):
                ins = nc.vector.tensor_tensor(w1[:, :, g], lse[g], w2[:], ALU.subtract)
            ins.then_inc(sub, 1)
            dve.wait_ge(ex, 1)
            link(nc.vector.tensor_tensor(w2[:], w1[:, :, 0], w1[:, :, 1], ALU.add))
            link(nc.vector.tensor_tensor(w2[:], w2[:], w1[:, :, 2], ALU.add))
            link(nc.vector.reciprocal(w2[:], w2[:]))
            for g in range(G):
                link(nc.vector.tensor_tensor(w1[:, :, g], w1[:, :, g], w2[:], ALU.mult))
            for g in range(G):
                link(nc.vector.tensor_tensor(al[:, :, g, 0], w1[:, :, g], w1[:, :, g], ALU.mult))
                link(nc.vector.tensor_tensor(al[:, :, g, 1], al[:, :, g, 1], al[:, :, g, 0], ALU.mult))
            link(nc.vector.tensor_tensor(w2[:], al[:, :, 0, 1], al[:, :, 1, 1], ALU.add))
            link(nc.vector.tensor_tensor(w2[:], w2[:], al[:, :, 2, 1], ALU.add))
            link(nc.vector.tensor_reduce(w3[:], w2[:], AX.X, ALU.add))
            nc.vector.tensor_scalar(w3[:], w3[:], 1.0 / AW, EPS, ALU.mult, ALU.add).then_inc(ms, 1)
            for k in range(TILES + G):
                take(k)
            dve.wait_ge(rt, 1)
            link(nc.vector.reciprocal(w3[:], w3[:]))
            for g in range(G):
                ts = slice(g * NT, g * NT + NT)
                link(nc.vector.tensor_tensor(w2[:, ts], w1[:, ts, g], w3[:, ts].unsqueeze(2).to_broadcast([P, NT, H]),
                                             ALU.mult))

            def scale(a):
                x = att[:, a].rearrange("p (h e) -> p h e", h=H)
                nc.vector.tensor_tensor(x, x, per_head(w2[:, a], P), ALU.mult).then_inc(a_s, 1)

            for a in range(A + 3):
                if a < A:
                    scale(a)
                if a >= 3:
                    take(TILES + G + a - 3)

        @blk.tensor
        def _(pe):
            for k, (kind, i) in enumerate(work):
                if k >= 4:
                    pe.wait_ge(t_l, k - 3)
                if kind == "a":
                    pe.wait_ge(a_n, i + 1)
                n = place(XH, work[k])[1]
                if kind == "y":
                    src = ysb[:n, i]
                else:
                    src = attS[:, GW * i:GW * i + GW] if kind == "s" else att[:, i]
                for x in range(2):
                    ins = nc.tensor.transpose(bank[k % 4][:, P * x:P * x + n], src[:, P * x:P * x + P],
                                              ident[:n, :n])
                ins.then_inc(t_p, 1)


def block_dense(nc, I, O, S, stages):
    XH, XL, WH, WL, wstage = S["XH"], S["XL"], S["WH"], S["WL"], S["wstage"]
    ident, gain_bc, hres = S["ident"], S["gain_bc"], S["hres"]
    bank = S["bank"]
    MM, TR, KT_ = bank[0:3], bank[3:5], bank[5:7]
    weights = {"m": "w_xkv", "o": "w_out", "q": "w_xq", "x": "w_xo"}
    NM = 2
    has_m = "m" in stages
    if has_m:
        blocks = [x for j in range(4) for x in (("o", j), ("m", 2 * j), ("m", 2 * j + 1))]
        blocks += [("q", j) for j in range(4)]
    else:
        blocks = [("x", j) for j in range(4)]
    steps = [(st, j, t, b) for b, (st, j) in enumerate(blocks) for t in range(NM if st == "m" else TILES)]
    normed = [s for s, (st, j, t, b) in enumerate(steps) if st == "q" or st == "m" and j < 4]
    norm_at = {s: n for n, s in enumerate(normed)}
    block_end = [max(s for s, x in enumerate(steps) if x[3] == b) + 1 for b in range(len(blocks))]
    by_dve = [sum(steps[r][0] != "m" or steps[r][1] < 4 for r in range(s)) for s in range(len(steps) + 1)]
    by_act = [s - by_dve[s] for s in range(len(steps) + 1)]
    preps = ([("m", i) for i in range(NM)] if has_m else []) + [("h", i) for i in range(TILES)]
    h0 = len(preps) - TILES
    prep_start, prep_end = {}, {}
    if has_m:
        for p in range(NM):
            prep_start[2 * p + 5], prep_end[2 * p + 6] = p, [p]
    for s, (st, j, t, b) in enumerate(steps):
        if st in "ox" and j == 3:
            prep_start[s] = h0 + t
            prep_end[s] = ([h0 + t - 1] if t else []) + ([h0 + t] if t == NT else [])

    def rows_of(kind, i):
        return P if kind == "m" else rows(i)

    with ExitStack() as c:
        def sb(name, shape, dt=F32):
            return c.enter_context(nc.sbuf_tensor(name + stages, shape, dt))

        def sem(name):
            return nc.alloc_semaphore(f"d{stages}_" + name)

        xn = sb("xn", [P, 2, D])
        kn = sb("kn", [P, 2, WB])
        ssq = sb("ssq", [P, 3, len(preps)])
        zr = sb("zr", [P, 3, max(1, len(normed))])

        ld = sem("ld")
        x_ld = [sem(f"x_ld{t}") for t in range(TILES if "o" in stages else 0)]
        w_ld, w_hi, w_lo = sem("w_ld"), sem("w_hi"), sem("w_lo")
        p_rt, p_n = sem("p_rt"), sem("p_n")
        p_tr, p_hi, p_lo = sem("p_tr"), sem("p_hi"), sem("p_lo")
        mm = sem("mm")
        ev_a, ev_d = sem("ev_a"), sem("ev_d")
        n_r, n_t, n_T = sem("n_r"), sem("n_t"), sem("n_T")
        k_st, v_st = [sem("k_st0"), sem("k_st1")], sem("v_st")
        c_act, c_dve = sem("c_act"), sem("c_dve")
        n_x = 2 if "o" in stages else 0
        n_ld = 16 * len(S["loads" + stages])

        def split_before(s):
            st, j, t, b = steps[s]
            return b + 1 < len(blocks) and t == (0 if st == "m" else 1)

        blk = c.enter_context(nc.Block())

        @blk.sync
        def _(sp):
            def load_x(t):
                src = I["x_prompt"][0, P * t:P * t + P] if t < NT else I["x_sample"].rearrange("b t d -> (b t) d")
                sp.dma_start(hres[:rows(t), t], src).then_inc(x_ld[t], 16)

            def load_weights(b):
                sp.wait_ge(w_lo, b)
                st, j = blocks[b]
                sp.dma_start(wstage[:], weight_block(I, weights[st], j)).then_inc(w_ld, 16)

            def load_rest():
                for dst, src in S["loads" + stages]:
                    sp.dma_start(dst, src).then_inc(ld, 16)

            if n_x:
                for t in range(TILES):
                    load_x(t)
                    if t == 2:
                        load_weights(1)
                    if t == 5:
                        load_rest()
            else:
                load_rest()
                load_weights(1)
            for b in range(2, len(blocks)):
                load_weights(b)
            if stages == "x":
                sp.wait_ge(w_lo, len(blocks))
                for g in range(2):
                    sp.dma_start(wstage[:, :, P * g:P * g + P], up_weights(I)[:, :, g, 0:P]).then_inc(S["w_next"], 16)

        @blk.gpsimd
        def _(pool):
            if has_m:
                kv = O["mem_kv_p"][0, 0]
                ks, vs = [0, 0], 0
                for s, (st, j, t, b) in enumerate(steps):
                    if st != "m":
                        continue
                    dst = kv[P * t:P * t + P, j // 4, j % 4]
                    if j < 4:
                        n = norm_at[s]
                        pool.wait_ge(ev_d, by_dve[s + 1])
                        pool.dma_start(dst, kn[:, n % 2]).then_inc(k_st[n % 2], 16)
                        ks[n % 2] += 16
                    else:
                        vs += 1
                        pool.wait_ge(ev_a, vs)
                        pool.dma_start(dst, S["Vm"][:, t, WB * (j - 4):WB * (j - 3)]).then_inc(v_st, 16)
                pool.wait_ge(k_st[0], ks[0])
                pool.wait_ge(k_st[1], ks[1])
                pool.wait_ge(v_st, 16 * vs)

        def source(kind, i):
            return S["mraw"][:, i] if kind == "m" else hres[:rows(i), i]

        def parts(kind, i, hi):
            if kind == "m":
                return (S["MH"] if hi else S["ML"])[:, :, P * i:P * i + P]
            return (XH if hi else XL)[:, :, P * i:P * i + rows(i)]

        @blk.scalar
        def _(act):
            done = 0

            def rsqrt_of_mean(sums, out, width):
                nonlocal done
                done += 1
                act.wait_ge(c_act, done)
                nc.scalar.activation(out, sums, ACT.Ln, scale=1.0 / width, bias=S["eps"][:sums.shape[0]])\
                    .then_inc(c_act, 1)
                done += 1
                act.wait_ge(c_act, done)
                return nc.scalar.activation(out, out, ACT.Exp, scale=-0.5)

            nc.scalar.preload_act_table_set("natural_log_exp_and_others")

            def split_weights(b):
                if b:
                    act.wait_ge(w_ld, 16 * b)
                else:
                    act.wait_ge(S["w_next"], 16 if has_m else 32)
                if b >= 2:
                    act.wait_ge(mm, block_end[b - 2])
                nc.scalar.activation(WH[:, b % 2], wstage[:], ACT.Copy).then_inc(w_hi, 1)

            def prep_square(p):
                kind, i = preps[p]
                n = rows_of(kind, i)
                if p >= 2:
                    act.wait_ge(p_tr, 2 * (p - 1))
                nc.scalar.activation(xn[:n, p % 2], source(kind, i), ACT.Square, accum_out=ssq[:n, 0, p:p + 1])\
                    .then_inc(c_act, 1)
                rsqrt_of_mean(ssq[:n, 0, p:p + 1], ssq[:n, 1, p:p + 1], D).then_inc(p_rt, 1)

            def prep_high(p):
                kind, i = preps[p]
                n = rows_of(kind, i)
                for half in range(2):
                    act.wait_ge(p_tr, 2 * p + half + 1)
                    nc.scalar.activation(parts(kind, i, True)[:, 4 * half:4 * half + 4],
                                         TR[half][:].rearrange("p (k n) -> p k n", k=4)[:, :, :n],
                                         ACT.Copy).then_inc(p_hi, 1)

            def take_transposed(n):
                st, j, t, b = steps[normed[n]]
                act.wait_ge(n_t, n + 1)
                src = KT_[n % 2][:, 0:2 * P].rearrange("p (k n) -> p k n", k=2)
                if st == "m":
                    dst = S["kmT"][:, 2 * j:2 * j + 2, P * t:P * t + P]
                else:
                    src = src[:, :, :rows(t)]
                    dst = S["qxT"][:, 2 * j:2 * j + 2, P * t:P * t + rows(t)]
                nc.scalar.activation(dst, src, ACT.Copy).then_inc(n_T, 1)

            split_weights(0)
            for s, (st, j, t, b) in enumerate(steps):
                if split_before(s):
                    split_weights(b + 1)
                if s == 5:
                    act.wait_ge(ld, n_ld)
                n_rows = P if st == "m" else rows(t)
                if st == "m" and j >= 4:
                    act.wait_ge(mm, s + 1)
                    nc.scalar.activation(S["Vm"][:, t, WB * (j - 4):WB * (j - 3)], MM[s % 3][:, 0:WB], ACT.Copy)\
                        .then_inc(ev_a, 1)
                elif s in norm_at:
                    n = norm_at[s]
                    act.wait_ge(mm, s + 1)
                    if n >= 2:
                        act.wait_ge(n_t, n - 1)
                        if has_m:
                            act.wait_ge(k_st[n % 2], 16 * min(NM * 2, n // 2))
                    nc.scalar.activation(kn[:n_rows, n % 2], MM[s % 3][:n_rows, 0:WB], ACT.Square,
                                         accum_out=zr[:n_rows, 0, n:n + 1]).then_inc(c_act, 1)
                    rsqrt_of_mean(zr[:n_rows, 0, n:n + 1], zr[:n_rows, 1, n:n + 1], WB).then_inc(n_r, 1)
                    if n:
                        take_transposed(n - 1)
                if s in prep_start:
                    act.wait_ge(ev_d, by_dve[s + 1])
                    prep_square(prep_start[s])
                for p in prep_end.get(s, []):
                    prep_high(p)
            if normed:
                take_transposed(len(normed) - 1)

        @blk.vector
        def _(dve):
            link = linker(dve, c_dve)

            def split_weights(b):
                dve.wait_ge(w_hi, b + 1)
                nc.vector.tensor_tensor(WL[:, b % 2], wstage[:], WH[:, b % 2].bitcast(F32), ALU.subtract)\
                    .then_inc(w_lo, 1)

            def prep_norm(p):
                kind, i = preps[p]
                n = rows_of(kind, i)
                dve.wait_ge(p_rt, p + 1)
                refine_rsqrt(nc, link, ssq[:n, 0, p:p + 1], ssq[:n, 1, p:p + 1], ssq[:n, 2, p:p + 1], D)
                gain = S["gain_m"] if kind == "m" else gain_bc
                nc.vector.scalar_tensor_tensor(xn[:n, p % 2], source(kind, i), ssq[:n, 1, p:p + 1],
                                               gain[:n], ALU.mult, ALU.mult).then_inc(p_n, 1)

            def prep_low(p):
                kind, i = preps[p]
                n = rows_of(kind, i)
                for half in range(2):
                    dve.wait_ge(p_hi, 2 * p + half + 1)
                    ks = slice(4 * half, 4 * half + 4)
                    nc.vector.tensor_tensor(parts(kind, i, False)[:, ks],
                                            TR[half][:].rearrange("p (k n) -> p k n", k=4)[:, :, :n],
                                            parts(kind, i, True)[:, ks].bitcast(F32), ALU.subtract).then_inc(p_lo, 1)

            split_weights(0)
            for s, (st, j, t, b) in enumerate(steps):
                if split_before(s):
                    split_weights(b + 1)
                if s == 5:
                    dve.wait_ge(ld, n_ld)
                n_rows = P if st == "m" else rows(t)
                src = MM[s % 3][:n_rows, 0:WB]
                if st in "ox":
                    if b == 0 and n_x:
                        dve.wait_ge(x_ld[t], 16)
                    dve.wait_ge(mm, s + 1)
                    dst = hres[:n_rows, t, WB * j:WB * j + WB]
                    nc.vector.tensor_tensor(dst, dst, src, ALU.add).then_inc(ev_d, 1)
                elif s in norm_at:
                    n = norm_at[s]
                    dve.wait_ge(n_r, n + 1)
                    refine_rsqrt(nc, link, *(zr[:n_rows, x, n:n + 1] for x in range(3)), WB)
                    gain = S["gain_xk"] if st == "m" else S["gain_xq"]
                    nc.vector.scalar_tensor_tensor(kn[:n_rows, n % 2], src, zr[:n_rows, 1, n:n + 1], gain[:n_rows],
                                                   ALU.mult, ALU.mult).then_inc(ev_d, 1)
                if s in prep_start:
                    prep_norm(prep_start[s])
                for p in prep_end.get(s, []):
                    prep_low(p)

        @blk.tensor
        def _(pe):
            def prep_transpose(p):
                kind, i = preps[p]
                n = rows_of(kind, i)
                pe.wait_ge(p_n, p + 1)
                for half in range(2):
                    if p:
                        pe.wait_ge(p_lo, 2 * p + half - 1)
                    for k in range(4):
                        ks = 4 * half + k
                        ins = nc.tensor.transpose(TR[half][:, P * k:P * k + n], xn[:n, p % 2, P * ks:P * ks + P],
                                                  ident[:n, :n])
                    ins.then_inc(p_tr, 1)

            def transpose_normed(n):
                st, j, t, b = steps[normed[n]]
                r = P if st == "m" else rows(t)
                pe.wait_ge(ev_d, by_dve[normed[n] + 1])
                if n >= 2:
                    pe.wait_ge(n_T, n - 1)
                for k in range(2):
                    ins = nc.tensor.transpose(KT_[n % 2][:, P * k:P * k + r], kn[:r, n % 2, P * k:P * k + P],
                                              ident[:r, :r])
                ins.then_inc(n_t, 1)

            for s, (st, j, t, b) in enumerate(steps):
                r = P if st == "m" else rows(t)
                if s == 0 or steps[s - 1][3] != b:
                    pe.wait_ge(w_lo, b + 1)
                if s >= 3:
                    q = steps[s - 3]
                    if q[0] == "m" and q[1] >= 4:
                        pe.wait_ge(ev_a, by_act[s - 2])
                    else:
                        pe.wait_ge(ev_d, by_dve[s - 2])
                if st == "m":
                    xh, xl = S["MH"], S["ML"]
                    pe.wait_ge(p_lo, 2 * (t + 1))
                else:
                    xh, xl = XH, XL
                    if st == "q" and j == 0:
                        pe.wait_ge(p_lo, 2 * (h0 + t + 1))
                cols = slice(P * t, P * t + r)
                for k in range(KT):
                    for i, (x, w) in enumerate(((xh, WH), (xh, WL), (xl, WH))):
                        ins = nc.tensor.matmul(MM[s % 3][:r, 0:WB], x[:, k, cols], w[:, b % 2, k],
                                               start=k == 0 and i == 0, stop=k == KT - 1 and i == 2)
                ins.then_inc(mm, 1)
                if s in norm_at and norm_at[s] >= 1:
                    transpose_normed(norm_at[s] - 1)
                for p in prep_end.get(s, []):
                    prep_transpose(p)
            if normed:
                transpose_normed(len(normed) - 1)


def block_cross(nc, I, O, S):
    ident, qxT, kmT, Vm, XH, XL = (S[x] for x in ("ident", "qxT", "kmT", "Vm", "XH", "XL"))
    ring, kTx, sTx, Pm, PT = S["cross_over"]
    bank = S["bank"]
    SC, TRB, OO, TRK = bank[0:2], bank[2:4], bank[4:6], bank[6]
    NU = NT * X + 1
    RING = 6
    loads = [(kv, b, h) for kv in range(2) for b in range(DB) for h in range(X)]
    NL = DB * X
    with ExitStack() as c:
        def sem(name):
            return nc.alloc_semaphore("s6_" + name)

        st = c.enter_context(nc.sbuf_tensor("st6", [P, 4, NU], F32))
        r_ld = [sem(f"r_ld{i}") for i in range(RING)]
        sp_, mx, ex, pn = sem("s"), sem("mx"), sem("ex"), sem("pn")
        tp, tc, op, oh, ol = sem("tp"), sem("tc"), sem("op"), sem("oh"), sem("ol")
        kp, kc, ks, vp = sem("kp"), sem("kc"), sem("ks"), sem("vp")
        sc_ = sem("sc")
        c_dve = sem("c_dve")
        blk = c.enter_context(nc.Block())

        def out_place(Xt, u):
            if u == NU - 1:
                return Xt[:, :, SEQ:T]
            i, h = u // X, u % X
            return Xt[:, 2 * h:2 * h + 2, P * i:P * i + P]

        def out_bank(u):
            if u == NU - 1:
                return OO[u % 2][:, 0:8 * TS].rearrange("p (k n) -> p k n", k=8)
            return OO[u % 2][:, 0:2 * P].rearrange("p (k n) -> p k n", k=2)

        @blk.sync
        def _(sp):
            sp.dma_start(S["wstage"][:], weight_block(I, "w_xo", 0)).then_inc(S["w_next"], 16)
            for j, (kv, b, h) in enumerate(loads):
                if j >= RING:
                    k = j - RING + 1
                    sp.wait_ge(kp if k <= NL else vp, k if k <= NL else k - NL)
                sp.dma_start(ring[:, j % RING], I["cache_mem_kv"][0, b, :, kv, h].rearrange("(m p) e -> p m e", p=P))\
                    .then_inc(r_ld[j % RING], 16)

        @blk.scalar
        def _(act):
            def take_output(u):
                act.wait_ge(op, u + 1)
                nc.scalar.activation(out_place(XH, u), out_bank(u), ACT.Copy).then_inc(oh, 1)

            def exps(u):
                act.wait_ge(mx, u + 1)
                if u >= 2:
                    act.wait_ge(tp, u - 1)
                nc.scalar.activation(Pm[:, u % 2], SC[u % 2][:, 0:2 * P], ACT.Exp, bias=st[:, 1, u:u + 1],
                                     scale=1.0 / 16, accum_out=st[:, 2, u:u + 1]).then_inc(ex, 1)

            def take_keys(j):
                act.wait_ge(kp, j + 1)
                if j >= 2:
                    act.wait_ge(ks, j - 1)
                nc.scalar.activation(kTx[:, j % 2], TRK[:].rearrange("p (e m) -> p e m", e=2), ACT.Copy)\
                    .then_inc(kc, 1)

            for u in range(NU - 1):
                take_keys(u)
                exps(u)
                if u >= 2:
                    take_output(u - 2)
            act.wait_ge(ks, NL)
            nc.scalar.activation(sTx[:], bank[7][:, 0:2 * P], ACT.Copy).then_inc(sc_, 1)
            exps(NU - 1)
            for u in range(NU - 3, NU):
                take_output(u)

        @blk.vector
        def _(dve):
            link = linker(dve, c_dve)

            def maxima(u):
                dve.wait_ge(sp_, u + 1)
                link(nc.vector.tensor_reduce(st[:, 0, u:u + 1], SC[u % 2][:, 0:2 * P], AX.X, ALU.max, negate=True))
                nc.vector.tensor_scalar(st[:, 1, u:u + 1], st[:, 0, u:u + 1], 1.0 / 16, None, ALU.mult).then_inc(mx, 1)

            def normalise(u):
                dve.wait_ge(ex, u + 1)
                link(nc.vector.reciprocal(st[:, 3, u:u + 1], st[:, 2, u:u + 1]))
                nc.vector.tensor_scalar(Pm[:, u % 2], Pm[:, u % 2], st[:, 3, u:u + 1], None, ALU.mult).then_inc(pn, 1)

            def take_probabilities(u):
                dve.wait_ge(tp, u + 1)
                if u >= 2:
                    dve.wait_ge(op, u - 1)
                nc.vector.tensor_copy(PT[:, u % 2], TRB[u % 2][:, 0:2 * P].rearrange("p (m n) -> p m n", m=2))\
                    .then_inc(tc, 1)

            def take_output(u):
                dve.wait_ge(oh, u + 1)
                nc.vector.tensor_tensor(out_place(XL, u), out_bank(u), out_place(XH, u).bitcast(F32), ALU.subtract)\
                    .then_inc(ol, 1)

            for u in range(NU + 2):
                if u < NU:
                    maxima(u)
                    normalise(u)
                if 0 < u <= NU:
                    take_probabilities(u - 1)
                if u >= 2:
                    take_output(u - 2)

        @blk.tensor
        def _(pe):
            def scores(u):
                i, h = u // X, u % X
                if u >= 2:
                    pe.wait_ge(ex, u - 1)
                for e in range(2):
                    ins = nc.tensor.matmul(SC[u % 2][:, 0:2 * P], qxT[:, 2 * h + e, P * i:P * i + P],
                                           kmT[:, 2 * h + e], start=e == 0, stop=e == 1)
                ins.then_inc(sp_, 1)

            def transpose_p(u):
                pe.wait_ge(pn, u + 1)
                if u >= 2:
                    pe.wait_ge(tc, u - 1)
                for m in range(2):
                    ins = nc.tensor.transpose(TRB[u % 2][:, P * m:P * m + P], Pm[:, u % 2, P * m:P * m + P], ident[:])
                ins.then_inc(tp, 1)

            def weigh(u):
                i, h = u // X, u % X
                pe.wait_ge(tc, u + 1)
                if u >= 2:
                    pe.wait_ge(ol, u - 1)
                for e in range(2):
                    for m in range(2):
                        col = 2 * P * h + P * e
                        ins = nc.tensor.matmul(OO[u % 2][:, P * e:P * e + P], Vm[:, m, col:col + P],
                                               PT[:, u % 2, m], start=m == 0, stop=m == 1)
                ins.then_inc(op, 1)

            def keys(j):
                pe.wait_ge(r_ld[j % RING], 16 * (j // RING + 1))
                if j:
                    pe.wait_ge(kc, j)
                for e in range(2):
                    for m in range(2):
                        ins = nc.tensor.transpose(TRK[:, 2 * P * e + P * m:2 * P * e + P * m + P],
                                                  ring[:, j % RING, m, P * e:P * e + P], ident[:])
                ins.then_inc(kp, 1)

            def sample_scores(j):
                _, b, h = loads[j]
                pe.wait_ge(kc, j + 1)
                for m in range(2):
                    col = P * m + TS * h + DT * b
                    for e in range(2):
                        ins = nc.tensor.matmul(bank[7][:, col:col + DT], kTx[:, j % 2, e, P * m:P * m + P],
                                               qxT[:, 2 * h + e, SEQ + DT * b:SEQ + DT * b + DT],
                                               start=e == 0, stop=e == 1)
                ins.then_inc(ks, 1)

            for u in range(NU - 1):
                keys(u)
                scores(u)
                if u:
                    sample_scores(u - 1)
                    transpose_p(u - 1)
                if u >= 2:
                    weigh(u - 2)
            sample_scores(NL - 1)
            u = NU - 1
            pe.wait_ge(sc_, 1)
            pe.wait_ge(ex, u - 1)
            for m in range(2):
                ins = nc.tensor.transpose(SC[u % 2][:, P * m:P * m + P], sTx[:, P * m:P * m + P], ident[:])
            ins.then_inc(sp_, 1)
            transpose_p(u - 1)
            weigh(u - 2)
            weigh(u - 1)
            transpose_p(u)
            pe.wait_ge(tc, u + 1)
            pe.wait_ge(ol, u - 1)
            for j in range(NL):
                _, b, h = loads[NL + j]
                pe.wait_ge(r_ld[(NL + j) % RING], 16 * ((NL + j) // RING + 1))
                for e in range(2):
                    col = TS * (2 * h + e) + DT * b
                    for m in range(2):
                        ins = nc.tensor.matmul(OO[u % 2][:, col:col + DT], ring[:, (NL + j) % RING, m, P * e:P * e + P],
                                               PT[:, u % 2, m, TS * h + DT * b:TS * h + DT * b + DT],
                                               start=m == 0, stop=m == 1)
                ins.then_inc(vp if j < NL - 1 else op, 1)


def up_weights(I):
    return I["w_up"][0].rearrange("(k p) (g c) -> p k g c", p=P, g=2)


def block_ffn(nc, I, O, S):
    XH, XL, WH, WL, wstage, ident, hres = (S[x] for x in ("XH", "XL", "WH", "WL", "wstage", "ident", "hres"))
    bank = S["bank"]
    NF = F // P
    TURNS = NF // 2
    W = 2 + SEQ + DB * (2 + DT)
    NW = W - 2
    CH = T // 3
    UNITS = 2 * TILES
    with ExitStack() as c:
        def sb(name, shape, dt=F32):
            return c.enter_context(nc.sbuf_tensor(name, shape, dt))

        def sem(name):
            return nc.alloc_semaphore("s8_" + name)

        AH, AL = sb("AH", [P, 2, T], F32R), sb("AL", [P, 2, T], F32R)
        DH, DL = sb("DH", [P, 2, D], F32R), sb("DL", [P, 2, D], F32R)
        dstage = sb("dstage", [P, D])
        UB = sb("UB", [P, 2, W])
        cv = sb("cv", [P, 2, NW])
        par = sb("par", [P, 2, P])
        pT = sb("pT", [P, 2, 2, 20])
        last = sb("last", [P, 2, 18])
        co = sb("co", [18, 2, P])

        up_ld, dn_ld, par_ld = sem("up_ld"), sem("dn_ld"), sem("par_ld")
        w_hi, w_lo, d_hi, d_lo = sem("w_hi"), sem("w_lo"), sem("d_hi"), sem("d_lo")
        par_p, par_c = sem("par_p"), sem("par_c")
        cached = sem("cached")
        up = sem("up")
        ub = sem("ub")
        tap = sem("tap")
        conv = sem("conv")
        silu, prod = sem("silu"), sem("prod")
        a_hi, a_lo = sem("a_hi"), sem("a_lo")
        lst, co_p, co_c, co_st = sem("lst"), sem("co_p"), sem("co_c"), sem("co_st")
        dn = sem("dn")
        y = sem("y")
        y_st = sem("y_st")
        zero = sem("zero")
        c_dve = sem("c_dve")
        blk = c.enter_context(nc.Block())
        tail = cv[:, 0, SEQ:].rearrange("p (b n) -> p b n", b=DB)[:, :, 2:]
        w_up = up_weights(I)
        seqs = UB[:, :, 2 + SEQ:W].rearrange("p g (b n) -> p g b n", b=DB)

        @blk.sync
        def _(sp):
            def tile(f, first):
                cols = bass.ds(f * P, P)
                if not first:
                    sp.wait_ge(w_lo, f)
                    for g in range(2):
                        sp.dma_start(wstage[:, :, P * g:P * g + P], w_up[:, :, g, cols]).then_inc(up_ld, 16)
                if first:
                    sp.wait_ge(zero, 1)
                else:
                    sp.wait_ge(par_p, f)
                for lo, hi, src in ((0, 16, I["state_ffn_conv"][0].rearrange("b r (g c) -> (b r) g c", g=2)),
                                    (16, 19, I["conv_w"][0].rearrange("r (g c) -> r g c", g=2)),
                                    (19, 20, I["conv_b"].rearrange("r (g c) -> r g c", g=2))):
                    sp.dma_start(par[lo:hi], src[:, :, cols]).then_inc(par_ld, 16)

            tile(0, True)
            with sp.Fori(1, NF) as f:
                tile(f, False)
            for t in range(TILES):
                sp.wait_ge(y, (TURNS - 1) * UNITS + 2 * t + 2)
                dst = O["yp"][0, P * t:P * t + P] if t < NT else O["ys"].rearrange("b t d -> (b t) d")
                sp.dma_start(dst, hres[:rows(t), t]).then_inc(y_st, 16)
            sp.wait_ge(y_st, 16 * TILES)

        @blk.gpsimd
        def _(pool):
            def store(f, value):
                cols = bass.ds(f * P, P)
                pool.wait_ge(co_c, value)
                pool.dma_start(O["conv_p"][0, 0].rearrange("r (g c) -> r g c", g=2)[:, :, cols], co[0:2])\
                    .then_inc(co_st, 16)
                pool.dma_start(O["conv_s"][0].rearrange("b r (g c) -> (b r) g c", g=2)[:, :, cols], co[2:18])\
                    .then_inc(co_st, 16)

            def load_down(f):
                pool.dma_start(dstage[:], I["w_down"][0, bass.ds(f * P, P)]).then_inc(dn_ld, 16)

            load_down(0)
            with pool.Fori(1, NF) as f:
                pool.wait_ge(d_lo, f)
                load_down(f)
                store(f - 1, f)
            store(NF - 1, NF)
            pool.wait_ge(co_st, 32 * NF)

        @blk.scalar
        def _(act):
            def split_up(f, slot, free, first=False):
                if first:
                    act.wait_ge(S["w_next"], 64)
                else:
                    act.wait_ge(up_ld, f * 32)
                if free:
                    act.wait_ge(up, f * 2 - 2)
                nc.scalar.activation(WH[:, slot], wstage[:], ACT.Copy).then_inc(w_hi, 1)

            def split_down(f, slot, free):
                act.wait_ge(dn_ld, f * 16 + 16)
                if free is not None:
                    act.wait_ge(dn, free)
                nc.scalar.activation(DH[:, slot], dstage[:], ACT.Copy).then_inc(d_hi, 1)

            def tile(f, slot, first, free, more):
                if more:
                    split_up(f + 1, 1 - slot, not first)
                act.wait_ge(cached, f + 1)
                for g in range(2):
                    act.wait_ge(up, f * 2 + g + 1)
                    for j in range(2):
                        nc.scalar.activation(UB[:, g, 2 + CH * j:2 + CH * j + CH], bank[3 * g + j][:, 0:CH], ACT.Copy)
                    n = SEQ - 2 * CH
                    nc.scalar.activation(UB[:, g, 2 + 2 * CH:2 + SEQ], bank[3 * g + 2][:, 0:n], ACT.Copy)
                    nc.scalar.activation(seqs[:, g, :, 2:],
                                         bank[3 * g + 2][:, n:CH].rearrange("p (b n) -> p b n", b=DB), ACT.Copy)\
                        .then_inc(ub, 1)
                    act.wait_ge(ub, f * 2 + g + 1)
                    if not first and g == 0:
                        act.wait_ge(a_lo, f)
                    nc.scalar.activation(cv[:, g], UB[:, g, 2:], ACT.Identity, scale=pT[:, slot, g, 18:19],
                                         bias=pT[:, slot, g, 19:20]).then_inc(tap, 1)
                act.wait_ge(conv, f * 2 + 1)
                nc.scalar.activation(cv[:, 0], cv[:, 0], ACT.Silu).then_inc(silu, 1)
                act.wait_ge(prod, f + 1)
                if free is not None:
                    act.wait_ge(dn, free)
                nc.scalar.activation(AH[:, slot, 0:SEQ], cv[:, 0, 0:SEQ], ACT.Copy)
                nc.scalar.activation(AH[:, slot, SEQ:T].rearrange("p (b n) -> p b n", b=DB),
                                     tail, ACT.Copy).then_inc(a_hi, 1)
                split_down(f, slot, free)

            split_up(0, 0, False, True)

            def turn(n, first, more):
                tile(n * 2, 0, first, None if first else n * UNITS, True)
                tile(n * 2 + 1, 1, False, None if first else n * UNITS, more)

            turn(0, True, True)
            with act.Fori(1, TURNS - 1) as n:
                turn(n, False, True)
            turn(TURNS - 1, False, False)

        @blk.vector
        def _(dve):
            nc.vector.memset(par[:], 0.0)
            nc.vector.memset(UB[:, :, 0:2], 0.0).then_inc(zero, 1)
            dve.wait_ge(zero, 1)

            def split_up(f, slot):
                dve.wait_ge(w_hi, f + 1)
                nc.vector.tensor_tensor(WL[:, slot], wstage[:], WH[:, slot].bitcast(F32), ALU.subtract)\
                    .then_inc(w_lo, 1)

            def params(f, slot):
                dve.wait_ge(par_p, f + 1)
                ps = bank[6][:, 0:2 * P].rearrange("p (g n) -> p g n", g=2)[:, :, 0:20]
                nc.vector.tensor_copy(pT[:, slot], ps).then_inc(par_c, 1)

            def cached_columns(f, slot, first):
                if not first:
                    dve.wait_ge(lst, f)
                    dve.wait_ge(conv, f * 2)
                dve.wait_ge(par_c, f + 1)
                for g in range(2):
                    ins = nc.vector.tensor_copy(seqs[:, g, :, 0:2],
                                                pT[:, slot, g, 0:16].rearrange("p (b n) -> p b n", b=DB))
                ins.then_inc(cached, 1)

            def convolve(f, slot, g, part):
                if part == 0:
                    dve.wait_ge(tap, f * 2 + g + 1)
                    nc.vector.scalar_tensor_tensor(cv[:, g], UB[:, g, 1:W - 1], pT[:, slot, g, 17:18], cv[:, g],
                                                   ALU.mult, ALU.add).then_inc(c_dve, 1)
                else:
                    dve.wait_ge(c_dve, f * 2 + g + 1)
                    nc.vector.scalar_tensor_tensor(cv[:, g], UB[:, g, 0:W - 2], pT[:, slot, g, 16:17], cv[:, g],
                                                   ALU.mult, ALU.add).then_inc(conv, 1)

            def columns(f, first):
                if not first:
                    dve.wait_ge(co_p, f)
                nc.vector.tensor_copy(last[:, :, 0:2], UB[:, :, SEQ:SEQ + 2])
                for g in range(2):
                    ins = nc.vector.tensor_copy(last[:, g, 2:18].rearrange("p (b n) -> p b n", b=DB),
                                                seqs[:, g, :, DT:DT + 2])
                ins.then_inc(lst, 1)

            def product(f):
                dve.wait_ge(silu, f + 1)
                dve.wait_ge(conv, f * 2 + 2)
                nc.vector.tensor_tensor(cv[:, 0], cv[:, 0], cv[:, 1], ALU.mult).then_inc(prod, 1)

            def low(f, slot):
                dve.wait_ge(a_hi, f + 1)
                nc.vector.tensor_tensor(AL[:, slot, 0:SEQ], cv[:, 0, 0:SEQ], AH[:, slot, 0:SEQ].bitcast(F32),
                                        ALU.subtract)
                nc.vector.tensor_tensor(AL[:, slot, SEQ:T].rearrange("p (b n) -> p b n", b=DB), tail,
                                        AH[:, slot, SEQ:T].rearrange("p (b n) -> p b n", b=DB).bitcast(F32),
                                        ALU.subtract).then_inc(a_lo, 1)
                dve.wait_ge(d_hi, f + 1)
                nc.vector.tensor_tensor(DL[:, slot], dstage[:], DH[:, slot].bitcast(F32), ALU.subtract)\
                    .then_inc(d_lo, 1)

            def columns_out(f, first):
                dve.wait_ge(co_p, f + 1)
                if not first:
                    dve.wait_ge(co_st, f * 32)
                nc.vector.tensor_copy(co[:], bank[7][0:18, 0:2 * P].rearrange("p (g n) -> p g n", g=2))\
                    .then_inc(co_c, 1)

            def add_down(n, lo, hi):
                for u in range(lo, hi):
                    t, half = u // 2, u % 2
                    dst = hres[:rows(t), t, 512 * half:512 * half + 512]
                    dve.wait_ge(dn, n * UNITS + u + 1)
                    nc.vector.tensor_tensor(dst, dst, bank[6 + u % 2][:rows(t)], ALU.add).then_inc(y, 1)

            split_up(0, 0)
            params(0, 0)
            cached_columns(0, 0, True)

            def turn(n, first, more):
                f = n * 2

                def adds(lo, hi):
                    if not first:
                        add_down(n - 1, lo, hi)

                split_up(f + 1, 1)
                if not first:
                    columns_out(f - 1, False)
                params(f + 1, 1)
                convolve(f, 0, 0, 0)
                convolve(f, 0, 0, 1)
                adds(0, 4)
                convolve(f, 0, 1, 0)
                adds(4, 6)
                convolve(f, 0, 1, 1)
                adds(6, 8)
                columns(f, first)
                cached_columns(f + 1, 1, False)
                adds(8, 11)
                product(f)
                adds(11, UNITS)
                low(f, 0)
                if more:
                    split_up(f + 2, 0)
                columns_out(f, first)
                if more:
                    params(f + 2, 0)
                for g in range(2):
                    convolve(f + 1, 1, g, 0)
                    convolve(f + 1, 1, g, 1)
                columns(f + 1, False)
                if more:
                    cached_columns(f + 2, 0, False)
                product(f + 1)
                low(f + 1, 1)

            turn(0, True, True)
            with dve.Fori(1, TURNS - 1) as n:
                turn(n, False, True)
            turn(TURNS - 1, False, False)
            columns_out(NF - 1, False)
            add_down(TURNS - 1, 0, UNITS)

        @blk.tensor
        def _(pe):
            def params(f):
                pe.wait_ge(par_ld, f * 48 + 48)
                for g in range(2):
                    ins = nc.tensor.transpose(bank[6][:, P * g:P * g + P], par[:, g], ident[:])
                ins.then_inc(par_p, 1)

            def up_project(f, slot, first, between):
                pe.wait_ge(w_lo, f + 1)
                for g in range(2):
                    if not first:
                        pe.wait_ge(ub, f * 2 + g - 1)
                    for j in range(3):
                        for k in range(KT):
                            for i, (w, x) in enumerate(((WH, XH), (WH, XL), (WL, XH))):
                                ins = nc.tensor.matmul(bank[3 * g + j][:, 0:CH], w[:, slot, k, P * g:P * g + P],
                                                       x[:, k, CH * j:CH * j + CH],
                                                       start=k == 0 and i == 0, stop=k == KT - 1 and i == 2)
                    ins.then_inc(up, 1)
                    if g == 0:
                        between()

            def columns_out(f):
                pe.wait_ge(lst, f + 1)
                for g in range(2):
                    ins = nc.tensor.transpose(bank[7][0:18, P * g:P * g + P], last[:, g], ident[:])
                ins.then_inc(co_p, 1)

            def down_project(n):
                pe.wait_ge(a_lo, n * 2 + 2)
                pe.wait_ge(d_lo, n * 2 + 2)
                pe.wait_ge(co_c, n * 2 + 2)
                for u in range(UNITS):
                    t, half = u // 2, u % 2
                    r = rows(t)
                    if u >= 2:
                        pe.wait_ge(y, n * UNITS + u - 1)
                    for s in range(2):
                        for i, (x, w) in enumerate(((AH, DH), (AH, DL), (AL, DH))):
                            ins = nc.tensor.matmul(bank[6 + u % 2][:r, :], x[:, s, P * t:P * t + r],
                                                   w[:, s, 512 * half:512 * half + 512],
                                                   start=s == 0 and i == 0, stop=s == 1 and i == 2)
                    ins.then_inc(dn, 1)

            def turn(n, first, more):
                f = n * 2

                def before_down():
                    if not first:
                        pe.wait_ge(co_c, f - 1)
                        columns_out(f - 1)
                    pe.wait_ge(par_c, f + 1)
                    params(f + 1)

                def after_down():
                    if not first:
                        pe.wait_ge(y, n * UNITS)
                    columns_out(f)
                    if more:
                        pe.wait_ge(par_c, f + 2)
                        params(f + 2)

                up_project(f, 0, first, before_down)
                if not first:
                    pe.wait_ge(par_c, f + 2)
                    down_project(n - 1)
                up_project(f + 1, 1, False, after_down)

            params(0)
            turn(0, True, True)
            with pe.Fori(1, TURNS - 1) as n:
                turn(n, False, True)
            turn(TURNS - 1, False, False)
            pe.wait_ge(co_c, NF - 1)
            columns_out(NF - 1)
            down_project(TURNS - 1)


def weight_block(I, name, j):
    return I[name][0, :, WB * j:WB * j + WB].rearrange("(k p) n -> p k n", p=P)


def cache_rows(O, g, t, kv):
    if t == NT:
        return [(O[f"kv_s{g}"][0, :, :, kv].rearrange("b t h e -> (b t) (h e)"), 0, TS)]
    dst = O[f"kv_p{g}"][0, 0, :, kv].rearrange("n h e -> n (h e)")
    if g == 0:
        return [(dst, 0, P)] if t == NT - 1 else []
    if g == 1:
        return [(dst[t // 2:t // 2 + 4 * (P - 1) + 1:4], 0, P)] if t % 2 else []
    return [(dst[t:t + 8 * (P - 1) + 1:8], 0, P)]


OUTS = [("yp", (1, SEQ, D)), ("ys", (DB, DT, D)),
        ("kv_p0", (1, 1, 128, 2, H, E)), ("kv_p1", (1, 1, 512, 2, H, E)), ("kv_p2", (1, 1, 1024, 2, H, E)),
        ("ssm_re_p", (1, 1, 16, 64)), ("ssm_im_p", (1, 1, 16, 64)), ("conv_p", (1, 1, 2, 5632)),
        ("mem_kv_p", (1, 1, 256, 2, 4, 256)),
        ("kv_s0", (1, DB, DT, 2, H, E)), ("kv_s1", (1, DB, DT, 2, H, E)), ("kv_s2", (1, DB, DT, 2, H, E)),
        ("ssm_re_s", (1, DB, 16, 64)), ("ssm_im_s", (1, DB, 16, 64)), ("conv_s", (1, DB, 2, 5632))]


def build(nc, I, O):
    with ExitStack() as c:
        def sb(name, shape, dt=F32):
            return c.enter_context(nc.sbuf_tensor(name, shape, dt))

        S = {"stat": nc.dram_tensor("stat", (SEQ, 2 * G * H), F32, kind="Internal").ap()}
        S["bank"] = [c.enter_context(nc.psum_tensor(f"bank{i}", [P, 512], F32)) for i in range(8)]
        S["ident"] = sb("ident", [P, P])
        S["gain_bc"] = sb("gain_bc", [P, D])
        S["eps"] = sb("eps", [P, 1])
        with ExitStack() as o:
            def so(name, shape):
                return o.enter_context(nc.sbuf_tensor(name, shape, F32))

            S["ssm_over"] = (so("BpR", [P, 8, 16]), so("BpI", [P, 8, 16]), so("ER", [P, 8, P]), so("EI", [P, 8, P]),
                             so("XR", [P, 8, P]), so("XI", [P, 8, P]), so("HR", [P, 8, P + 1]),
                             so("HI", [P, 8, P + 1]), so("ta", [P, 8, P]), so("tb", [P, 8, P]),
                             so("BAR", [P, 8, P]), so("BAI", [P, 8, P]))
            S["MZ"] = so("MZ", [16, 16, P])
            S["t1"] = so("t1", [P, 8, P])
            S["tH"] = so("tH", [P, 8 * 9 * 16])
            S["ssm_mats"] = (so("CAR", [P, 8, 9, 16]), so("CAI", [P, 8, 9, 16]), so("WBR", [P, 8, P]),
                             so("WBI", [P, 8, P]), so("TZ", [P, 16, P]), so("UT", [P, 16, P]), so("Sin", [DB, 2, D]))
        S["wstage"] = sb("wstage", [P, KT, WB])
        S["w_next"] = nc.alloc_semaphore("w_next")
        before = nc.snapshot_sems()
        with ExitStack() as o:
            def co(name, shape):
                return o.enter_context(nc.sbuf_tensor(name, shape, F32))

            S["cross_over"] = (co("ring6", [P, 6, 2, 2 * P]), co("kTx", [P, 2, 2, 2 * P]), co("sTx", [P, 2 * P]),
                               co("Pm6", [P, 2, 2 * P]), co("PT6", [P, 2, 2, P]))
        with ExitStack() as o:
            S["ringS"] = o.enter_context(nc.sbuf_tensor("ringS", [P, 12, 4, GW], F32))
            S["kTcS"] = o.enter_context(nc.sbuf_tensor("kTcS", [P, 8, 2, P], F32))
        S["WH"] = sb("WH", [P, 2, KT, WB], F32R)
        S["WL"] = sb("WL", [P, 2, KT, WB], F32R)
        S["XH"] = sb("XH", [P, KT, T], F32R)
        S["XL"] = sb("XL", [P, KT, T], F32R)
        with ExitStack() as a:
            def sa(name, shape, dt=F32):
                return a.enter_context(nc.sbuf_tensor(name, shape, dt))

            S["mask"] = sa("mask", [P, 3 * P])
            S["rope"] = sa("rope", [P, G * NT + 1, 32])
            S["qk_gain"] = sa("qk_gain", [P, 2, E])
            S["U"] = sa("U", [P, 16, NT, 16])
            S["US"] = sa("US", [TS, SW])
            S["att"] = sa("att", [P, G * NT, GW])
            S["qkS"] = sa("qkS", [P, G, 2, 2, TS])
            S["vS"] = sa("vS", [TS, G, GW])
            S["negm"] = sa("negm", [P, G * NT, H])
            S["lsum"] = sa("lsum", [P, G * NT, H])
            S["tables"] = [(S["ident"][:], I["c_ident"]), (S["mask"][:], I["c_mask"]),
                           (S["rope"][:], I["c_rope"]), (S["gain_bc"][:], I["norm_mix"][0].partition_broadcast(P)),
                           (S["qk_gain"][:, 0], I["q_norm"][0].partition_broadcast(P)),
                           (S["qk_gain"][:, 1], I["k_norm"][0].partition_broadcast(P))]
            with ExitStack() as b:
                S["qT"] = b.enter_context(nc.sbuf_tensor("qT", [P, 2, SEQ], F32))
                S["kT"] = b.enter_context(nc.sbuf_tensor("kT", [P, 2, SEQ], F32))
                S["V"] = b.enter_context(nc.sbuf_tensor("V", [P, NT, GW], F32))
                block_project(nc, I, O, S)
            S["ysb"] = sa("ysb", [P, TILES, SW])
            block_ssm(nc, I, O, S)
            S["attS"] = sa("attS", [TS, AW])
            S["smask"] = sa("smask", [P, G, P + TS])
            S["al"] = sa("al", [P, G * NT, G, 2, H])
            block_sample(nc, I, O, S)
            block_mix(nc, I, O, S)
        nc.clear_and_free_semaphores(nc.allocated_since(before))
        nc.all_engine_barrier()
        S["hres"] = sb("hres", [P, TILES, D])
        with ExitStack() as b:
            def sb_(name, shape):
                return b.enter_context(nc.sbuf_tensor(name, shape, F32))

            S["kmT"], S["Vm"] = sb_("kmT", [P, KT, 2 * P]), sb_("Vm", [P, 2, D])
            S["gain_xq"] = sb_("gain_xq", [P, WB])
            with ExitStack() as m:
                def sm(name, shape, dt=F32):
                    return m.enter_context(nc.sbuf_tensor(name, shape, dt))

                S["MH"], S["ML"] = sm("MH", [P, KT, 2 * P], F32R), sm("ML", [P, KT, 2 * P], F32R)
                S["mraw"] = sm("mraw", [P, 2, D])
                S["gain_m"], S["gain_xk"] = sm("gain_m", [P, D]), sm("gain_xk", [P, WB])
            S["qxT"] = sb_("qxT", [P, KT, T])
            S["loadsmoq"] = [(S["gain_bc"][:], I["norm_x"][0].partition_broadcast(P)),
                             (S["gain_m"][:], I["norm_mem"][0].partition_broadcast(P)),
                             (S["gain_xk"][:], I["xk_norm"][0].partition_broadcast(P)),
                             (S["gain_xq"][:], I["xq_norm"][0].partition_broadcast(P)),
                             (S["mraw"][:], I["mem_prompt"][0].rearrange("(t p) d -> p t d", p=P))]
            block_dense(nc, I, O, S, "moq")
            block_cross(nc, I, O, S)
            S["loadsx"] = [(S["gain_bc"][:], I["norm_ffn"][0].partition_broadcast(P))]
        block_dense(nc, I, O, S, "x")
        block_ffn(nc, I, O, S)


def shape_constants():
    q, k = np.arange(P)[:, None], np.arange(P)[None, :]
    prev = np.where(k >= q, 0, NEG)
    own = np.where(k <= q, 0, NEG)
    pair = np.where((k % 2 == q % 2) & (k <= q), 0, NEG)
    mask = np.concatenate([prev, own, pair], 1).astype(np.float32)
    pos = np.zeros((P, G * NT + 1), np.int64)
    for g in range(G):
        for t in range(NT):
            pos[:, g * NT + t] = first_token(g, t) + STRIDE[g] * np.arange(P)
    pos[:TS, G * NT] = PAST + np.arange(TS) % DT
    inv = np.power(np.float32(500000.0), -np.arange(8, dtype=np.float32) * np.float32(2.0) / np.float32(16))
    ang = pos.astype(np.float32)[:, :, None] * inv.astype(np.float32)
    cos, sin = np.cos(ang), np.sin(ang)
    rope = np.concatenate([cos, cos, -sin, sin], 2).astype(np.float32)
    b, t = (np.arange(P) % TS // DT)[:, None], (np.arange(P) % DT)[:, None]
    key, nb, ni = np.arange(P)[None, :], np.arange(TS)[None, :] // DT, np.arange(TS)[None, :] % DT
    ok = [np.concatenate([key >= t, (nb == b) & (ni <= t)], 1),
          np.concatenate([(key >= 0) & (t >= 0), (nb == b) & (ni == t)], 1),
          np.concatenate([key // 64 == t % 2, (nb == b) & (ni == t)], 1)]
    smask = np.stack([np.where(x, 0, NEG) for x in ok], 1).astype(np.float32)
    return {"c_smask": smask, "c_ident": np.eye(P, dtype=np.float32), "c_mask": mask, "c_rope": rope}


def kernel(**inputs):
    import numpy as _np
    import concourse.bacc as _bacc
    from concourse import mybir as _mybir
    from concourse.bass_utils import run_bass_kernel_spmd as _run

    nc = _bacc.Bacc("TRN2", target_bir_lowering=False, num_devices=1)
    arrays, I, O = {}, {}, {}
    for name, a in [*inputs.items(), *shape_constants().items()]:
        a = _np.ascontiguousarray(a)
        arrays[name] = a
        I[name] = nc.dram_tensor(name, a.shape, _mybir.dt.from_np(a.dtype), kind="ExternalInput").ap()
    for name, shape in OUTS:
        O[name] = nc.dram_tensor("out_" + name, shape, F32, kind="ExternalOutput").ap()
    build(nc, I, O)
    r = _run(nc, [arrays], core_ids=[0])
    return tuple(r.results[0]["out_" + name] for name, _ in OUTS)
```
